# Optimizing a Trainium2 kernel written in Bass

```python
import math
import jax, jax.numpy as jnp
from jax import lax
import numpy as np

D_MODEL = 1024
BATCH = 1
SEQ = 256
DEPTH = 2

NORM_EPS = 1e-6
D_FF = 2816
D_MIX = D_MODEL
MLA_HEADS = 8
MLA_NOPE_DIM = 64
MLA_ROPE_DIM = 32
MLA_V_DIM = 64
MLA_QK_DIM = MLA_NOPE_DIM + MLA_ROPE_DIM
MLA_Q_RANK = 256
MLA_KV_RANK = 128
MLA_WIDTH = MLA_HEADS * MLA_V_DIM
ROPE_THETA = 10000.0
Q_BLOCK = 128
CONV_WIDTH = D_MIX // 4
CONV_KERNEL = 31
HY_WIDTH = D_MIX - MLA_WIDTH - CONV_WIDTH
HY_ORDER = 2
HY_SHORT_KERNEL = 3
HY_EMB_DIM = 33
HY_FILTER_DIM = 64
HY_FAST_DECAY_PCT = 0.3
HY_SLOW_DECAY_PCT = 1.5
HY_DECAY_TARGET = 1e-2
HY_FILTER_OUT = HY_ORDER * 2 * HY_WIDTH
IN_MLA_Q = MLA_Q_RANK
IN_MLA_KV = MLA_KV_RANK
IN_MLA_KPE = MLA_ROPE_DIM
IN_CONV = 2 * CONV_WIDTH
IN_HY = (HY_ORDER + 1) * HY_WIDTH
OFF_Q = 0
OFF_KV = OFF_Q + IN_MLA_Q
OFF_KPE = OFF_KV + IN_MLA_KV
OFF_CONV = OFF_KPE + IN_MLA_KPE
OFF_HY = OFF_CONV + IN_CONV
IN_COLS = OFF_HY + IN_HY


def rmsnorm(x, g):
    xf = x.astype(jnp.float32)
    xf = xf * lax.rsqrt(jnp.mean(xf * xf, axis=-1, keepdims=True) + NORM_EPS)
    return (xf * g.astype(jnp.float32)).astype(x.dtype)

def layernorm(x, g, b):
    xf = x.astype(jnp.float32)
    mu = jnp.mean(xf, axis=-1, keepdims=True)
    var = jnp.mean(jnp.square(xf - mu), axis=-1, keepdims=True)
    y = (xf - mu) * lax.rsqrt(var + NORM_EPS)
    return (y * g.astype(jnp.float32) + b.astype(jnp.float32)).astype(x.dtype)

def swiglu(h, w_gate, w_up, w_down):
    return (jax.nn.silu(h @ w_gate) * (h @ w_up)) @ w_down

def depthwise_conv(u, w, b):
    k, c = w.shape
    pad = k // 2
    y = lax.conv_general_dilated(u, w[:, None, :].astype(u.dtype), window_strides=(1,),
                                 padding=[(pad, pad)], dimension_numbers=('NWC', 'WIO', 'NWC'),
                                 feature_group_count=c)
    return y + b.astype(u.dtype)

def rope_cos_sin(positions, dtype):
    inv_freq = 1.0 / (ROPE_THETA ** (jnp.arange(0, MLA_ROPE_DIM, 2, dtype=jnp.float32) / MLA_ROPE_DIM))
    ang = positions.astype(jnp.float32)[..., None] * inv_freq
    return jnp.cos(ang).astype(dtype), jnp.sin(ang).astype(dtype)

def apply_rope(x, cos, sin):
    x1, x2 = jnp.split(x, 2, axis=-1)
    return jnp.concatenate([x1 * cos - x2 * sin, x1 * sin + x2 * cos], axis=-1)

def mla_mixer(h_q, h_kv, k_pe, positions, q_norm, w_qb, kv_norm, w_kvb):
    b, l, _ = h_q.shape
    cos, sin = rope_cos_sin(positions, h_q.dtype)
    q = (rmsnorm(h_q, q_norm) @ w_qb).reshape(b, l, MLA_HEADS, MLA_QK_DIM)
    q_pe = apply_rope(q[..., MLA_NOPE_DIM:], cos[:, :, None], sin[:, :, None])
    q = jnp.concatenate([q[..., :MLA_NOPE_DIM], q_pe], axis=-1) * (MLA_QK_DIM ** -0.5)
    kv = (rmsnorm(h_kv, kv_norm) @ w_kvb).reshape(b, l, MLA_HEADS, MLA_NOPE_DIM + MLA_V_DIM)
    k_pe = apply_rope(k_pe, cos, sin)
    k = jnp.concatenate([kv[..., :MLA_NOPE_DIM],
                         jnp.broadcast_to(k_pe[:, :, None], (b, l, MLA_HEADS, MLA_ROPE_DIM))], axis=-1)
    v = kv[..., MLA_NOPE_DIM:]
    n_blk = l // Q_BLOCK
    q_blocks = q.reshape(b, n_blk, Q_BLOCK, MLA_HEADS, MLA_QK_DIM).transpose(1, 0, 2, 3, 4)

    def attend(qb):
        s = jnp.einsum('bqhd,bkhd->bhqk', qb, k).astype(jnp.float32)
        p = jax.nn.softmax(s, axis=-1).astype(v.dtype)
        return jnp.einsum('bhqk,bkhd->bqhd', p, v)

    o = lax.map(attend, q_blocks)
    return o.transpose(1, 0, 2, 3, 4).reshape(b, l, MLA_WIDTH)

def conformer_conv_mixer(h_conv, dw_w, dw_b, ln_g, ln_b):
    a, g = jnp.split(h_conv, 2, axis=-1)
    u = a * jax.nn.sigmoid(g)
    u = depthwise_conv(u, dw_w, dw_b)
    return jax.nn.silu(layernorm(u, ln_g, ln_b))

def hyena_filters(l, w1, b1, w2, b2, w3, b3, w4, freq):
    f32 = jnp.float32
    t = jnp.linspace(0.0, 1.0, l, dtype=f32)[:, None]
    bands = (HY_EMB_DIM - 1) // 2
    ang = 2.0 * math.pi * jnp.arange(l, dtype=f32)[:, None] / l
    fb = jnp.linspace(1e-4, bands - 1, bands, dtype=f32)[None, :]
    z = jnp.concatenate([t, jnp.cos(fb * ang), -jnp.sin(fb * ang)], axis=-1)
    fr = freq.astype(f32)
    hdn = jnp.sin(fr * (z @ w1.astype(f32) + b1.astype(f32)))
    hdn = jnp.sin(fr * (hdn @ w2.astype(f32) + b2.astype(f32)))
    hdn = jnp.sin(fr * (hdn @ w3.astype(f32) + b3.astype(f32)))
    h = (hdn @ w4.astype(f32)).reshape(l, HY_ORDER, 2, HY_WIDTH)
    max_decay = math.log(HY_DECAY_TARGET) / HY_FAST_DECAY_PCT
    min_decay = math.log(HY_DECAY_TARGET) / HY_SLOW_DECAY_PCT
    deltas = jnp.linspace(min_decay, max_decay, HY_WIDTH, dtype=f32)
    h = h * jnp.exp(-t * jnp.abs(deltas))[:, None, None, :]
    fwd, bwd = h[:, :, 0], h[:, :, 1]
    k = jnp.concatenate([fwd, jnp.zeros_like(fwd[:1]), jnp.flip(bwd[1:], axis=0)], axis=0)
    return k / jnp.sum(jnp.abs(k), axis=0, keepdims=True)

def fft_long_conv(u, k, d):
    l = u.shape[1]
    uf = u.astype(jnp.float32)
    uk = jnp.fft.rfft(uf, n=2 * l, axis=1) * jnp.fft.rfft(k, axis=0)[None]
    y = jnp.fft.irfft(uk, n=2 * l, axis=1)[:, :l]
    return (y + uf * d.astype(jnp.float32)).astype(u.dtype)

def hyena_mixer(h_hy, short_w, short_b, w1, b1, w2, b2, w3, b3, w4, freq, bias_d):
    u = depthwise_conv(h_hy, short_w, short_b)
    v, x1, x2 = jnp.split(u, HY_ORDER + 1, axis=-1)
    k = hyena_filters(h_hy.shape[1], w1, b1, w2, b2, w3, b3, w4, freq)
    z = x1 * fft_long_conv(v, k[:, 0], bias_d[0])
    return x2 * fft_long_conv(z, k[:, 1], bias_d[1])

def first_inputs(seed: int = 0) -> dict:
    key = jax.random.key(seed)
    ks = iter(jax.random.split(key, 64))
    f32 = jnp.float32

    def nrm(shape, scale):
        return jax.random.normal(next(ks), shape, f32) * scale

    def gain(shape):
        return 1.0 + nrm(shape, 0.05)

    dd = DEPTH
    return {
        "x": nrm((BATCH, SEQ, D_MODEL), 1.0),
        "positions": jnp.broadcast_to(jnp.arange(SEQ, dtype=jnp.int32)[None], (BATCH, SEQ)),
        "ffn1_norm": gain((dd, D_MODEL)),
        "ffn1_w_gate": nrm((dd, D_MODEL, D_FF), D_MODEL ** -0.5),
        "ffn1_w_up": nrm((dd, D_MODEL, D_FF), D_MODEL ** -0.5),
        "ffn1_w_down": nrm((dd, D_FF, D_MODEL), D_FF ** -0.5),
        "mix_norm": gain((dd, D_MODEL)),
        "w_in": nrm((dd, D_MODEL, IN_COLS), D_MODEL ** -0.5),
        "mla_q_norm": gain((dd, MLA_Q_RANK)),
        "mla_w_qb": nrm((dd, MLA_Q_RANK, MLA_HEADS * MLA_QK_DIM), MLA_Q_RANK ** -0.5),
        "mla_kv_norm": gain((dd, MLA_KV_RANK)),
        "mla_w_kvb": nrm((dd, MLA_KV_RANK, MLA_HEADS * (MLA_NOPE_DIM + MLA_V_DIM)), MLA_KV_RANK ** -0.5),
        "conv_dw_w": nrm((dd, CONV_KERNEL, CONV_WIDTH), CONV_KERNEL ** -0.5),
        "conv_dw_b": nrm((dd, CONV_WIDTH), 0.02),
        "conv_ln_g": gain((dd, CONV_WIDTH)),
        "conv_ln_b": nrm((dd, CONV_WIDTH), 0.02),
        "hy_short_w": nrm((dd, HY_SHORT_KERNEL, IN_HY), HY_SHORT_KERNEL ** -0.5),
        "hy_short_b": nrm((dd, IN_HY), 0.02),
        "hy_filt_w1": nrm((dd, HY_EMB_DIM, HY_FILTER_DIM), HY_EMB_DIM ** -0.5),
        "hy_filt_b1": nrm((dd, HY_FILTER_DIM), 0.1),
        "hy_filt_w2": nrm((dd, HY_FILTER_DIM, HY_FILTER_DIM), HY_FILTER_DIM ** -0.5),
        "hy_filt_b2": nrm((dd, HY_FILTER_DIM), 0.1),
        "hy_filt_w3": nrm((dd, HY_FILTER_DIM, HY_FILTER_DIM), HY_FILTER_DIM ** -0.5),
        "hy_filt_b3": nrm((dd, HY_FILTER_DIM), 0.1),
        "hy_filt_w4": nrm((dd, HY_FILTER_DIM, HY_FILTER_OUT), HY_FILTER_DIM ** -0.5),
        "hy_filt_freq": gain((dd, HY_FILTER_DIM)),
        "hy_bias_d": nrm((dd, HY_ORDER, HY_WIDTH), 0.5),
        "out_norm": gain((dd, D_MIX)),
        "w_out": nrm((dd, D_MIX, D_MODEL), D_MIX ** -0.5),
        "ffn2_norm": gain((dd, D_MODEL)),
        "ffn2_w_gate": nrm((dd, D_MODEL, D_FF), D_MODEL ** -0.5),
        "ffn2_w_up": nrm((dd, D_MODEL, D_FF), D_MODEL ** -0.5),
        "ffn2_w_down": nrm((dd, D_FF, D_MODEL), D_FF ** -0.5),
        "final_norm": gain((D_MODEL,)),
    }

def first_block(x, positions, ffn1_norm, ffn1_w_gate, ffn1_w_up, ffn1_w_down, mix_norm, w_in,
              mla_q_norm, mla_w_qb, mla_kv_norm, mla_w_kvb, conv_dw_w, conv_dw_b, conv_ln_g, conv_ln_b,
              hy_short_w, hy_short_b, hy_filt_w1, hy_filt_b1, hy_filt_w2, hy_filt_b2, hy_filt_w3, hy_filt_b3,
              hy_filt_w4, hy_filt_freq, hy_bias_d, out_norm, w_out, ffn2_norm, ffn2_w_gate, ffn2_w_up,
              ffn2_w_down, final_norm):
    e1 = MLA_WIDTH
    e2 = MLA_WIDTH + CONV_WIDTH
    for i in range(DEPTH):
        x = x + 0.5 * swiglu(rmsnorm(x, ffn1_norm[i]), ffn1_w_gate[i], ffn1_w_up[i], ffn1_w_down[i])
        h = rmsnorm(x, mix_norm[i]) @ w_in[i]
        y_mla = mla_mixer(h[..., OFF_Q:OFF_KV], h[..., OFF_KV:OFF_KPE], h[..., OFF_KPE:OFF_CONV], positions,
                          mla_q_norm[i], mla_w_qb[i], mla_kv_norm[i], mla_w_kvb[i])
        y_conv = conformer_conv_mixer(h[..., OFF_CONV:OFF_HY], conv_dw_w[i], conv_dw_b[i],
                                      conv_ln_g[i], conv_ln_b[i])
        y_hy = hyena_mixer(h[..., OFF_HY:], hy_short_w[i], hy_short_b[i], hy_filt_w1[i], hy_filt_b1[i],
                           hy_filt_w2[i], hy_filt_b2[i], hy_filt_w3[i], hy_filt_b3[i], hy_filt_w4[i],
                           hy_filt_freq[i], hy_bias_d[i])
        g = out_norm[i]
        y = jnp.concatenate([rmsnorm(y_mla, g[:e1]), rmsnorm(y_conv, g[e1:e2]), rmsnorm(y_hy, g[e2:])], axis=-1)
        x = x + y @ w_out[i]
        x = x + 0.5 * swiglu(rmsnorm(x, ffn2_norm[i]), ffn2_w_gate[i], ffn2_w_up[i], ffn2_w_down[i])
    return rmsnorm(x, final_norm)


N_GROUPS = 4
FOURIER_WIDTH = 512
FOURIER_GROUP = FOURIER_WIDTH // N_GROUPS
CONV_WIDTH_2 = 512
CONV_K = 3
POOL_WIDTH = 512
POOL_GROUP = POOL_WIDTH // N_GROUPS
POOL_WINDOWS = (2, 4, 8, 16)
OUT_GROUP = D_MODEL // N_GROUPS
N_BRANCHES = 3
EPS = 1e-6

OFF_F = 0
OFF_B = OFF_F + FOURIER_WIDTH
OFF_C = OFF_B + CONV_WIDTH_2
OFF_V = OFF_C + CONV_WIDTH_2
OFF_P = OFF_V + CONV_WIDTH_2
OFF_G = OFF_P + POOL_WIDTH
IN_WIDTH = OFF_G + N_BRANCHES * D_MODEL


def rmsnorm_2(x, g):
    xf = x.astype(jnp.float32)
    y = xf * lax.rsqrt(jnp.mean(xf * xf, axis=-1, keepdims=True) + EPS)
    return (y * g.astype(jnp.float32)).astype(x.dtype)

def swiglu_2(h, w1, w3, w2):
    return (jax.nn.silu(h @ w1) * (h @ w3)) @ w2

def fourier_mix(u, w_map):
    b, s, _ = u.shape
    ug = u.reshape(b, s, N_GROUPS, FOURIER_GROUP).astype(jnp.float32)
    f = jnp.fft.fftn(ug, axes=(1, 3), norm="ortho").real.astype(u.dtype)
    y = jnp.einsum("bsgc,gcd->bsgd", f, w_map)
    return y.reshape(b, s, D_MODEL)

def short_conv(bg, cg, v, w_conv, w_out):
    z = cg * v
    zp = jnp.pad(z, ((0, 0), (1, 1), (0, 0)))
    conv = w_conv[0] * zp[:, :-2] + w_conv[1] * zp[:, 1:-1] + w_conv[2] * zp[:, 2:]
    return (bg * conv) @ w_out

def pool_mix(u, w_map, scale):
    s = u.shape[1]
    t = jnp.arange(s, dtype=jnp.float32)
    outs = []
    for i, w in enumerate(POOL_WINDOWS):
        half = w // 2
        ug = u[..., i * POOL_GROUP:(i + 1) * POOL_GROUP].astype(jnp.float32)
        cs = jnp.pad(jnp.cumsum(ug, axis=1), ((0, 0), (1, 0), (0, 0)))
        padded = jnp.pad(cs, ((0, 0), (half, half), (0, 0)), mode="edge")
        win = padded[:, w:w + s] - padded[:, :s]
        count = jnp.minimum(t + half, float(s)) - jnp.maximum(t - half, 0.0)
        pooled = win / count[None, :, None] - ug
        outs.append(pooled.astype(u.dtype) @ w_map[i])
    return jnp.concatenate(outs, axis=-1) * scale

def second_inputs(seed: int = 0) -> dict:
    key = jax.random.key(seed)
    ks = jax.random.split(key, 20)
    f32 = jnp.float32

    def nrm(k, shape, fan_in):
        return jax.random.normal(k, shape, f32) * (fan_in ** -0.5)

    def gain(k, shape):
        return 1.0 + 0.02 * jax.random.normal(k, shape, f32)

    L, D = DEPTH, D_MODEL
    return {
        "x": jax.random.normal(ks[0], (BATCH, SEQ, D), f32),
        "g_ffn1": gain(ks[1], (L, D)),
        "w1_a": nrm(ks[2], (L, D, D_FF), D),
        "w3_a": nrm(ks[3], (L, D, D_FF), D),
        "w2_a": nrm(ks[4], (L, D_FF, D), D_FF),
        "g_mix": gain(ks[5], (L, D)),
        "w_in": nrm(ks[6], (L, D, IN_WIDTH), D),
        "w_fourier": nrm(ks[7], (L, N_GROUPS, FOURIER_GROUP, OUT_GROUP), FOURIER_GROUP),
        "w_conv": nrm(ks[8], (L, CONV_K, CONV_WIDTH_2), CONV_K),
        "w_conv_out": nrm(ks[9], (L, CONV_WIDTH_2, D), CONV_WIDTH_2),
        "w_pool": nrm(ks[10], (L, N_GROUPS, POOL_GROUP, OUT_GROUP), POOL_GROUP),
        "pool_scale": gain(ks[11], (L, D)),
        "w_o": nrm(ks[12], (L, D, D), D),
        "g_ffn2": gain(ks[13], (L, D)),
        "w1_b": nrm(ks[14], (L, D, D_FF), D),
        "w3_b": nrm(ks[15], (L, D, D_FF), D),
        "w2_b": nrm(ks[16], (L, D_FF, D), D_FF),
        "g_final": gain(ks[17], (D,)),
    }

def second_block(x, g_ffn1, w1_a, w3_a, w2_a, g_mix, w_in, w_fourier, w_conv, w_conv_out,
              w_pool, pool_scale, w_o, g_ffn2, w1_b, w3_b, w2_b, g_final):
    b, s, d = x.shape
    for l in range(DEPTH):
        h = rmsnorm_2(x, g_ffn1[l])
        x = x + 0.5 * swiglu_2(h, w1_a[l], w3_a[l], w2_a[l])

        h = rmsnorm_2(x, g_mix[l])
        p = h @ w_in[l]
        gates = jax.nn.sigmoid(p[..., OFF_G:].astype(jnp.float32)).astype(x.dtype)
        gates = gates.reshape(b, s, N_BRANCHES, d)
        y_f = fourier_mix(p[..., OFF_F:OFF_B], w_fourier[l])
        y_c = short_conv(p[..., OFF_B:OFF_C], p[..., OFF_C:OFF_V], p[..., OFF_V:OFF_P],
                         w_conv[l], w_conv_out[l])
        y_p = pool_mix(p[..., OFF_P:OFF_G], w_pool[l], pool_scale[l])
        merged = gates[:, :, 0] * y_f + gates[:, :, 1] * y_c + gates[:, :, 2] * y_p
        x = x + merged @ w_o[l]

        h = rmsnorm_2(x, g_ffn2[l])
        x = x + 0.5 * swiglu_2(h, w1_b[l], w3_b[l], w2_b[l])
    return rmsnorm_2(x, g_final)


def setup_inputs(seed=0):
    out = dict(first_inputs(seed))
    for name, value in second_inputs(seed + 1).items():
        if name != "x":
            out[name + "_2"] = value
    return out


def reference(
    x, positions, ffn1_norm, ffn1_w_gate, ffn1_w_up, ffn1_w_down, mix_norm, w_in, mla_q_norm,
    mla_w_qb, mla_kv_norm, mla_w_kvb, conv_dw_w, conv_dw_b, conv_ln_g, conv_ln_b, hy_short_w,
    hy_short_b, hy_filt_w1, hy_filt_b1, hy_filt_w2, hy_filt_b2, hy_filt_w3, hy_filt_b3,
    hy_filt_w4, hy_filt_freq, hy_bias_d, out_norm, w_out, ffn2_norm, ffn2_w_gate, ffn2_w_up,
    ffn2_w_down, final_norm, g_ffn1_2, w1_a_2, w3_a_2, w2_a_2, g_mix_2, w_in_2, w_fourier_2,
    w_conv_2, w_conv_out_2, w_pool_2, pool_scale_2, w_o_2, g_ffn2_2, w1_b_2, w3_b_2, w2_b_2,
    g_final_2,
):
    x = first_block(
        x, positions, ffn1_norm, ffn1_w_gate, ffn1_w_up, ffn1_w_down, mix_norm, w_in,
        mla_q_norm, mla_w_qb, mla_kv_norm, mla_w_kvb, conv_dw_w, conv_dw_b, conv_ln_g,
        conv_ln_b, hy_short_w, hy_short_b, hy_filt_w1, hy_filt_b1, hy_filt_w2, hy_filt_b2,
        hy_filt_w3, hy_filt_b3, hy_filt_w4, hy_filt_freq, hy_bias_d, out_norm, w_out, ffn2_norm,
        ffn2_w_gate, ffn2_w_up, ffn2_w_down, final_norm,
    )
    return second_block(
        x, g_ffn1_2, w1_a_2, w3_a_2, w2_a_2, g_mix_2, w_in_2, w_fourier_2, w_conv_2,
        w_conv_out_2, w_pool_2, pool_scale_2, w_o_2, g_ffn2_2, w1_b_2, w3_b_2, w2_b_2,
        g_final_2,
    )


_drawn_inputs = setup_inputs


def setup_inputs(seed=0):
    import zlib

    import numpy as np

    out = dict(_drawn_inputs(seed))
    spreads = {}
    factors = {'conv_ln_b': 3.376,
     'hy_filt_freq': 3.079,
     'g_ffn1_2': 4.065,
     'pool_scale_2': 22.251,
     'g_ffn2_2': 31.602,
     'g_final_2': 22.933,
     'g_mix_2': 3.383}
    for name, (base, spread) in spreads.items():
        noise = np.random.default_rng([zlib.crc32(name.encode()), seed]).standard_normal(out[name].shape)
        drawn = base * np.exp(spread * noise) if base else spread * noise
        out[name] = __import__('jax').numpy.asarray(drawn.astype(out[name].dtype))
    for name, factor in factors.items():
        out[name] = (out[name] * factor).astype(out[name].dtype)
    return out
```

```python
import math

import numpy as np

import concourse.bass as bass
from concourse import mybir
from contextlib import ExitStack

P = 128
SEQ = 256
DM = 1024
FF = 2816
DEPTH = 2
EPS = 1e-6
NT = SEQ // P
KT = DM // P
FFU = FF // P
HALF = 512
A_COLS = 2 * KT * P
HEADS, NOPE, ROPE, VD = 8, 64, 32, 64
QKD = NOPE + ROPE
QR, KVR = 256, 128
CW = 256
CK = 31
PADC = CK // 2
FILT = 64
EMB = 33
NFFT = 2 * SEQ
IN1 = 1696
PANELS1 = [("ca", 416), ("cg", 672), ("q", 0), ("kv", 256), ("v", 928), ("x1", 1184), ("x2", 1440)]
GROUPS = 4
IN2 = 5 * 512 + 3 * DM
PANELS2 = ([("F", 0), ("F", 1), ("P", 0), ("P", 1), ("C", 0), ("V", 0), ("B", 0), ("C", 1), ("V", 1), ("B", 1)])
OFF2 = {"F": 0, "B": 512, "C": 1024, "V": 1536, "P": 2048, "G": 2560}
WINDOWS = (2, 4, 8, 16)
PADP = 8

COL1, COL2 = {}, {}
_n = 0
for _name, _k in (("ffn1", 8), ("mix", 8), ("q", 2), ("kv", 1), ("dww", 62), ("dwb", 2), ("hsw", 18), ("hsb", 6),
                  ("out", 8), ("ffn2", 8)):
    COL1[_name] = (_n, _k)
    _n += _k
ROWS1 = _n
_n = 0
for _name, _k in (("ffn1", 8), ("mix", 8), ("wc", 12), ("ps", 8), ("ffn2", 8)):
    COL2[_name] = (_n, _k)
    _n += _k
ROWS2 = _n

TWO_PI = 2.0 * math.pi
PI_A = 6.28125
PI_B = float(np.float32(np.round((TWO_PI - PI_A) * 2.0**21) / 2.0**21))
PI_C = float(TWO_PI - PI_A - PI_B)
ROUND = 12582912.0
PI_F = 3.1415925

CREDIT = 2


def order_mix1():
    o = ["A", "A", "glu", "f0", "A", "taps", "f1", "A", "taps", "qkv_sq", "f2", "stat", "taps", "A",
         "h0", "kb", "short0", "A", "n0", "spec0", "short1", "A", "h1", "short2", "n1",
         "spec1", "values", "fwd0", "taps", "q0", "k0", "kpe", "rot0", "inv0", "taps"]
    o += ["s0", "s1", "p0", "fwd1", "taps", "q1", "k1", "rot1", "s2", "o0", "p1", "s3", "o1", "p2", "inv1", "taps", "B",
          "q2", "k2", "rot2", "s4", "o2", "p3", "s5", "o3", "p4", "taps",
          "q3", "k3", "rot3", "s6", "o4", "p5", "s7", "o5", "p6", "taps", "o6", "p7", "taps", "B", "o7",
          "conv_out", "y_norm"]
    return o


N_PARAM1 = 14
N_PARAM2 = 2
N_BLOCK1 = 5
N_BLOCK2 = 3
TAP_PARTS = order_mix1().count("taps")


def tap_range(part):
    return range(CK * part // TAP_PARTS, CK * (part + 1) // TAP_PARTS)


def small_steps1():
    s = []
    for it in order_mix1():
        if it in ("f0", "f1", "f2", "stat", "kb"):
            s.append(it)
        elif it in ("h0", "h1"):
            s += [f"{it}t{t}" for t in range(NT)]
        elif it == "values":
            s += ["val0", "val1"]
        elif it.startswith("n") or it.startswith("short"):
            s.append(it)
        elif it.startswith("spec"):
            s += ["A" + it[4:], "B" + it[4:]]
        elif it.startswith("fwd"):
            s += ["re" + it[3:], "im" + it[3:]]
        elif it.startswith("inv") or it.startswith("rot") or it == "conv_out":
            s.append(it)
        elif it == "kpe":
            s.append(it)
        elif it[0] in "qkspo" and it[1:].isdigit():
            s.append(it)
    return s


SMALL1 = small_steps1()
SMALL2 = ([f"c{g}" for g in range(GROUPS)] + ["t0", "t1"] + [f"yf{m}" for m in range(4)] + [f"yp{m}" for m in range(4)])


def order_mix2():
    return ["A", "A", "c0", "c1", "c2", "c3", "A", "A", "pool", "t0", "A", "A", "z0", "A", "bc0", "t1",
            "A", "A", "z1", "A", "bc1", "yf0", "yf1", "yf2", "yf3", "yp0", "yp1", "yp2", "yp3",
            "Y0", "Y1", "Y2", "Y3"] + ["G"] * 4


def norms_before(L):
    return 4 * min(L, DEPTH) + 3 * max(L - DEPTH, 0)


def host_constants():
    f64 = np.float64
    t = np.arange(SEQ, dtype=f64)
    f = np.arange(SEQ, dtype=f64)
    ang = 2 * np.pi * np.outer(t, f) / NFFT
    alt = np.where(np.arange(SEQ) % 2 == 0, 1.0, -1.0)
    cf = np.cos(ang)
    sf = -np.sin(ang)
    sf[:, 0] = alt
    w = np.full(SEQ, 2.0 / NFFT)
    w[0] = 1.0 / NFFT
    ci = w[:, None] * np.cos(ang.T)
    si = -w[:, None] * np.sin(ang.T)
    si[0, :] = alt / NFFT
    ps = 2 * np.pi * np.outer(t, t) / SEQ
    k = np.arange(P, dtype=f64)
    pc = 2 * np.pi * np.outer(k, k) / P
    norm = 1.0 / math.sqrt(SEQ * P)
    f32 = np.float32
    tt = np.linspace(0.0, 1.0, SEQ, dtype=f32)[:, None]
    bands = (EMB - 1) // 2
    a = (f32(2.0 * math.pi) * np.arange(SEQ, dtype=f32)[:, None] / f32(SEQ)).astype(f32)
    fb = np.linspace(1e-4, bands - 1, bands, dtype=f32)[None, :]
    z = np.concatenate([tt, np.cos(fb * a), -np.sin(fb * a)], axis=-1).astype(f32)
    max_decay = math.log(1e-2) / 0.3
    min_decay = math.log(1e-2) / 1.5
    deltas = np.linspace(min_decay, max_decay, CW, dtype=f32)
    decay = np.exp(-tt * np.abs(deltas)).astype(f32)
    rot = np.zeros((QKD, QKD))
    for i in range(ROPE // 2):
        rot[NOPE + 16 + i, NOPE + i] = -1.0
        rot[NOPE + i, NOPE + 16 + i] = 1.0
    invf = np.zeros((QKD, 1), f32)
    base = 1.0 / (f32(10000.0) ** (np.arange(0, ROPE, 2, dtype=f32) / f32(ROPE)))
    invf[NOPE:NOPE + 16, 0] = base
    invf[NOPE + 16:, 0] = base
    rc = np.zeros((P, GROUPS, SEQ))
    for g, win in enumerate(WINDOWS):
        cnt = np.minimum(t + win // 2, SEQ) - np.maximum(t - win // 2, 0)
        rc[:, g, :] = 1.0 / cnt
    out = {
        "k_dft": np.stack([cf, sf, ci, si]),
        "k_seq": np.stack([np.cos(ps) * norm, -np.sin(ps) * norm]),
        "k_chan": np.concatenate([np.cos(pc), np.sin(pc)], axis=1),
        "k_emb": np.ascontiguousarray(z.T),
        "k_decay": decay,
        "k_rot": rot,
        "k_invf": invf,
        "k_count": rc,
        "k_eye": np.eye(P),
    }
    return {n: np.ascontiguousarray(v, dtype=f32) for n, v in out.items()}


def build(nc: bass.Bass, T, out: bass.AP):
    F32 = mybir.dt.float32
    F32R = mybir.dt.float32r
    I32 = mybir.dt.int32
    ALU = mybir.AluOpType
    ACT = mybir.ActivationFunctionType
    AX = mybir.AxisListType.X
    MULT, ADD, SUB = ALU.mult, ALU.add, ALU.subtract

    ctx = ExitStack()
    with ctx:
        def sb(name, shape, dt=F32):
            return ctx.enter_context(nc.sbuf_tensor(name, shape, dt))

        def sem(name):
            return ctx.enter_context(nc.semaphore(name))

        acc = ctx.enter_context(nc.psum_tensor("acc", [P, 4, HALF], F32))
        pair = [ctx.enter_context(nc.psum_tensor(f"pair{i}", [P, 2, HALF], F32)) for i in range(2)]

        raw_a = [sb(f"raw_a{i}", [P, A_COLS]) for i in range(2)]
        raw_b = [sb(f"raw_b{i}", [P, DM]) for i in range(2)]
        a_hi = [sb(f"a_hi{i}", [P, A_COLS], F32R) for i in range(2)]
        a_lo = [sb(f"a_lo{i}", [P, A_COLS], F32R) for i in range(2)]
        b_hi = [sb(f"b_hi{i}", [P, DM], F32R) for i in range(2)]
        b_lo = [sb(f"b_lo{i}", [P, DM], F32R) for i in range(2)]
        x = sb("x", [P, NT, DM])
        xT = sb("xT", [P, KT, 2, SEQ], F32R)
        hT = [sb(f"hT{i}", [P, 2, SEQ], F32R) for i in range(2)]
        second = sb("second", [P, 2, SEQ])
        gu = sb("gu", [P, 2, SEQ])
        sh = sb("sh", [P, 2, SEQ])
        xn = sb("xn", [P, NT, DM])
        cols = sb("cols", [P, 2 * DEPTH, P])
        eye = sb("eye", [P, P])
        ones = sb("ones", [P, P])
        ssq = sb("ssq", [P, 8])
        var = sb("var", [P, 8])
        rstd = sb("rstd", [P, 8])
        minus_half = sb("minus_half", [P, 8])

        a_full = [sem(f"a_full{i}") for i in range(2)]
        b_full = [sem(f"b_full{i}") for i in range(2)]
        a_hi_ready = sem("a_hi_ready")
        a_split = sem("a_split")
        b_hi_ready = sem("b_hi_ready")
        b_split = sem("b_split")
        proj_done = sem("proj_done")
        second_out = sem("second_out")
        pair_summed = sem("pair_summed")
        silu_done = sem("silu_done")
        h_done = sem("h_done")
        h_hi_ready = sem("h_hi_ready")
        h_split = sem("h_split")
        down_done = sem("down_done")
        acc_half = sem("acc_half")
        x_done = sem("x_done")
        ssq_done = sem("ssq_done")
        var_done = sem("var_done")
        rstd_done = sem("rstd_done")
        xn_done = sem("xn_done")
        xT_in_psum = sem("xT_in_psum")
        xT_hi = sem("xT_hi")
        xT_split = sem("xT_split")
        made = sem("made")
        taken = [sem(f"taken{i}") for i in range(4)]
        dve_step = sem("dve_step")
        act_step = sem("act_step")
        consts_in = sem("consts_in")
        rows_in = sem("rows_in")
        rows_T = sem("rows_T")
        cols_done = sem("cols_done")
        params_in = [sem(f"params_in{i}") for i in range(2 * DEPTH)]
        gain_in = sem("gain_in")
        stored = sem("stored")
        half_set = sem("half_set")
        block1_in = sem("block1_in")
        block2_in = sem("block2_in")
        EVENTS1 = {"gate_tanh": 1, "filt_arg": 3, "filt_hidden": 3, "filt_taps": 2, "filt_abs": 2, "filt_sums": 2,
                   "qkv_squares": 1, "q_gained": 1, "qkv_rstd": 1, "kv_diag": 1, "short_mid": 3, "short_done": 3,
                   "spectrum": 2, "q_roped": 4, "kpe_roped": 1, "neg_max": HEADS, "conv_done": 1, "ln_var": 1,
                   "ln_rstd": 1, "ln_done": 1, "conv_silu": 1, "rope_arg": 2, "rope_done": 2}
        EVENTS2 = {"pooled": 1, "bc_f32": 2, "bc_hi": 2, "bc_split": 2, "gate_done": 12, "merged": 4}
        ev = {n: sem(n) for n in (*EVENTS1, *EVENTS2)}

        def nth(L, name, i=0):
            return (L % DEPTH) * (EVENTS1 if name in EVENTS1 else EVENTS2)[name] + i + 1

        def colv(L, name, i=0, parts=P):
            o = (COL1 if L < DEPTH else COL2)[name][0]
            return cols[0:parts, L, o + i:o + i + 1]

        small = {}
        for L in range(2 * DEPTH):
            base = L * len(SMALL1) if L < DEPTH else DEPTH * len(SMALL1) + (L - DEPTH) * len(SMALL2)
            for n, name in enumerate(SMALL1 if L < DEPTH else SMALL2):
                small[L, name] = base + n

        def bank(L, name):
            return acc[:, small[L, name] % 4, :]

        class Obj:
            pass

        def scope1(c):
            def s(name, shape, dt=F32):
                return c.enter_context(nc.sbuf_tensor(name, shape, dt))
            m = Obj()
            m.dft = s("dft", [P, 4, NT, SEQ])
            m.decay = s("decay", [P, NT, CW])
            m.cs = s("cossin", [QKD, 2, SEQ])
            m.rotm = s("rotm", [QKD, QKD])
            m.invf = s("invf", [QKD, 1])
            m.lngb = s("lngb", [P, 2, CW])
            m.wqb = s("wqb", [P, 2, HEADS * QKD])
            m.wkvb = s("wkvb", [P, HEADS * (NOPE + VD)])
            early = s("early", [P, 6088])
            m.w4 = early[0:FILT, 0:1024]
            m.emb = early[0:EMB, 1024:1280]
            m.w1 = early[0:EMB, 1280:1344]
            m.w2 = early[0:FILT, 1344:1408]
            m.w3 = early[0:FILT, 1408:1472]
            m.fcol = early[0:FILT, 1472:1476]
            m.dB = early[:, 1480:1992].rearrange("p (o c) -> p o c", o=2)
            m.farg = early[0:FILT, 1992:2248]
            m.fq = early[0:FILT, 2248:2504]
            m.hdn = early[0:FILT, 2504:2760]
            m.kt = early[:, 2760:3784].rearrange("p (t d c) -> p t d c", t=NT, d=2)
            m.ab = early[:, 3784:4808].rearrange("p (t d c) -> p t d c", t=NT, d=2)
            m.ks = early[:, 4808:5320].rearrange("p (t c) -> p t c", t=NT)
            m.kd = early[:, 5320:5832].rearrange("p (t c) -> p t c", t=NT)
            m.rn = early[:, 5832:6088]
            m.V = early[:, 4808:5832].rearrange("p (t c) -> p t c", t=NT)
            m.qraw = early[0:QKD, 0:512]
            m.qc = early[0:QKD, 1024:1536]
            m.qp = [early[0:QKD, 512:1024], early[0:QKD, 1992:2504]]
            m.kT = [early[0:QKD, 2760:3272], early[0:QKD, 3272:3784]]
            m.PT = [early[:, 3784:4296], early[:, 4296:4808]]
            m.kpe = early[0:QKD, 2504:2760]
            m.kpe2 = early[0:QKD, 5832:6088]
            m.pos = s("pos", [QKD, SEQ], I32)
            m.posf = early[0:QKD, 2760:3016]
            m.fq96 = early[0:QKD, 3016:3272]
            m.ra = early[0:QKD, 3272:3784].rearrange("p (a c) -> p a c", a=2)
            m.Pm = [gu, sh]
            m.KA = [s(f"KA{o}", [P, 2, CW]) for o in range(2)]
            m.KB = [s(f"KB{o}", [P, 2, CW]) for o in range(2)]
            m.KN = s("KN", [1, 2, CW])
            m.ca = s("ca", [P, 2, SEQ])
            m.cg = s("cg", [P, 2, SEQ])
            m.u = s("u", [P, 2, SEQ + 2 * PADC])
            m.co = s("co", [P, 2, SEQ])
            m.hq = s("hq", [P, 2, SEQ])
            m.qn = m.hq
            m.hk = s("hk", [P, 2, SEQ])
            m.kvn = s("kvn", [P, SEQ])
            m.hs = s("hs", [P, 2, SEQ + 2])
            m.sc = s("sc", [P, 2, SEQ])
            m.tv = [s(f"tv{j}", [P, NT, CW]) for j in range(3)]
            m.tmp = m.cg
            m.Yr = m.ca
            m.Yi = s("Yi", [P, 2, CW])
            m.mx = s("mx", [P, 2 * HEADS])
            m.sm = s("sm", [P, 2 * HEADS])
            m.rs = s("rs", [P, 2 * HEADS])
            m.qs = s("qs", [P, 4])
            m.bn = s("bn", [P, NT, 6])
            m.mv = s("mv", [P, NT, 2])
            return m

        def scope2(c):
            def s(name, shape, dt=F32):
                return c.enter_context(nc.sbuf_tensor(name, shape, dt))
            m = Obj()
            m.seq = s("seq", [P, 2, NT, SEQ])
            m.chan = s("chan", [P, 2 * P])
            m.count = s("count", [P, GROUPS, SEQ])
            m.wf = s("wf", [P, GROUPS, SEQ])
            m.wp = s("wp", [P, GROUPS, SEQ])
            m.uF = s("uF", [P, GROUPS, SEQ])
            m.ab = s("ab2", [P, NT, GROUPS, 2 * P])
            m.fT = s("fT", [P, GROUPS, SEQ])
            m.uP = s("uP", [P, GROUPS, SEQ + 2 * PADP])
            m.d1 = s("d1", [P, GROUPS, SEQ + 2 * PADP])
            m.d2 = s("d2", [P, GROUPS, SEQ + 2 * PADP])
            m.c = s("c2", [P, 2, SEQ])
            m.v = s("v2", [P, 2, SEQ])
            m.z = s("z2", [P, GROUPS, SEQ + 2])
            m.cv = s("cv2", [P, 2, SEQ])
            m.bc = s("bc2", [P, GROUPS, 2, SEQ], F32R)
            m.yf = s("yf", [P, KT, SEQ])
            m.yc = m.ab[:, :, :, :].rearrange("p t g c -> p (t g) c")
            m.yp = s("yp", [P, KT, SEQ])
            m.gs = s("gs", [P, 2, SEQ])
            m.th = s("th", [P, 2, SEQ])
            m.cvp = m.yf[:, 0:GROUPS, :]
            m.mg = s("mg", [P, 2, SEQ])
            return m

        c1 = ExitStack()
        with c1:
            m1 = scope1(c1)
        c2 = ExitStack()
        with c2:
            m2 = scope2(c2)

        def ffn_weights(L, which):
            l = L % DEPTH
            if L < DEPTH:
                n = "ffn1" if which == 0 else "ffn2"
                return T[n + "_w_gate"][l], T[n + "_w_up"][l], T[n + "_w_down"][l]
            s = "a" if which == 0 else "b"
            return T[f"w1_{s}_2"][l], T[f"w3_{s}_2"][l], T[f"w2_{s}_2"][l]

        block = ctx.enter_context(nc.Block())

        def a_flat(tile, nt=KT):
            return tile[:, 0:nt * 2 * P].rearrange("p (t n) -> p t n", t=nt)

        def a_gate_up(tile):
            return tile[:, :].rearrange("p (g t n) -> p g t n", g=2, t=KT)

        def two(ap):
            return ap.rearrange("p (t c) -> p t c", t=2)

        @block.sync
        def _(sp):
            k = 0
            b = 0

            def rows(w):
                return w.rearrange("(t p) n -> p t n", p=P)

            def gate_up_unit(wg, wu, at, u, wait):
                sp.wait_ge(a_split, wait)
                dst = a_gate_up(raw_a[u])
                sp.dma_start(dst[:, 0], rows(wg)[:, :, at]).then_inc(a_full[u], 16)
                sp.dma_start(dst[:, 1], rows(wu)[:, :, at]).then_inc(a_full[u], 16)

            def down_unit(wd, at, v, wait):
                sp.wait_ge(b_split, wait)
                sp.dma_start(raw_b[v][:, :], wd[at, :]).then_inc(b_full[v], 16)

            def first_gate_up(L, which):
                nonlocal k
                wg, wu, _ = ffn_weights(L, which)
                gate_up_unit(wg, wu, slice(0, P), k % 2, k + 1)
                k += 1

            def ffn(L, which, following):
                nonlocal k, b
                wg, wu, wd = ffn_weights(L, which)
                with sp.Fori(0, FFU // 2 - 1) as i:
                    for e in range(2):
                        gate_up_unit(wg, wu, bass.ds(i * (2 * P) + (e + 1) * P, P), (k + e) % 2, i * 2 + (k + e + 1))
                        down_unit(wd, bass.ds(i * (2 * P) + e * P, P), (b + e) % 2, i * 2 + (b + e + 1))
                k += FFU - 2
                b += FFU - 2
                gate_up_unit(wg, wu, slice((FFU - 1) * P, FFU * P), k % 2, k + 1)
                down_unit(wd, slice((FFU - 2) * P, (FFU - 1) * P), b % 2, b + 1)
                k += 1
                following()
                down_unit(wd, slice((FFU - 1) * P, FFU * P), (b + 1) % 2, b + 2)
                b += 2

            def panel(w, start, nt=KT):
                nonlocal k
                sp.wait_ge(a_split, k + 1)
                sp.dma_start(a_flat(raw_a[k % 2], nt), rows(w)[:, :, start:start + 2 * P])\
                  .then_inc(a_full[k % 2], 32)
                k += 1

            def row_unit(w, j):
                nonlocal b
                sp.wait_ge(b_split, b + 1)
                sp.dma_start(raw_b[b % 2][:, :], w[j * P:(j + 1) * P, :]).then_inc(b_full[b % 2], 16)
                b += 1

            sp.dma_start(eye[:, :], T["k_eye"]).then_inc(consts_in, 16)
            for t in range(NT):
                sp.dma_start(x[:, t, :], T["x"][0, t * P:(t + 1) * P, :]).then_inc(consts_in, 16)
            first_gate_up(0, 0)
            for L in range(2 * DEPTH):
                l = L % DEPTH
                if L < DEPTH:
                    ffn(L, 0, lambda: panel(T["w_in"][l], PANELS1[0][1]))
                    for _, start in PANELS1[1:]:
                        panel(T["w_in"][l], start)
                    first_gate_up(L, 1)
                    for j in range(KT):
                        row_unit(T["w_out"][l], j)
                else:
                    w = T["w_in_2"][l]
                    ffn(L, 0, lambda: panel(w, OFF2["F"]))
                    for name, j in PANELS2[1:]:
                        panel(w, OFF2[name] + j * 2 * P)
                    for j in range(4):
                        panel(T["w_conv_out_2"][l], j * 2 * P, nt=4)
                    panel(w, OFF2["G"])
                    for m in range(4):
                        for g in (1, 2):
                            panel(w, OFF2["G"] + g * DM + m * 2 * P)
                        if m < 3:
                            panel(w, OFF2["G"] + (m + 1) * 2 * P)
                        else:
                            first_gate_up(L, 1)
                        row_unit(T["w_o_2"][l], 2 * m)
                        row_unit(T["w_o_2"][l], 2 * m + 1)
                ffn(L, 1, (lambda: first_gate_up(L + 1, 0)) if L < 2 * DEPTH - 1 else (lambda: None))
                if l == DEPTH - 1:
                    g = T["final_norm"] if L < DEPTH else T["g_final_2"]
                    sp.wait_ge(xT_split, 4 * norms_before(L + 1))
                    sp.dma_start(xn[:, 1, :], g.rearrange("(o n) -> o n", o=1).broadcast_to([P, DM])).then_inc(gain_in, 16)
            for t in range(NT):
                sp.wait_ge(x_done, 6 * 2 * DEPTH + 2 + t + 1)
                sp.dma_start(out[0, t * P:(t + 1) * P, :], x[:, t, :]).then_inc(stored, 16)
            sp.wait_ge(stored, 16 * NT)

        @block.gpsimd
        def _(pool):
            nparam = 0

            def load_vectors(L):
                l = L % DEPTH
                if L < DEPTH:
                    names = [("ffn1", T["ffn1_norm"][l]), ("mix", T["mix_norm"][l]), ("q", T["mla_q_norm"][l]),
                             ("kv", T["mla_kv_norm"][l]), ("dww", T["conv_dw_w"][l]), ("dwb", T["conv_dw_b"][l]),
                             ("hsw", T["hy_short_w"][l]), ("hsb", T["hy_short_b"][l]), ("out", T["out_norm"][l]),
                             ("ffn2", T["ffn2_norm"][l])]
                    at = COL1
                else:
                    names = [("ffn1", T["g_ffn1_2"][l]), ("mix", T["g_mix_2"][l]), ("wc", T["w_conv_2"][l]),
                             ("ps", T["pool_scale_2"][l]), ("ffn2", T["g_ffn2_2"][l])]
                    at = COL2
                for n, ap in names:
                    o, cnt = at[n]
                    if len(ap.shape) == 1:
                        src = ap.rearrange("(c p) -> c p", p=P)
                    else:
                        src = ap.rearrange("j (c p) -> (j c) p", p=P)
                    pool.dma_start(xn[o:o + cnt, L // 2, (L % 2) * P:(L % 2 + 1) * P], src).then_inc(rows_in, 16)

            for L in range(2 * DEPTH):
                load_vectors(L)
            m = m1
            n_const = 0

            def const(dst, src):
                nonlocal n_const
                pool.dma_start(dst, src).then_inc(block1_in, 16)
                n_const += 1
            const(m.dft[:, :, :, :].rearrange("p a t n -> p (a t) n"), T["k_dft"].rearrange("a (t p) n -> p (a t) n", p=P))
            const(m.decay[:, :, :], T["k_decay"].rearrange("(t p) n -> p t n", p=P))
            const(m.rotm[:, :], T["k_rot"])
            const(m.invf[:, :], T["k_invf"])
            const(m.pos[:, :], T["positions"].broadcast_to([QKD, SEQ]))
            assert n_const == N_BLOCK1

            def powers(cols_, waits):
                pool.wait_ge(*waits)
                return pool.tensor_tensor(rstd[:, cols_], var[:, cols_], minus_half[:, cols_], ALU.pow)

            def load1(L):
                l = L % DEPTH
                if l:
                    pool.wait_ge(xT_split, 4 * (norms_before(L - 1) + 3))
                s = params_in[L]
                pool.dma_start(m.wqb[:, :, :], T["mla_w_qb"][l].rearrange("(t p) n -> p t n", p=P)).then_inc(s, 16)
                pool.dma_start(m.wkvb[:, :], T["mla_w_kvb"][l]).then_inc(s, 16)
                pool.dma_start(m.w4, T["hy_filt_w4"][l]).then_inc(s, 16)
                pool.dma_start(m.emb, T["k_emb"]).then_inc(s, 16)
                pool.dma_start(m.w1, T["hy_filt_w1"][l]).then_inc(s, 16)
                pool.dma_start(m.w2, T["hy_filt_w2"][l]).then_inc(s, 16)
                pool.dma_start(m.w3, T["hy_filt_w3"][l]).then_inc(s, 16)
                for i, n in enumerate(("hy_filt_b1", "hy_filt_b2", "hy_filt_b3", "hy_filt_freq")):
                    pool.dma_start(m.fcol[:, i:i + 1], T[n][l].rearrange("(p o) -> p o", o=1)).then_inc(s, 16)
                pool.dma_start(m.dB, T["hy_bias_d"][l].rearrange("(q o) c -> q o c", q=1).broadcast_to([P, 2, CW])).then_inc(s, 16)
                for i, n in enumerate(("conv_ln_g", "conv_ln_b")):
                    pool.dma_start(m.lngb[:, i, :], T[n][l].rearrange("(o c) -> o c", o=1).broadcast_to([P, CW])).then_inc(s, 16)

            def load2(L):
                l = L % DEPTH
                m = m2
                s = params_in[L]
                if l:
                    pool.wait_ge(xT_split, 4 * (norms_before(L - 1) + 3))
                else:
                    pool.wait_ge(xT_split, 4 * (norms_before(L - 1) + 3))
                    pool.dma_start(m.seq[:, :, :, :].rearrange("p a t n -> p (a t) n"),
                                   T["k_seq"].rearrange("a (t p) n -> p (a t) n", p=P)).then_inc(block2_in, 16)
                    pool.dma_start(m.chan[:, :], T["k_chan"]).then_inc(block2_in, 16)
                    pool.dma_start(m.count[:, :, :], T["k_count"]).then_inc(block2_in, 16)
                pool.dma_start(m.wf[:, :, :], T["w_fourier_2"][l].rearrange("g p n -> p g n")).then_inc(s, 16)
                pool.dma_start(m.wp[:, :, :], T["w_pool_2"][l].rearrange("g p n -> p g n")).then_inc(s, 16)

            vk = 0

            def norm():
                nonlocal vk
                vk += 1
                powers(slice(0, 2), (var_done, vk)).then_inc(rstd_done, 1)

            pool.wait_ge(half_set, 1)
            for L in range(2 * DEPTH):
                if L < DEPTH:
                    load1(L)
                    norm()
                    norm()
                    pool.wait_ge(taken[small[L, "stat"] % 4], small[L, "stat"] // 4 + 1)
                    pool.tensor_tensor(rstd[:, 0:4], var[:, 0:4], minus_half[:, 0:4], ALU.pow).then_inc(ev["qkv_rstd"], 1)
                    pool.wait_ge(ev["ln_var"], nth(L, "ln_var"))
                    pool.tensor_tensor(rstd[:, 6:8], var[:, 6:8], minus_half[:, 6:8], ALU.pow).then_inc(ev["ln_rstd"], 1)
                    vk += 1
                    powers(slice(0, 6), (var_done, vk)).then_inc(rstd_done, 1)
                else:
                    load2(L)
                    norm()
                    norm()
                norm()
                if L % DEPTH == DEPTH - 1:
                    norm()

        @block.tensor
        def _(pe):
            k = b = h = 0
            n = 0
            done = {}

            pe.wait_ge(half_set, 1)
            pe.matmul(pair[0][0:1, 0, 0:4], ones[:, 0:1], ones[:, 0:4], start=True, stop=True).then_inc(proj_done, CREDIT)
            pe.matmul(pair[1][0:1, 0, 0:4], ones[:, 0:1], ones[:, 0:4], start=True, stop=True).then_inc(down_done, CREDIT)
            pe.wait_ge(consts_in, 16 * 3)
            pe.wait_ge(rows_in, 16 * 30)
            for L in range(2 * DEPTH):
                r = ROWS1 if L < DEPTH else ROWS2
                mm = pe.transpose(acc[:, 0, L * P:L * P + r], xn[0:r, L // 2, (L % 2) * P:(L % 2 + 1) * P], eye[0:r, 0:r])
            mm.then_inc(rows_T, 1)

            def transposes():
                nonlocal n
                for t in range(NT):
                    pe.wait_ge(xn_done, NT * n + t + 1)
                    for kt in range(KT):
                        o = (kt % 2) * SEQ + t * P
                        mm = pe.transpose(acc[:, kt // 2, o:o + P], xn[:, t, kt * P:(kt + 1) * P], eye[:, :])
                        if t == NT - 1 and kt % 2:
                            mm.then_inc(xT_in_psum, 1)
                n += 1

            def project(k, par, blocks, src, nt, first):
                pe.wait_ge(a_hi_ready, k + 1)
                pe.wait_ge(a_split, k + 1 + CREDIT)
                pe.wait_ge(pair_summed, k + 1)
                if first:
                    for kt in range(nt):
                        if kt % 2 == 0:
                            pe.wait_ge(xT_split, 4 * (n - 1) + kt // 2 + 1)
                        for e in range(2):
                            hi, lo = blocks(a_hi[par], e, kt), blocks(a_lo[par], e, kt)
                            pe.matmul(pair[par][:, e, :], hi, src[:, kt, :, :], start=(kt == 0), stop=False)
                            mm = pe.matmul(pair[par][:, e, 0:SEQ], lo, src[:, kt, 0, :], start=False, stop=(kt == nt - 1))
                else:
                    for e in range(2):
                        for kt in range(nt):
                            hi, lo = blocks(a_hi[par], e, kt), blocks(a_lo[par], e, kt)
                            pe.matmul(pair[par][:, e, :], hi, src[:, kt, :, :], start=(kt == 0), stop=False)
                            mm = pe.matmul(pair[par][:, e, 0:SEQ], lo, src[:, kt, 0, :], start=False, stop=(kt == nt - 1))
                mm.then_inc(proj_done, 1)

            def gate_up(tile, e, kt):
                return a_gate_up(tile)[:, e, kt, :]

            def panel_block(tile, e, kt):
                return a_flat(tile)[:, kt, e * P:(e + 1) * P]

            def kv_block(tile, e, kt):
                return a_flat(tile)[:, kt, e * NOPE:e * NOPE + P]

            def conv_block(tile, e, kt):
                return a_flat(tile, 4)[:, kt, e * P:(e + 1) * P]

            def down(b, par, parts, first, last):
                pe.wait_ge(b_hi_ready, b + 1)
                pe.wait_ge(b_split, b + 1 + CREDIT)
                for t in range(NT):
                    hi, lo = parts(t)
                    for j in range(2):
                        pe.matmul(acc[:, 2 * t + j, :], hi, b_hi[par][:, j * HALF:(j + 1) * HALF], start=first, stop=False)
                    for j in range(2):
                        pe.matmul(acc[:, 2 * t + j, :], hi, b_lo[par][:, j * HALF:(j + 1) * HALF], start=False, stop=False)
                    for j in range(2):
                        mm = pe.matmul(acc[:, 2 * t + j, :], lo, b_hi[par][:, j * HALF:(j + 1) * HALF], start=False, stop=last)
                    if last and t == 0:
                        mm.then_inc(acc_half, 1)
                mm.then_inc(down_done, 1)

            def from_h(h, par):
                pe.wait_ge(h_hi_ready, h + 1)
                pe.wait_ge(h_split, h + 1)
                return lambda t: (hT[par][:, 0, t * P:(t + 1) * P], hT[par][:, 1, t * P:(t + 1) * P])

            def ffn(L):
                nonlocal k, b, h
                transposes()
                project(k, k % 2, gate_up, xT, KT, True)
                project(k + 1, (k + 1) % 2, gate_up, xT, KT, False)
                down(b, b % 2, from_h(h, h % 2), True, False)
                with pe.Fori(0, FFU // 2 - 1) as i:
                    for e in range(2):
                        project(i * 2 + (k + 2 + e), (k + e) % 2, gate_up, xT, KT, False)
                        down(i * 2 + (b + 1 + e), (b + 1 + e) % 2, from_h(i * 2 + (h + 1 + e), (h + 1 + e) % 2), False, False)
                down(b + FFU - 1, (b + FFU - 1) % 2, from_h(h + FFU - 1, (h + FFU - 1) % 2), False, True)
                k += FFU
                b += FFU
                h += FFU

            def take(L, name):
                s = small[L, name]
                if s >= 4:
                    pe.wait_ge(taken[s % 4], s // 4)
                return acc[:, s % 4, :]

            def got(L, name):
                s = small[L, name]
                pe.wait_ge(taken[s % 4], s // 4 + 1)

            def mixer1(L):
                nonlocal k, b
                m = m1
                cf, sf, ci, si = (m.dft[:, i] for i in range(4))
                pe.wait_ge(params_in[L], 16 * N_PARAM1)
                if L == 0:
                    pe.wait_ge(block1_in, 16 * N_BLOCK1)
                    pe.wait_ge(ev["rope_done"], 2)
                transposes()
                pk = {}
                ip = 0
                for it in order_mix1():
                    i = int(it[-1]) if it[-1].isdigit() else None
                    kind = it.rstrip("0123456789")
                    if it == "A":
                        project(k, k % 2, kv_block if PANELS1[ip][0] == "kv" else panel_block, xT, KT, ip == 0)
                        ip += 1
                        k += 1
                    elif kind == "f":
                        o = take(L, it)
                        if i == 0:
                            pe.matmul(o[0:FILT, 0:SEQ], m.w1, m.emb, start=True, stop=True).then_inc(made, 1)
                        else:
                            pe.wait_ge(ev["filt_hidden"], nth(L, "filt_hidden", i - 1))
                            pe.matmul(o[0:FILT, 0:SEQ], (m.w2, m.w3)[i - 1], m.hdn, start=True, stop=True).then_inc(made, 1)
                    elif it == "stat":
                        o = take(L, it)
                        pe.wait_ge(ev["qkv_squares"], nth(L, "qkv_squares"))
                        for t in range(NT):
                            for e in range(2):
                                pe.matmul(o[:, t:t + 1], gu[:, e, t * P:(t + 1) * P], ones[:, 0:1], start=(e == 0), stop=(e == 1))
                        for t in range(NT):
                            mm = pe.matmul(o[:, NT + t:NT + t + 1], sh[:, 0, t * P:(t + 1) * P], ones[:, 0:1], start=True, stop=True)
                        mm.then_inc(made, 1)
                    elif kind == "h":
                        pe.wait_ge(ev["filt_hidden"], nth(L, "filt_hidden", 2))
                        for t in range(NT):
                            o = take(L, f"{it}t{t}")
                            pe.matmul(o, m.hdn[:, t * P:(t + 1) * P], m.w4[:, i * 2 * CW:(i + 1) * 2 * CW],
                                      start=True, stop=True).then_inc(made, 1)
                    elif it == "kb":
                        o = take(L, it)
                        pe.wait_ge(ev["kv_diag"], nth(L, "kv_diag"))
                        for t in range(NT):
                            mm = pe.matmul(o[:, t * P:(t + 1) * P], ones[:, :], m.kvn[:, t * P:(t + 1) * P], start=True, stop=True)
                        mm.then_inc(made, 1)
                    elif it == "values":
                        got(L, "kb")
                        wv = m.wkvb[:, :].rearrange("p (h c) -> p h c", h=HEADS)[:, :, NOPE:NOPE + VD]
                        for t in range(NT):
                            o = take(L, f"val{t}")
                            pe.matmul(o.rearrange("p (h c) -> p h c", h=HEADS), m.kvn[:, t * P:(t + 1) * P], wv,
                                      start=True, stop=True).then_inc(made, 1)
                    elif kind == "short":
                        o = take(L, it)
                        pe.wait_ge(ev["short_done"], nth(L, "short_done", i))
                        for t in range(NT):
                            for e in range(2):
                                mm = pe.transpose(o[:, t * CW + e * P:t * CW + (e + 1) * P], m.sc[:, e, t * P:(t + 1) * P], eye[:, :])
                        mm.then_inc(made, 1)
                    elif kind == "n":
                        o = take(L, it)
                        pe.wait_ge(ev["filt_abs"], nth(L, "filt_abs", i))
                        pe.wait_ge(ev["filt_sums"], nth(L, "filt_sums", i))
                        for j in range(4):
                            pe.matmul(o[:, 0:CW], ones[:, :], m.ab[:, j // 2, j % 2, :], start=(j == 0), stop=(j == 3))
                        for t in range(NT):
                            mm = pe.matmul(o[0:1, CW:2 * CW], sf[:, t, 0:1], m.ks[:, t, :], start=(t == 0), stop=(t == NT - 1))
                        mm.then_inc(made, 1)
                    elif kind == "spec" or kind == "fwd":
                        if kind == "spec":
                            srcs = [("A", cf, m.ks), ("B", sf, m.kd)]
                        else:
                            got(L, "short0" if i == 0 else "inv0")
                            srcs = [("re", cf, m.tv[0]), ("im", sf, m.tv[0])]
                        for nm, mat, src in srcs:
                            o = take(L, f"{nm}{i}")
                            for ft in range(2):
                                for t in range(NT):
                                    mm = pe.matmul(o[:, ft * CW:(ft + 1) * CW], mat[:, t, ft * P:(ft + 1) * P], src[:, t, :],
                                                   start=(t == 0), stop=(t == NT - 1))
                            mm.then_inc(made, 1)
                    elif kind == "inv":
                        o = take(L, it)
                        pe.wait_ge(ev["spectrum"], nth(L, "spectrum", i))
                        for t in range(NT):
                            for ft in range(2):
                                pe.matmul(o[:, t * CW:(t + 1) * CW], ci[:, ft, t * P:(t + 1) * P], m.Yr[:, ft, :],
                                          start=(ft == 0), stop=False)
                                mm = pe.matmul(o[:, t * CW:(t + 1) * CW], si[:, ft, t * P:(t + 1) * P], m.Yi[:, ft, :],
                                               start=False, stop=(ft == 1))
                        mm.then_inc(made, 1)
                    elif kind == "q":
                        o = take(L, it)
                        pe.wait_ge(ev["q_gained"], nth(L, "q_gained"))
                        for e in range(2):
                            c = (2 * i + e) * QKD
                            for j in range(2):
                                mm = pe.matmul(o[0:QKD, e * SEQ:(e + 1) * SEQ], m.wqb[:, j, c:c + QKD], m.qn[:, j, :],
                                               start=(j == 0), stop=(j == 1))
                        mm.then_inc(made, 1)
                    elif kind == "rot":
                        o = take(L, it)
                        got(L, f"q{i}")
                        pe.matmul(o[0:QKD, :], m.rotm[:, :], m.qraw, start=True, stop=True).then_inc(made, 1)
                    elif it == "kpe":
                        o = take(L, it)
                        pe.matmul(o[0:QKD, 0:SEQ], m.rotm[NOPE:QKD, :], m.hk[NOPE:QKD, 1, :], start=True, stop=True).then_inc(made, 1)
                    elif kind == "k":
                        o = take(L, it)
                        got(L, "kb")
                        for e in range(2):
                            c = (2 * i + e) * (NOPE + VD)
                            mm = pe.matmul(o[0:NOPE, e * SEQ:(e + 1) * SEQ], m.wkvb[:, c:c + NOPE], m.kvn[:, :], start=True, stop=True)
                        mm.then_inc(made, 1)
                    elif kind == "s":
                        o = take(L, it)
                        p2, e = i // 2, i % 2
                        pe.wait_ge(ev["q_roped"], nth(L, "q_roped", p2))
                        pe.wait_ge(ev["kpe_roped"], nth(L, "kpe_roped"))
                        got(L, f"k{p2}")
                        for t in range(NT):
                            mm = pe.matmul(o[:, t * SEQ:(t + 1) * SEQ], m.qp[p2 % 2][:, e * SEQ + t * P:e * SEQ + (t + 1) * P],
                                           m.kT[p2 % 2][:, e * SEQ:(e + 1) * SEQ], start=True, stop=True)
                        mm.then_inc(made, 1)
                    elif kind == "p":
                        o = take(L, it)
                        got(L, f"s{i}")
                        for t in range(NT):
                            for kk in range(NT):
                                mm = pe.transpose(o[:, kk * SEQ + t * P:kk * SEQ + (t + 1) * P],
                                                  m.Pm[i % 2][:, t, kk * P:(kk + 1) * P], eye[:, :])
                        mm.then_inc(made, 1)
                    elif kind == "o":
                        o = take(L, it)
                        got(L, f"p{i}")
                        got(L, "val1")
                        for t in range(NT):
                            for kk in range(NT):
                                mm = pe.matmul(o[:, t * VD:(t + 1) * VD], m.PT[i % 2][:, kk * SEQ + t * P:kk * SEQ + (t + 1) * P],
                                               m.V[:, kk, i * VD:(i + 1) * VD], start=(kk == 0), stop=(kk == NT - 1))
                        mm.then_inc(made, 1)
                    elif it == "conv_out":
                        o = take(L, it)
                        pe.wait_ge(ev["conv_done"], nth(L, "conv_done"))
                        for t in range(NT):
                            for e in range(2):
                                mm = pe.transpose(o[:, t * CW + e * P:t * CW + (e + 1) * P], m.co[:, e, t * P:(t + 1) * P], eye[:, :])
                        mm.then_inc(made, 1)
                transposes()
                pe.wait_ge(xT_split, 4 * n)
                for j in range(KT):
                    down(b, b % 2, lambda t, j=j: (xT[:, j, 0, t * P:(t + 1) * P], xT[:, j, 1, t * P:(t + 1) * P]),
                         j == 0, j == KT - 1)
                    b += 1

            def mixer2(L):
                nonlocal k, b, h
                m = m2
                transposes()
                first_k = k
                ia = gm = 0
                for it in order_mix2():
                    i = int(it[-1]) if it[-1].isdigit() else None
                    if it == "A":
                        project(k, k % 2, panel_block, xT, KT, ia == 0)
                        ia += 1
                        k += 1
                        if ia == 1:
                            pe.wait_ge(params_in[L], 16 * N_PARAM2)
                            pe.wait_ge(block2_in, 16 * N_BLOCK2)
                    elif it[0] == "c":
                        o = take(L, it)
                        pe.wait_ge(pair_summed, first_k + i // 2 + 1 + CREDIT)
                        for t in range(NT):
                            mm = pe.matmul(o[:, t * SEQ:(t + 1) * SEQ], m.uF[:, i, t * P:(t + 1) * P], m.chan[:, :], start=True, stop=True)
                        mm.then_inc(made, 1)
                    elif it[0] == "t":
                        o = take(L, it)
                        got(L, f"c{2 * i + 1}")
                        got(L, f"c{2 * i}")
                        for e in range(2):
                            g = 2 * i + e
                            for t in range(NT):
                                for a in range(2):
                                    mm = pe.matmul(o[:, e * SEQ:(e + 1) * SEQ], m.ab[:, t, g, a * P:(a + 1) * P], m.seq[:, a, t, :],
                                                   start=(t == 0 and a == 0), stop=(t == NT - 1 and a == 1))
                        mm.then_inc(made, 1)
                    elif it[:2] in ("yf", "yp"):
                        o = take(L, it)
                        if it[1] == "f":
                            got(L, f"t{i // 2}")
                            w, src = m.wf, m.fT[:, i, :]
                        else:
                            pe.wait_ge(ev["pooled"], nth(L, "pooled"))
                            w, src = m.wp, m.d1[:, i, 0:SEQ]
                        for e in range(2):
                            mm = pe.matmul(o[:, e * SEQ:(e + 1) * SEQ], w[:, i, e * P:(e + 1) * P], src, start=True, stop=True)
                        mm.then_inc(made, 1)
                    elif it[0] == "Y":
                        if i == 0:
                            pe.wait_ge(ev["bc_split"], nth(L, "bc_split", 1))
                        project(k, k % 2, conv_block, m.bc, 4, False)
                        k += 1
                    elif it == "G":
                        for g in range(3):
                            project(k, k % 2, panel_block, xT, KT, False)
                            k += 1
                            if g == 0 and gm == 0:
                                for s in range(4):
                                    got(L, f"yp{s}")
                            if g == 0 and gm > 0:
                                for e in range(2):
                                    down(b, b % 2, from_h(h, h % 2), gm == 1 and e == 0, False)
                                    b += 1
                                    h += 1
                        gm += 1
                for e in range(2):
                    down(b, b % 2, from_h(h, h % 2), False, e == 1)
                    b += 1
                    h += 1

            for L in range(2 * DEPTH):
                ffn(L)
                if L < DEPTH:
                    mixer1(L)
                else:
                    mixer2(L)
                ffn(L)

        @block.scalar
        def _(act):
            k = b = h = f = n = xk = sq = 0
            steps = 0

            def link(ins):
                nonlocal steps
                steps += 1
                ins.then_inc(act_step, 1)
                act.wait_ge(act_step, steps)

            def split_a(k, par, use):
                act.wait_ge(a_full[par], (use + 1) * 32)
                act.wait_ge(proj_done, k + 1)
                act.activation(a_hi[par][:, :], raw_a[par][:, :], ACT.Copy).then_inc(a_hi_ready, 1)

            def split_b(b, par, use):
                act.wait_ge(b_full[par], (use + 1) * 16)
                act.wait_ge(down_done, b + 1)
                act.activation(b_hi[par][:, :], raw_b[par][:, :], ACT.Copy).then_inc(b_hi_ready, 1)

            def second_half(k, par):
                act.wait_ge(proj_done, k + 1 + CREDIT)
                act.wait_ge(pair_summed, k + CREDIT)
                act.activation(second[:, :, :], pair[par][:, :, SEQ:2 * SEQ], ACT.Copy).then_inc(second_out, 1)

            def squares(x_at, wait):
                nonlocal sq
                for t in range(NT):
                    wait(t)
                    ins = act.activation(xn[:, x_at(t), :], x[:, t, :], ACT.Square, accum_out=ssq[:, t:t + 1])
                    if t < NT - 1:
                        link(ins)
                ins.then_inc(ssq_done, 1)
                sq += 1

            def norm_to_xT(L, gain):
                nonlocal n
                for q in range(4):
                    act.wait_ge(xT_in_psum, 4 * n + q + 1)
                    for e in range(2):
                        kt = 2 * q + e
                        ins = act.activation(xT[:, kt, 0, :], acc[:, q, e * SEQ:(e + 1) * SEQ], ACT.Copy, scale=colv(L, gain, kt))
                    ins.then_inc(xT_hi, 1)
                n += 1

            def x_ready(t):
                if xk:
                    act.wait_ge(x_done, xk - NT + t + 1)
                elif t == 0:
                    act.wait_ge(consts_in, 16 * 3)

            def ffn_step(k, b, m, h, ka, kb_, kh, ua, ub, more=True):
                if more:
                    split_a(k + 1, (ka + 1) % 2, ua)
                split_b(b, kb_, ub)
                second_half(k, ka)
                act.wait_ge(pair_summed, k + 1 + CREDIT)
                act.activation(sh[:, 0, :], gu[:, 0, :], ACT.Silu).then_inc(silu_done, 1)
                act.wait_ge(h_done, m + 1)
                act.activation(hT[kh][:, 0, :], sh[:, 1, :], ACT.Copy).then_inc(h_hi_ready, 1)

            def ffn(L, gain, last):
                nonlocal k, b, h, f, xk
                squares(lambda t: t, x_ready)
                norm_to_xT(L, gain)
                with act.Fori(0, FFU // 2 - 1 if last else FFU // 2) as i:
                    for e in range(2):
                        ffn_step(i * 2 + (k + e), i * 2 + (b + e), i * 2 + (f + e), i * 2 + (h + e), (k + e) % 2, (b + e) % 2,
                                 (h + e) % 2, i + (k + e + 1) // 2, i + (b + e) // 2)
                if last:
                    for j in (FFU - 2, FFU - 1):
                        ffn_step(k + j, b + j, f + j, h + j, (k + j) % 2, (b + j) % 2, (h + j) % 2, (k + j + 1) // 2,
                                 (b + j) // 2, more=j < FFU - 1)
                k += FFU
                b += FFU
                h += FFU
                f += FFU
                xk += NT

            def read(L, name):
                act.wait_ge(made, small[L, name] + 1)
                return acc[:, small[L, name] % 4, :]

            def free(L, name):
                return taken[small[L, name] % 4]

            def panel():
                nonlocal k
                split_a(k + 1, (k + 1) % 2, (k + 1) // 2)
                second_half(k, k % 2)
                k += 1

            def row_split():
                nonlocal b
                split_b(b, b % 2, b // 2)
                b += 1

            def mixer1(L):
                nonlocal k, b, xk, sq, h
                m = m1
                squares(lambda t: t, x_ready)
                norm_to_xT(L, "mix")
                pk = {}
                ip = 0
                rows_done = 0
                for it in order_mix1():
                    i = int(it[-1]) if it[-1].isdigit() else None
                    kind = it.rstrip("0123456789")
                    if it == "A":
                        pk[PANELS1[ip][0]] = k
                        panel()
                        ip += 1
                    elif it == "B":
                        row_split()
                        rows_done += 1
                    elif it == "glu":
                        act.wait_ge(pair_summed, pk["cg"] + 1 + CREDIT)
                        act.activation(m.cg[:, :, :], m.cg[:, :, :], ACT.Tanh, scale=0.5).then_inc(ev["gate_tanh"], 1)
                    elif kind == "f":
                        act.wait_ge(ev["filt_arg"], nth(L, "filt_arg", i))
                        act.activation(m.hdn, m.farg, ACT.Sin).then_inc(ev["filt_hidden"], 1)
                    elif kind == "h":
                        act.wait_ge(ev["filt_taps"], nth(L, "filt_taps", i))
                        act.activation(m.ab, m.kt, ACT.Abs).then_inc(ev["filt_abs"], 1)
                    elif it == "qkv_sq":
                        act.wait_ge(pair_summed, pk["kv"] + 1 + CREDIT)
                        act.activation(gu[:, :, :], m.hq[:, :, :], ACT.Square)
                        act.activation(sh[:, 0, :], m.hk[:, 0, :], ACT.Square).then_inc(ev["qkv_squares"], 1)
                        act.wait_ge(ev["qkv_squares"], nth(L, "qkv_squares"))
                        for e in range(2):
                            ins = act.activation(m.qn[:, e, :], m.hq[:, e, :], ACT.Copy, scale=colv(L, "q", e))
                        ins.then_inc(ev["q_gained"], 1)
                    elif it == "values":
                        for t in range(NT):
                            o = read(L, f"val{t}")
                            act.activation(m.V[:, t, :], o, ACT.Copy).then_inc(free(L, f"val{t}"), 1)
                    elif kind == "short":
                        act.wait_ge(pair_summed, pk[("v", "x1", "x2")[i]] + 1 + CREDIT)
                        for e in range(2):
                            ins = act.activation(m.sc[:, e, :], m.hs[:, e, 1:SEQ + 1], ACT.Identity,
                                                 scale=colv(L, "hsw", 6 + 2 * i + e), bias=colv(L, "hsb", 2 * i + e))
                        ins.then_inc(ev["short_mid"], 1)
                        o = read(L, it)
                        act.activation(m.tv[i][:, :, :], two(o), ACT.Copy).then_inc(free(L, it), 1)
                    elif kind == "q":
                        o = read(L, it)
                        if i:
                            act.wait_ge(ev["q_roped"], nth(L, "q_roped", i - 1))
                        act.activation(m.qraw, o[0:QKD, :], ACT.Copy).then_inc(free(L, it), 1)
                    elif kind == "k" and i is not None:
                        o = read(L, it)
                        act.activation(m.kT[i % 2][0:NOPE, :], o[0:NOPE, :], ACT.Copy).then_inc(free(L, it), 1)
                    elif kind == "s":
                        act.wait_ge(ev["neg_max"], nth(L, "neg_max", i))
                        o = read(L, it)
                        for t in range(NT):
                            ins = act.activation(m.Pm[i % 2][:, t, :], o[:, t * SEQ:(t + 1) * SEQ], ACT.Exp, scale=m.qs[:, t:t + 1],
                                                 bias=m.mx[:, 2 * i + t:2 * i + t + 1], accum_out=m.sm[:, 2 * i + t:2 * i + t + 1])
                        ins.then_inc(free(L, it), 1)
                    elif kind == "p":
                        o = read(L, it)
                        if i >= 2:
                            act.wait_ge(made, small[L, f"o{i - 2}"] + 1)
                        act.activation(m.PT[i % 2], o, ACT.Copy).then_inc(free(L, it), 1)
                    elif it == "conv_out":
                        act.wait_ge(ev["ln_done"], nth(L, "ln_done"))
                        y = xn[:, :, 2 * CW:3 * CW]
                        act.activation(y, y, ACT.Silu).then_inc(ev["conv_silu"], 1)
                    elif it == "y_norm":
                        act.wait_ge(ev["conv_silu"], nth(L, "conv_silu"))
                        act.wait_ge(taken[small[L, "o7"] % 4], small[L, "o7"] // 4 + 1)
                        act.wait_ge(taken[small[L, "inv1"] % 4], small[L, "inv1"] // 4 + 1)
                        for s, (lo, hi) in enumerate(((0, 512), (512, 768), (768, 1024))):
                            for t in range(NT):
                                ins = act.activation(second[:, :, :].rearrange("p a c -> p (a c)")[:, 0:hi - lo], xn[:, t, lo:hi],
                                                     ACT.Square, accum_out=ssq[:, 2 * s + t:2 * s + t + 1])
                                if (s, t) != (2, NT - 1):
                                    link(ins)
                        ins.then_inc(ssq_done, 1)
                        sq += 1
                norm_to_xT(L, "out")
                for j in range(rows_done, KT):
                    row_split()
                xk += NT

            def mixer2(L):
                nonlocal k, b, xk, h
                m = m2
                squares(lambda t: t, x_ready)
                norm_to_xT(L, "mix")
                gm = 0
                for it in order_mix2():
                    i = int(it[-1]) if it[-1].isdigit() else None
                    if it == "A" or it[0] == "Y":
                        panel()
                    elif it[0] == "c":
                        o = read(L, it)
                        act.activation(m.ab[:, :, i, :], two(o), ACT.Copy).then_inc(free(L, it), 1)
                    elif it[0] == "t":
                        o = read(L, it)
                        act.activation(m.fT[:, 2 * i:2 * i + 2, :], two(o), ACT.Copy).then_inc(free(L, it), 1)
                    elif it[:2] == "yf":
                        o = read(L, it)
                        act.activation(m.yf[:, 2 * i:2 * i + 2, :], two(o), ACT.Copy).then_inc(free(L, it), 1)
                    elif it[:2] == "yp":
                        o = read(L, it)
                        for e in range(2):
                            ins = act.activation(m.yp[:, 2 * i + e, :], o[:, e * SEQ:(e + 1) * SEQ], ACT.Copy, scale=colv(L, "ps", 2 * i + e))
                        ins.then_inc(free(L, it), 1)
                    elif it[:2] == "bc":
                        act.wait_ge(ev["bc_f32"], nth(L, "bc_f32", i))
                        act.activation(m.bc[:, 2 * i:2 * i + 2, 0, :], m.gs[:, :, :], ACT.Copy).then_inc(ev["bc_hi"], 1)
                    elif it == "G":
                        for g in range(3):
                            panel()
                            act.wait_ge(pair_summed, k + CREDIT)
                            act.activation(m.th[:, :, :], m.gs[:, :, :], ACT.Tanh, scale=0.5).then_inc(ev["gate_done"], 1)
                        for e in range(2):
                            row_split()
                        act.wait_ge(ev["merged"], nth(L, "merged", gm))
                        for e in range(2):
                            act.activation(hT[h % 2][:, 0, :], m.mg[:, e, :], ACT.Copy).then_inc(h_hi_ready, 1)
                            h += 1
                        gm += 1
                xk += NT

            def final_norm():
                nonlocal xk
                squares(lambda t: 0, x_ready)
                xk += NT

            for i in range(2):
                act.wait_ge(ev["rope_arg"], i + 1)
                act.activation(m1.cs[:, i, :], m1.ra[:, i, :], ACT.Sin).then_inc(ev["rope_done"], 1)
            act.wait_ge(cols_done, 1)
            split_a(0, 0, 0)
            for L in range(2 * DEPTH):
                ffn(L, "ffn1", False)
                if L < DEPTH:
                    mixer1(L)
                else:
                    mixer2(L)
                ffn(L, "ffn2", L == 2 * DEPTH - 1)
                if L % DEPTH == DEPTH - 1:
                    final_norm()

        @block.vector
        def _(dve):
            k = b = h = f = n = sq = vk = 0
            steps = 0

            def step(ins):
                nonlocal steps
                steps += 1
                ins.then_inc(dve_step, 1)
                return steps

            def link(ins):
                dve.wait_ge(dve_step, step(ins))

            def split_a(k, par):
                dve.wait_ge(a_hi_ready, k + 1)
                dve.tensor_tensor(a_lo[par][:, :], raw_a[par][:, :], a_hi[par][:, :], SUB).then_inc(a_split, 1)

            def split_b(b, par):
                dve.wait_ge(b_hi_ready, b + 1)
                dve.tensor_tensor(b_lo[par][:, :], raw_b[par][:, :], b_hi[par][:, :], SUB).then_inc(b_split, 1)

            def total(k, par, dst):
                dve.wait_ge(second_out, k + 1)
                dve.tensor_tensor(dst, pair[par][:, :, 0:SEQ], second[:, :, :], ADD).then_inc(pair_summed, 1)

            def variance(cols_, width):
                return dve.tensor_scalar(var[:, cols_], ssq[:, cols_], 1.0 / width, EPS, MULT, ADD)

            def xT_low(L, gain):
                nonlocal n
                for q in range(4):
                    dve.wait_ge(xT_hi, 4 * n + q + 1)
                    for e in range(2):
                        kt = 2 * q + e
                        ins = dve.scalar_tensor_tensor(xT[:, kt, 1, :], acc[:, q, e * SEQ:(e + 1) * SEQ], colv(L, gain, kt),
                                                       xT[:, kt, 0, :].bitcast(F32), MULT, SUB)
                    ins.then_inc(xT_split, 1)
                n += 1

            def norm(L, gain):
                nonlocal sq, vk
                sq += 1
                vk += 1
                dve.wait_ge(ssq_done, sq)
                variance(slice(0, 2), DM).then_inc(var_done, 1)
                dve.wait_ge(rstd_done, vk)
                for t in range(NT):
                    dve.tensor_scalar(xn[:, t, :], x[:, t, :], rstd[:, t:t + 1], None, MULT).then_inc(xn_done, 1)
                xT_low(L, gain)

            def update_x(scale, b):
                nonlocal phases
                phases += 1
                for t in range(NT):
                    if t == 0:
                        dve.wait_ge(acc_half, phases)
                    else:
                        dve.wait_ge(down_done, b + 1 + CREDIT)
                    dve.scalar_tensor_tensor(x[:, t, :], acc[:, 2 * t:2 * t + 2, :].rearrange("p a c -> p (a c)"), scale, x[:, t, :],
                                             MULT, ADD).then_inc(x_done, 1)
            phases = 0

            def h_low(h, kh, src):
                dve.wait_ge(h_hi_ready, h + 1)
                dve.tensor_tensor(hT[kh][:, 1, :], src, hT[kh][:, 0, :], SUB).then_inc(h_split, 1)

            def ffn(L, gain, last):
                nonlocal k, b, h, f
                norm(L, gain)

                def one(k, b, m, h, ka, kb_, kh, more=True):
                    if more:
                        split_a(k + 1, (ka + 1) % 2)
                    split_b(b, kb_)
                    total(k, ka, gu[:, :, :])
                    dve.wait_ge(silu_done, m + 1)
                    dve.tensor_tensor(sh[:, 1, :], sh[:, 0, :], gu[:, 1, :], MULT).then_inc(h_done, 1)
                    h_low(h, kh, sh[:, 1, :])
                with dve.Fori(0, FFU // 2 - 1 if last else FFU // 2) as i:
                    for e in range(2):
                        one(i * 2 + (k + e), i * 2 + (b + e), i * 2 + (f + e), i * 2 + (h + e), (k + e) % 2, (b + e) % 2, (h + e) % 2)
                if last:
                    for j in (FFU - 2, FFU - 1):
                        one(k + j, b + j, f + j, h + j, (k + j) % 2, (b + j) % 2, (h + j) % 2, j < FFU - 1)
                k += FFU
                b += FFU
                h += FFU
                f += FFU
                update_x(0.5, b - 1)

            def read(L, name):
                dve.wait_ge(made, small[L, name] + 1)
                return acc[:, small[L, name] % 4, :]

            def free(L, name):
                return taken[small[L, name] % 4]

            def took(L, name):
                dve.wait_ge(free(L, name), small[L, name] // 4 + 1)

            def panel(dst):
                nonlocal k
                split_a(k + 1, (k + 1) % 2)
                total(k, k % 2, dst)
                k += 1

            def row_split():
                nonlocal b
                split_b(b, b % 2)
                b += 1

            def reduced(src, tmp, dst, turn):
                link(dve.tensor_scalar(tmp, src, 1.0 / TWO_PI, turn, MULT, ADD))
                link(dve.tensor_scalar(tmp, tmp, ROUND, ROUND, ADD, SUB))
                link(dve.scalar_tensor_tensor(dst, tmp, -PI_A, src, MULT, ADD))
                link(dve.scalar_tensor_tensor(dst, tmp, -PI_B, dst, MULT, ADD))
                link(dve.scalar_tensor_tensor(dst, tmp, -PI_C, dst, MULT, ADD))
                if turn:
                    link(dve.tensor_scalar(dst, dst, TWO_PI * turn, None, ADD))
                return dve.tensor_scalar(dst, dst, PI_F, -PI_F, ALU.min, ALU.max)

            def bcast(ap, n_):
                q = ap.rearrange("p (o c) -> p o c", o=1)
                return q.broadcast_to([q.shape[0], n_, q.shape[2]])

            def mixer1(L):
                nonlocal k, b, sq, vk
                m = m1
                norm(L, "mix")
                dst = {"ca": m.ca[:, :, :], "cg": m.cg[:, :, :], "q": m.hq[:, :, :], "kv": m.hk[:, :, :],
                       "v": m.hs[:, :, 1:SEQ + 1], "x1": m.hs[:, :, 1:SEQ + 1], "x2": m.hs[:, :, 1:SEQ + 1]}
                dve.wait_ge(params_in[L], 16 * N_PARAM1)
                ip = taps = rows_done = 0
                tap_step = [0, 0]
                pk = {}
                for it in order_mix1():
                    i = int(it[-1]) if it[-1].isdigit() else None
                    kind = it.rstrip("0123456789")
                    if it == "A":
                        pk[PANELS1[ip][0]] = k
                        panel(dst[PANELS1[ip][0]])
                        ip += 1
                    elif it == "B":
                        row_split()
                        rows_done += 1
                    elif it == "glu":
                        dve.wait_ge(ev["gate_tanh"], nth(L, "gate_tanh"))
                        link(dve.scalar_tensor_tensor(m.u[:, :, PADC:PADC + SEQ], m.cg[:, :, :], 1.0, m.ca[:, :, :], ADD, MULT))
                    elif it == "taps":
                        for j in tap_range(taps):
                            for e in range(2):
                                src = m.u[:, e, j:j + SEQ]
                                if j == 0:
                                    tap_step[e] = step(dve.tensor_scalar(m.co[:, e, :], src, colv(L, "dww", 2 * j + e), None, MULT))
                                else:
                                    dve.wait_ge(dve_step, tap_step[e])
                                    tap_step[e] = step(dve.scalar_tensor_tensor(m.co[:, e, :], src, colv(L, "dww", 2 * j + e),
                                                                               m.co[:, e, :], MULT, ADD))
                        taps += 1
                    elif kind == "f":
                        o = read(L, it)
                        dve.tensor_scalar(m.farg, o[0:FILT, 0:SEQ], m.fcol[:, i:i + 1], m.fcol[:, 3:4], ADD, MULT).then_inc(free(L, it), 1)
                        took(L, it)
                        reduced(m.farg, m.fq, m.farg, 0.0).then_inc(ev["filt_arg"], 1)
                    elif kind == "h":
                        if i:
                            dve.wait_ge(ev["filt_abs"], nth(L, "filt_abs", i - 1))
                        for t in range(NT):
                            o = read(L, f"{it}t{t}")
                            dve.tensor_tensor(m.kt[:, t], two(o), bcast(m.decay[:, t, :], 2), MULT).then_inc(free(L, f"{it}t{t}"), 1)
                        for t in range(NT):
                            took(L, f"{it}t{t}")
                        link(dve.memset(m.kt[0:1, 0, 1, :], 0.0))
                        dve.tensor_tensor(m.ks, m.kt[:, :, 0, :], m.kt[:, :, 1, :], ADD).then_inc(ev["filt_taps"], 1)
                        dve.tensor_tensor(m.kd, m.kt[:, :, 0, :], m.kt[:, :, 1, :], SUB).then_inc(ev["filt_sums"], 1)
                    elif kind == "n":
                        o = read(L, it)
                        link(dve.reciprocal(m.rn, o[:, 0:CW]))
                        dve.tensor_tensor(m.KN[:, i, :], o[0:1, CW:2 * CW], m.rn[0:1, :], MULT).then_inc(free(L, it), 1)
                        took(L, it)
                        link(dve.tensor_tensor(m.KN[:, i, :], m.KN[:, i, :], m.dB[0:1, i, :], ADD))
                    elif kind == "spec":
                        o = read(L, f"A{i}")
                        dve.tensor_tensor(m.KA[i][:, :, :], two(o), bcast(m.rn, 2), MULT).then_inc(free(L, f"A{i}"), 1)
                        o = read(L, f"B{i}")
                        dve.tensor_tensor(m.KB[i][:, :, :], two(o), bcast(m.rn, 2), MULT).then_inc(free(L, f"B{i}"), 1)
                        took(L, f"A{i}")
                        link(dve.tensor_tensor(m.KA[i][:, :, :], m.KA[i][:, :, :], bcast(m.dB[:, i, :], 2), ADD))
                        took(L, f"B{i}")
                        link(dve.memset(m.KB[i][0:1, 0, :], 0.0))
                    elif it == "stat":
                        o = read(L, it)
                        dve.tensor_scalar(var[:, 0:2], o[:, 0:2], 1.0 / QR, EPS, MULT, ADD)
                        dve.tensor_scalar(var[:, 2:4], o[:, 2:4], 1.0 / KVR, EPS, MULT, ADD).then_inc(free(L, it), 1)
                        dve.wait_ge(ev["qkv_rstd"], nth(L, "qkv_rstd"))
                        dve.tensor_scalar(m.qs[:, 0:2], rstd[:, 0:2], float(QKD) ** -0.5, None, MULT)
                        link(dve.tensor_scalar(m.qs[:, 2:4], rstd[:, 0:2], -float(QKD) ** -0.5, None, MULT))
                        for t in range(NT):
                            ins = dve.tensor_scalar(m.kvn[:, t * P:(t + 1) * P], eye[:, :], rstd[:, 2 + t:3 + t], None, MULT)
                        ins.then_inc(ev["kv_diag"], 1)
                    elif it == "kb":
                        o = read(L, it)
                        dve.scalar_tensor_tensor(m.kvn[:, :], m.hk[:, 0, :], colv(L, "kv"), o[:, 0:SEQ], MULT, MULT).then_inc(free(L, it), 1)
                    elif kind == "short":
                        dve.wait_ge(ev["short_mid"], nth(L, "short_mid", i))
                        s0 = [step(dve.scalar_tensor_tensor(m.sc[:, e, :], m.hs[:, e, 0:SEQ], colv(L, "hsw", 2 * i + e), m.sc[:, e, :],
                                                            MULT, ADD)) for e in range(2)]
                        for e in range(2):
                            dve.wait_ge(dve_step, s0[e])
                            ins = dve.scalar_tensor_tensor(m.sc[:, e, :], m.hs[:, e, 2:SEQ + 2], colv(L, "hsw", 12 + 2 * i + e),
                                                           m.sc[:, e, :], MULT, ADD)
                        ins.then_inc(ev["short_done"], 1)
                    elif kind == "fwd":
                        r = read(L, f"re{i}")
                        link(dve.tensor_tensor(m.Yr[:, :, :], two(r), m.KA[i][:, :, :], MULT))
                        dve.tensor_tensor(m.Yi[:, :, :], two(r), m.KB[i][:, :, :], MULT).then_inc(free(L, f"re{i}"), 1)
                        q = read(L, f"im{i}")
                        link(dve.tensor_tensor(m.tmp[:, :, :], two(q), m.KB[i][:, :, :], MULT))
                        link(dve.tensor_tensor(m.Yr[:, :, :], m.Yr[:, :, :], m.tmp[:, :, :], SUB))
                        link(dve.tensor_tensor(m.tmp[:, :, :], two(q), m.KA[i][:, :, :], MULT))
                        took(L, f"re{i}")
                        link(dve.tensor_tensor(m.Yi[:, :, :], m.Yi[:, :, :], m.tmp[:, :, :], ADD))
                        dve.tensor_tensor(m.Yi[0:1, 0, :], q[0:1, 0:CW], m.KN[:, i, :], MULT).then_inc(free(L, f"im{i}"), 1)
                        took(L, f"im{i}")
                        dve.tensor_copy(m.mx[0:1, 0:1], m.Yi[0:1, 0, 0:1]).then_inc(ev["spectrum"], 1)
                    elif kind == "inv":
                        o = read(L, it)
                        if i == 0:
                            dve.wait_ge(free(L, "short1"), small[L, "short1"] // 4 + 1)
                            dve.tensor_tensor(m.tv[0][:, :, :], two(o), m.tv[1][:, :, :], MULT).then_inc(free(L, it), 1)
                        else:
                            dve.wait_ge(free(L, "short2"), small[L, "short2"] // 4 + 1)
                            dve.tensor_tensor(xn[:, :, 3 * CW:4 * CW], two(o), m.tv[2][:, :, :], MULT).then_inc(free(L, it), 1)
                    elif kind == "rot":
                        o = read(L, it)
                        took(L, f"q{i}")
                        link(dve.tensor_tensor(two(m.qc), two(m.qraw), bcast(m.cs[:, 0, :], 2), MULT))
                        dve.tensor_tensor(two(m.qp[i % 2]), two(o[0:QKD, :]), bcast(m.cs[:, 1, :], 2), MULT).then_inc(free(L, it), 1)
                        took(L, it)
                        dve.tensor_tensor(m.qp[i % 2], m.qp[i % 2], m.qc, ADD).then_inc(ev["q_roped"], 1)
                    elif it == "kpe":
                        r = slice(NOPE, QKD)
                        o = read(L, it)
                        link(dve.tensor_tensor(m.kpe[r], m.hk[r, 1, :], m.cs[r, 0, :], MULT))
                        dve.tensor_tensor(m.kpe2[r], o[r, 0:SEQ], m.cs[r, 1, :], MULT).then_inc(free(L, it), 1)
                        took(L, it)
                        for j in range(2):
                            ins = dve.tensor_tensor(two(m.kT[j])[r], bcast(m.kpe[r], 2), bcast(m.kpe2[r], 2), ADD)
                        ins.then_inc(ev["kpe_roped"], 1)
                    elif kind == "s":
                        o = read(L, it)
                        link(dve.tensor_reduce(m.mx[:, 2 * i:2 * i + 2], two(o), AX, ALU.max))
                        dve.tensor_tensor(m.mx[:, 2 * i:2 * i + 2], m.mx[:, 2 * i:2 * i + 2], m.qs[:, 2:4], MULT).then_inc(ev["neg_max"], 1)
                    elif kind == "o":
                        took(L, f"s{i}")
                        link(dve.reciprocal(m.rs[:, 2 * i:2 * i + 2], m.sm[:, 2 * i:2 * i + 2]))
                        o = read(L, it)
                        dve.tensor_tensor(xn[:, :, i * VD:(i + 1) * VD], o[:, 0:2 * VD].rearrange("p (t c) -> p t c", t=2),
                                          m.rs[:, 2 * i:2 * i + 2].rearrange("p (t o) -> p t o", o=1).broadcast_to([P, NT, VD]),
                                          MULT).then_inc(free(L, it), 1)
                    elif it == "conv_out":
                        for e in range(2):
                            dve.wait_ge(dve_step, tap_step[e])
                            ins = dve.tensor_scalar(m.co[:, e, :], m.co[:, e, :], 0.5, colv(L, "dwb", e), MULT, ADD)
                        ins.then_inc(ev["conv_done"], 1)
                        o = read(L, it)
                        y = xn[:, :, 2 * CW:3 * CW]
                        dve.tensor_copy(y, two(o)).then_inc(free(L, it), 1)
                        took(L, it)
                        for t in range(NT):
                            st = step(dve.bn_stats(m.bn[:, t, :], y[:, t, :]))
                        dve.wait_ge(dve_step, st)
                        for t in range(NT):
                            st = step(dve.bn_aggr(m.mv[:, t, :], m.bn[:, t, :]))
                        dve.wait_ge(dve_step, st)
                        dve.tensor_scalar(var[:, 6:8], m.mv[:, :, 1], EPS, None, ADD).then_inc(ev["ln_var"], 1)
                        dve.wait_ge(ev["ln_rstd"], nth(L, "ln_rstd"))
                        for t in range(NT):
                            st = step(dve.tensor_scalar(y[:, t, :], y[:, t, :], m.mv[:, t, 0:1], rstd[:, 6 + t:7 + t], SUB, MULT))
                        dve.wait_ge(dve_step, st)
                        link(dve.tensor_tensor(y, y, bcast(m.lngb[:, 0, :], 2), MULT))
                        dve.tensor_tensor(y, y, bcast(m.lngb[:, 1, :], 2), ADD).then_inc(ev["ln_done"], 1)
                sq += 1
                vk += 1
                dve.wait_ge(ssq_done, sq)
                variance(slice(0, 2), 2 * CW)
                variance(slice(2, 6), CW).then_inc(var_done, 1)
                dve.wait_ge(rstd_done, vk)
                for t in range(NT):
                    for s, (lo, hi) in enumerate(((0, 512), (512, 768), (768, 1024))):
                        ins = dve.tensor_scalar(xn[:, t, lo:hi], xn[:, t, lo:hi], rstd[:, 2 * s + t:2 * s + t + 1], None, MULT)
                    ins.then_inc(xn_done, 1)
                xT_low(L, "out")
                for j in range(rows_done, KT):
                    row_split()
                update_x(1.0, b - 1)

            def mixer2(L):
                nonlocal k, b, h
                m = m2
                if L == DEPTH:
                    dve.memset(m.uP[:, :, 0:PADP], 0.0)
                    dve.memset(m.uP[:, :, PADP + SEQ:], 0.0)
                    dve.memset(m.z[:, :, 0:1], 0.0)
                    link(dve.memset(m.z[:, :, SEQ + 1:], 0.0))
                norm(L, "mix")
                ia = gm = 0
                for it in order_mix2():
                    i = int(it[-1]) if it[-1].isdigit() else None
                    if it == "A":
                        name, j = PANELS2[ia]
                        panel({"F": m.uF[:, 2 * j:2 * j + 2, :], "P": m.uP[:, 2 * j:2 * j + 2, PADP:PADP + SEQ],
                               "C": m.c[:, :, :], "V": m.v[:, :, :], "B": m.gs[:, :, :]}[name])
                        ia += 1
                    elif it[0] == "Y":
                        panel(m.yc[:, 2 * i:2 * i + 2, :])
                    elif it == "pool":
                        dve.wait_ge(pair_summed, k + CREDIT)
                        if L == DEPTH:
                            dve.wait_ge(block2_in, 16 * N_BLOCK2)
                        w = SEQ + 2 * PADP
                        link(dve.tensor_tensor(m.d1[:, :, 0:w - 1], m.uP[:, :, 0:w - 1], m.uP[:, :, 1:w], ADD))
                        link(dve.tensor_tensor(m.d2[:, 1:4, 0:w - 3], m.d1[:, 1:4, 0:w - 3], m.d1[:, 1:4, 2:w - 1], ADD))
                        link(dve.tensor_tensor(m.d1[:, 2:4, 0:w - 7], m.d2[:, 2:4, 0:w - 7], m.d2[:, 2:4, 4:w - 3], ADD))
                        link(dve.tensor_tensor(m.d2[:, 3, 0:w - 15], m.d1[:, 3, 0:w - 15], m.d1[:, 3, 8:w - 7], ADD))
                        for g, d in enumerate((m.d1, m.d2, m.d1, m.d2)):
                            at = PADP - WINDOWS[g] // 2
                            link(dve.tensor_tensor(m.cvp[:, g, :], d[:, g, at:at + SEQ], m.count[:, g, :], MULT))
                        dve.tensor_tensor(m.d1[:, :, 0:SEQ], m.cvp[:, :, :], m.uP[:, :, PADP:PADP + SEQ], SUB).then_inc(ev["pooled"], 1)
                    elif it[0] == "z":
                        zz = m.z[:, 2 * i:2 * i + 2, :]
                        dve.wait_ge(pair_summed, k + CREDIT)
                        link(dve.tensor_tensor(zz[:, :, 1:SEQ + 1], m.c[:, :, :], m.v[:, :, :], MULT))
                        st = [step(dve.tensor_scalar(m.cv[:, e, :], zz[:, e, 0:SEQ], colv(L, "wc", 2 * i + e), None, MULT)) for e in range(2)]
                        for j in (1, 2):
                            for e in range(2):
                                dve.wait_ge(dve_step, st[e])
                                st[e] = step(dve.scalar_tensor_tensor(m.cv[:, e, :], zz[:, e, j:j + SEQ], colv(L, "wc", 4 * j + 2 * i + e),
                                                                      m.cv[:, e, :], MULT, ADD))
                        dve.wait_ge(dve_step, st[1])
                    elif it[:2] == "bc":
                        dve.wait_ge(pair_summed, k + CREDIT)
                        dve.tensor_tensor(m.gs[:, :, :], m.gs[:, :, :], m.cv[:, :, :], MULT).then_inc(ev["bc_f32"], 1)
                        dve.wait_ge(ev["bc_hi"], nth(L, "bc_hi", i))
                        dve.tensor_tensor(m.bc[:, 2 * i:2 * i + 2, 1, :], m.gs[:, :, :], m.bc[:, 2 * i:2 * i + 2, 0, :], SUB)\
                           .then_inc(ev["bc_split"], 1)
                    elif it == "G":
                        for g, y in enumerate((m.yf, m.yc, m.yp)):
                            yy = y[:, 2 * gm:2 * gm + 2, :]
                            panel(m.gs[:, :, :])
                            dve.wait_ge(ev["gate_done"], nth(L, "gate_done", 3 * gm + g))
                            if g == 0:
                                if gm == 0:
                                    for s in ("yf", "yp"):
                                        for q in range(4):
                                            took(L, f"{s}{q}")
                                link(dve.scalar_tensor_tensor(m.mg[:, :, :], m.th[:, :, :], 1.0, yy, ADD, MULT))
                            else:
                                link(dve.scalar_tensor_tensor(m.cv[:, :, :], m.th[:, :, :], 1.0, yy, ADD, MULT))
                                ins = dve.tensor_tensor(m.mg[:, :, :], m.mg[:, :, :], m.cv[:, :, :], ADD)
                                if g == 1:
                                    link(ins)
                                else:
                                    ins.then_inc(ev["merged"], 1)
                        for e in range(2):
                            row_split()
                        for e in range(2):
                            h_low(h, h % 2, m.mg[:, e, :])
                            h += 1
                        gm += 1
                update_x(0.5, b - 1)

            def final_norm(L):
                nonlocal sq, vk
                sq += 1
                vk += 1
                dve.wait_ge(ssq_done, sq)
                variance(slice(0, 2), DM).then_inc(var_done, 1)
                dve.wait_ge(rstd_done, vk)
                dve.wait_ge(gain_in, 16 * (L // DEPTH + 1))
                for t in range(NT):
                    dve.scalar_tensor_tensor(x[:, t, :], x[:, t, :], rstd[:, t:t + 1], xn[:, 1, :], MULT, MULT).then_inc(x_done, 1)

            dve.memset(ones[:, :], 1.0)
            dve.memset(second[:, 0, 0:1], 0.0).then_inc(a_split, CREDIT)
            dve.memset(second[:, 0, 1:2], 0.0).then_inc(b_split, CREDIT)
            dve.memset(second[:, 0, 2:3], 0.0).then_inc(pair_summed, CREDIT)
            dve.memset(m1.u[:, :, 0:PADC], 0.0)
            dve.memset(m1.u[:, :, PADC + SEQ:], 0.0)
            dve.memset(m1.hs[:, :, 0:1], 0.0)
            dve.memset(m1.hs[:, :, SEQ + 1:], 0.0)
            dve.memset(minus_half[:, :], -0.5).then_inc(half_set, 1)
            dve.wait_ge(rows_T, 1)
            for L in range(2 * DEPTH):
                r = ROWS1 if L < DEPTH else ROWS2
                ins = dve.tensor_copy(cols[:, L, 0:r], acc[:, 0, L * P:L * P + r])
            ins.then_inc(cols_done, 1)
            dve.wait_ge(cols_done, 1)
            dve.wait_ge(block1_in, 16 * N_BLOCK1)
            link(dve.tensor_copy(m1.posf, m1.pos[:, :]))
            link(dve.tensor_scalar(m1.posf, m1.posf, m1.invf[:, 0:1], None, MULT))
            for i, turn in enumerate((0.25, 0.0)):
                reduced(m1.posf, m1.fq96, m1.ra[:, i, :], turn).then_inc(ev["rope_arg"], 1)
                dve.wait_ge(ev["rope_arg"], i + 1)
            split_a(0, 0)
            for L in range(2 * DEPTH):
                ffn(L, "ffn1", False)
                if L < DEPTH:
                    mixer1(L)
                else:
                    mixer2(L)
                ffn(L, "ffn2", L == 2 * DEPTH - 1)
                if L % DEPTH == DEPTH - 1:
                    final_norm(L)


def kernel(**inputs):
    import concourse.bacc as bacc
    from concourse.bass_utils import run_bass_kernel_spmd

    nc = bacc.Bacc("TRN2", target_bir_lowering=False, num_devices=1)
    arrays = {n: np.ascontiguousarray(v) for n, v in inputs.items()}
    arrays.update(host_constants())
    feed = {f"in_{n}": v for n, v in arrays.items()}
    T = {n: nc.dram_tensor(f"in_{n}", v.shape, mybir.dt.from_np(v.dtype), kind="ExternalInput").ap() for n, v in arrays.items()}
    out = nc.dram_tensor("out_0", (1, SEQ, DM), mybir.dt.float32, kind="ExternalOutput").ap()
    build(nc, T, out)
    r = run_bass_kernel_spmd(nc, [feed], core_ids=[0])
    return r.results[0]["out_0"]
```

```python
import math

import numpy as np

import concourse.bass as bass
from concourse import mybir
from contextlib import ExitStack

P = 128
SEQ = 256
DM = 1024
FF = 2816
DEPTH = 2
EPS = 1e-6
NT = SEQ // P
KT = DM // P
FFU = FF // P
HALF = 512
A_COLS = 2 * KT * P
HEADS, NOPE, ROPE, VD = 8, 64, 32, 64
QKD = NOPE + ROPE
QR, KVR = 256, 128
CW = 256
CK = 31
PADC = CK // 2
FILT = 64
EMB = 33
NFFT = 2 * SEQ
IN1 = 1696
PANELS1 = [("ca", 416), ("cg", 672), ("q", 0), ("kv", 256), ("v", 928), ("x1", 1184), ("x2", 1440)]
GROUPS = 4
IN2 = 5 * 512 + 3 * DM
PANELS2 = ([("F", 0), ("F", 1), ("P", 0), ("P", 1), ("C", 0), ("V", 0), ("B", 0), ("C", 1), ("V", 1), ("B", 1)])
OFF2 = {"F": 0, "B": 512, "C": 1024, "V": 1536, "P": 2048, "G": 2560}
WINDOWS = (2, 4, 8, 16)
PADP = 8

COL1, COL2 = {}, {}
_n = 0
for _name, _k in (("ffn1", 8), ("mix", 8), ("q", 2), ("kv", 1), ("dww", 62), ("dwb", 2), ("hsw", 18), ("hsb", 6),
                  ("out", 8), ("ffn2", 8)):
    COL1[_name] = (_n, _k)
    _n += _k
ROWS1 = _n
_n = 0
for _name, _k in (("ffn1", 8), ("mix", 8), ("wc", 12), ("ps", 8), ("ffn2", 8)):
    COL2[_name] = (_n, _k)
    _n += _k
ROWS2 = _n

TWO_PI = 2.0 * math.pi
PI_A = 6.28125
PI_B = float(np.float32(np.round((TWO_PI - PI_A) * 2.0**21) / 2.0**21))
PI_C = float(TWO_PI - PI_A - PI_B)
ROUND = 12582912.0
PI_F = 3.1415925

CREDIT = 2


def order_mix1():
    o = ["A", "A", "glu", "f0", "A", "taps", "f1", "rope", "A", "taps", "qkv_sq", "f2", "stat", "taps", "A",
         "h0", "kb", "short0", "A", "n0", "spec0", "short1", "A", "h1", "short2", "n1",
         "spec1", "values", "fwd0", "taps", "q0", "k0", "kpe", "rot0", "inv0", "taps"]
    o += ["s0", "s1", "p0", "fwd1", "taps", "q1", "k1", "rot1", "s2", "o0", "p1", "s3", "o1", "p2", "inv1", "taps", "B",
          "q2", "k2", "rot2", "s4", "o2", "p3", "s5", "o3", "p4", "taps",
          "q3", "k3", "rot3", "s6", "o4", "p5", "s7", "o5", "p6", "taps", "o6", "p7", "taps", "o7",
          "conv_out", "y_norm"]
    return o


N_PARAM1 = 14
N_PARAM2 = 2
N_BLOCK1 = 5
N_BLOCK2 = 3
TAP_PARTS = order_mix1().count("taps")


def tap_range(part):
    return range(CK * part // TAP_PARTS, CK * (part + 1) // TAP_PARTS)


def small_steps1():
    s = []
    for it in order_mix1():
        if it in ("f0", "f1", "f2", "stat", "kb"):
            s.append(it)
        elif it in ("h0", "h1"):
            s += [f"{it}t{t}" for t in range(NT)]
        elif it == "values":
            s += ["val0", "val1"]
        elif it.startswith("n") or it.startswith("short"):
            s.append(it)
        elif it.startswith("spec"):
            s += ["A" + it[4:], "B" + it[4:]]
        elif it.startswith("fwd"):
            s += ["re" + it[3:], "im" + it[3:]]
        elif it.startswith("inv") or it.startswith("rot") or it == "conv_out":
            s.append(it)
        elif it == "kpe":
            s.append(it)
        elif it[0] in "qkspo" and it[1:].isdigit():
            s.append(it)
    return s


SMALL1 = small_steps1()
SMALL2 = ([f"c{g}" for g in range(GROUPS)] + ["t0", "t1"] + [f"yf{m}" for m in range(4)] + [f"yp{m}" for m in range(4)])


def order_mix2():
    return ["A", "A", "c0", "c1", "c2", "c3", "A", "A", "pool", "t0", "A", "A", "z0", "A", "bc0", "t1",
            "A", "A", "z1", "A", "bc1", "yf0", "yf1", "yf2", "yf3", "yp0", "yp1", "yp2", "yp3",
            "Y0", "Y1", "Y2", "Y3"] + ["G"] * 4


def norms_before(L):
    return 4 * min(L, DEPTH) + 3 * max(L - DEPTH, 0)


def squares_before(L):
    return 7 * min(L, DEPTH) + 6 * max(L - DEPTH, 0) + (2 if L > DEPTH else 0)


def host_constants():
    f64 = np.float64
    t = np.arange(SEQ, dtype=f64)
    f = np.arange(SEQ, dtype=f64)
    ang = 2 * np.pi * np.outer(t, f) / NFFT
    alt = np.where(np.arange(SEQ) % 2 == 0, 1.0, -1.0)
    cf = np.cos(ang)
    sf = -np.sin(ang)
    sf[:, 0] = alt
    w = np.full(SEQ, 2.0 / NFFT)
    w[0] = 1.0 / NFFT
    ci = w[:, None] * np.cos(ang.T)
    si = -w[:, None] * np.sin(ang.T)
    si[0, :] = alt / NFFT
    ps = 2 * np.pi * np.outer(t, t) / SEQ
    k = np.arange(P, dtype=f64)
    pc = 2 * np.pi * np.outer(k, k) / P
    norm = 1.0 / math.sqrt(SEQ * P)
    f32 = np.float32
    tt = np.linspace(0.0, 1.0, SEQ, dtype=f32)[:, None]
    bands = (EMB - 1) // 2
    a = (f32(2.0 * math.pi) * np.arange(SEQ, dtype=f32)[:, None] / f32(SEQ)).astype(f32)
    fb = np.linspace(1e-4, bands - 1, bands, dtype=f32)[None, :]
    z = np.concatenate([tt, np.cos(fb * a), -np.sin(fb * a)], axis=-1).astype(f32)
    max_decay = math.log(1e-2) / 0.3
    min_decay = math.log(1e-2) / 1.5
    deltas = np.linspace(min_decay, max_decay, CW, dtype=f32)
    decay = np.exp(-tt * np.abs(deltas)).astype(f32)
    rot = np.zeros((QKD, QKD))
    for i in range(ROPE // 2):
        rot[NOPE + 16 + i, NOPE + i] = -1.0
        rot[NOPE + i, NOPE + 16 + i] = 1.0
    invf = np.zeros((QKD, 1), f32)
    base = 1.0 / (f32(10000.0) ** (np.arange(0, ROPE, 2, dtype=f32) / f32(ROPE)))
    invf[NOPE:NOPE + 16, 0] = base
    invf[NOPE + 16:, 0] = base
    rc = np.zeros((P, GROUPS, SEQ))
    for g, win in enumerate(WINDOWS):
        cnt = np.minimum(t + win // 2, SEQ) - np.maximum(t - win // 2, 0)
        rc[:, g, :] = 1.0 / cnt
    out = {
        "k_dft": np.stack([cf, sf, ci, si]),
        "k_seq": np.stack([np.cos(ps) * norm, -np.sin(ps) * norm]),
        "k_chan": np.concatenate([np.cos(pc), np.sin(pc)], axis=1),
        "k_emb": np.ascontiguousarray(z.T),
        "k_decay": decay,
        "k_rot": rot,
        "k_invf": invf,
        "k_count": rc,
        "k_eye": np.eye(P),
    }
    return {n: np.ascontiguousarray(v, dtype=f32) for n, v in out.items()}


def build(nc: bass.Bass, T, out: bass.AP):
    F32 = mybir.dt.float32
    F32R = mybir.dt.float32r
    I32 = mybir.dt.int32
    ALU = mybir.AluOpType
    ACT = mybir.ActivationFunctionType
    AX = mybir.AxisListType.X
    MULT, ADD, SUB = ALU.mult, ALU.add, ALU.subtract

    ctx = ExitStack()
    with ctx:
        def sb(name, shape, dt=F32):
            return ctx.enter_context(nc.sbuf_tensor(name, shape, dt))

        def sem(name):
            return ctx.enter_context(nc.semaphore(name))

        acc = ctx.enter_context(nc.psum_tensor("acc", [P, 4, HALF], F32))
        pair = [ctx.enter_context(nc.psum_tensor(f"pair{i}", [P, 2, SEQ], F32)) for i in range(2)]
        rb_psum = ctx.enter_context(nc.psum_tensor("rb_psum", [P, SEQ], F32))
        cols_psum = ctx.enter_context(nc.psum_tensor("cols_psum", [P, 2 * DEPTH, P], F32))
        acc_halves = acc[:, :, :].rearrange("p (j t) n -> p j t n", j=2)

        raw_a = [sb(f"raw_a{i}", [P, A_COLS]) for i in range(2)]
        raw_b = [sb(f"raw_b{i}", [P, DM]) for i in range(2)]
        a_hi = [sb(f"a_hi{i}", [P, A_COLS], F32R) for i in range(2)]
        a_lo = [sb(f"a_lo{i}", [P, A_COLS], F32R) for i in range(2)]
        b_hi = [sb(f"b_hi{i}", [P, DM], F32R) for i in range(2)]
        b_lo = [sb(f"b_lo{i}", [P, DM], F32R) for i in range(2)]
        x = sb("x", [P, NT, DM])
        xT = sb("xT", [P, KT, 2, SEQ], F32R)
        hT = [sb(f"hT{i}", [P, 2, SEQ], F32R) for i in range(2)]
        junk = sb("junk", [P, 2 * SEQ])
        rb = sb("rb", [P, SEQ])
        diag = sb("diag", [P, NT, P])
        gu = sb("gu", [P, 2, SEQ])
        sh = sb("sh", [P, 2, SEQ])
        xn = sb("xn", [P, NT, DM])
        cols = sb("cols", [P, 2 * DEPTH, P])
        eye = sb("eye", [P, P])
        ones = sb("ones", [P, P])
        ssq = sb("ssq", [P, 8])
        var = sb("var", [P, 8])
        rstd = sb("rstd", [P, 8])
        minus_half = sb("minus_half", [P, 8])

        a_full = [sem(f"a_full{i}") for i in range(2)]
        b_full = [sem(f"b_full{i}") for i in range(2)]
        a_hi_ready = sem("a_hi_ready")
        a_split = sem("a_split")
        b_hi_ready = sem("b_hi_ready")
        b_split = sem("b_split")
        proj_done = sem("proj_done")
        pair_read = sem("pair_read")
        gate_scaled = sem("gate_scaled")
        silu_done = sem("silu_done")
        h_done = sem("h_done")
        h_hi_ready = sem("h_hi_ready")
        h_split = sem("h_split")
        down_done = sem("down_done")
        acc_bank = sem("acc_bank")
        x_done = sem("x_done")
        ssq_done = sem("ssq_done")
        var_done = sem("var_done")
        rstd_done = sem("rstd_done")
        diag_done = sem("diag_done")
        rb_in_psum = sem("rb_in_psum")
        rb_read = sem("rb_read")
        xn_done = sem("xn_done")
        xT_in_psum = sem("xT_in_psum")
        xT_hi = sem("xT_hi")
        xT_split = sem("xT_split")
        made = sem("made")
        taken = [sem(f"taken{i}") for i in range(4)]
        dve_step = sem("dve_step")
        act_step = sem("act_step")
        consts_in = sem("consts_in")
        rows_in = sem("rows_in")
        rows_T = sem("rows_T")
        cols_done = sem("cols_done")
        more_rows_in = sem("more_rows_in")
        params_in = [sem(f"params_in{i}") for i in range(2 * DEPTH)]
        gain_in = sem("gain_in")
        stored = sem("stored")
        half_set = sem("half_set")
        block1_in = sem("block1_in")
        block2_in = sem("block2_in")
        EVENTS1 = {"gate_tanh": 1, "filt_arg": 3, "filt_hidden": 3, "filt_taps": 2, "filt_abs": 2, "filt_sums": 2,
                   "qkv_squares": 1, "q_gained": 1, "qkv_rstd": 1, "kv_diag": 1, "short_mid": 3, "short_done": 3,
                   "spectrum": 2, "q_roped": 4, "kpe_roped": 1, "neg_max": HEADS, "conv_done": 1, "ln_var": 1,
                   "ln_rstd": 1, "ln_done": 1, "conv_silu": 1, "rope_arg": 2, "rope_done": 2}
        EVENTS2 = {"pooled": 1, "bc_f32": 2, "bc_hi": 2, "bc_split": 2, "gate_done": 12, "merged": 4}
        ev = {n: sem(n) for n in (*EVENTS1, *EVENTS2)}

        def nth(L, name, i=0):
            return (L % DEPTH) * (EVENTS1 if name in EVENTS1 else EVENTS2)[name] + i + 1

        def colv(L, name, i=0, parts=P):
            o = (COL1 if L < DEPTH else COL2)[name][0]
            return cols[0:parts, L, o + i:o + i + 1]

        small = {}
        for L in range(2 * DEPTH):
            base = L * len(SMALL1) if L < DEPTH else DEPTH * len(SMALL1) + (L - DEPTH) * len(SMALL2)
            for n, name in enumerate(SMALL1 if L < DEPTH else SMALL2):
                small[L, name] = base + n

        def bank(L, name):
            return acc[:, small[L, name] % 4, :]

        class Obj:
            pass

        def scope1(c):
            def s(name, shape, dt=F32):
                return c.enter_context(nc.sbuf_tensor(name, shape, dt))
            m = Obj()
            m.dft = s("dft", [P, 4, NT, SEQ])
            m.decay = s("decay", [P, NT, CW])
            m.cs = s("cossin", [QKD, 2, SEQ])
            m.rotm = s("rotm", [QKD, QKD])
            m.invf = s("invf", [QKD, 1])
            m.lngb = s("lngb", [P, 2, CW])
            m.wqb = s("wqb", [P, 2, HEADS * QKD])
            m.wkvb = s("wkvb", [P, HEADS * (NOPE + VD)])
            early = s("early", [P, 6088])
            m.w4 = early[0:FILT, 0:1024]
            m.emb = early[0:EMB, 1024:1280]
            m.w1 = early[0:EMB, 1280:1344]
            m.w2 = early[0:FILT, 1344:1408]
            m.w3 = early[0:FILT, 1408:1472]
            m.fcol = early[0:FILT, 1472:1476]
            m.dB = early[:, 1480:1992].rearrange("p (o c) -> p o c", o=2)
            m.farg = early[0:FILT, 1992:2248]
            m.fq = early[0:FILT, 2248:2504]
            m.hdn = early[0:FILT, 2504:2760]
            m.kt = early[:, 2760:3784].rearrange("p (t d c) -> p t d c", t=NT, d=2)
            m.ab = early[:, 3784:4808].rearrange("p (t d c) -> p t d c", t=NT, d=2)
            m.ks = early[:, 4808:5320].rearrange("p (t c) -> p t c", t=NT)
            m.kd = early[:, 5320:5832].rearrange("p (t c) -> p t c", t=NT)
            m.rn = early[:, 5832:6088]
            m.V = early[:, 4808:5832].rearrange("p (t c) -> p t c", t=NT)
            m.qraw = early[0:QKD, 0:512]
            m.qc = early[0:QKD, 1024:1536]
            m.qp = [early[0:QKD, 512:1024], early[0:QKD, 1992:2504]]
            m.kT = [early[0:QKD, 2760:3272], early[0:QKD, 3272:3784]]
            m.PT = [early[:, 3784:4296], early[:, 4296:4808]]
            m.kpe = early[0:QKD, 2504:2760]
            m.kpe2 = early[0:QKD, 5832:6088]
            m.pos = s("pos", [QKD, SEQ], I32)
            m.posf = early[0:QKD, 2760:3016]
            m.fq96 = early[0:QKD, 3016:3272]
            m.ra = early[0:QKD, 3272:3784].rearrange("p (a c) -> p a c", a=2)
            m.Pm = [gu, sh]
            m.KA = [s(f"KA{o}", [P, 2, CW]) for o in range(2)]
            m.KB = [s(f"KB{o}", [P, 2, CW]) for o in range(2)]
            m.KN = s("KN", [1, 2, CW])
            m.ca = s("ca", [P, 2, SEQ])
            m.cg = s("cg", [P, 2, SEQ])
            m.u = s("u", [P, 2, SEQ + 2 * PADC])
            m.co = s("co", [P, 2, SEQ])
            m.hq = s("hq", [P, 2, SEQ])
            m.qn = m.hq
            m.hk = s("hk", [P, 2, SEQ])
            m.kvn = s("kvn", [P, SEQ])
            m.hs = s("hs", [P, 2, SEQ + 2])
            m.sc = s("sc", [P, 2, SEQ])
            m.tv = [s(f"tv{j}", [P, NT, CW]) for j in range(3)]
            m.tmp = m.cg
            m.Yr = m.ca
            m.Yi = s("Yi", [P, 2, CW])
            m.mx = s("mx", [P, 2 * HEADS])
            m.sm = s("sm", [P, 2 * HEADS])
            m.rs = s("rs", [P, 2 * HEADS])
            m.qs = s("qs", [P, 4])
            m.bn = s("bn", [P, NT, 6])
            m.mv = s("mv", [P, NT, 2])
            return m

        def scope2(c):
            def s(name, shape, dt=F32):
                return c.enter_context(nc.sbuf_tensor(name, shape, dt))
            m = Obj()
            m.seq = s("seq", [P, 2, NT, SEQ])
            m.chan = s("chan", [P, 2 * P])
            m.count = s("count", [P, GROUPS, SEQ])
            m.wf = s("wf", [P, GROUPS, SEQ])
            m.wp = s("wp", [P, GROUPS, SEQ])
            m.uF = s("uF", [P, GROUPS, SEQ])
            m.ab = s("ab2", [P, NT, GROUPS, 2 * P])
            m.fT = s("fT", [P, GROUPS, SEQ])
            m.uP = s("uP", [P, GROUPS, SEQ + 2 * PADP])
            m.d1 = s("d1", [P, GROUPS, SEQ + 2 * PADP])
            m.d2 = s("d2", [P, GROUPS, SEQ + 2 * PADP])
            m.c = s("c2", [P, 2, SEQ])
            m.v = s("v2", [P, 2, SEQ])
            m.z = s("z2", [P, GROUPS, SEQ + 2])
            m.cv = s("cv2", [P, 2, SEQ])
            m.bc = s("bc2", [P, GROUPS, 2, SEQ], F32R)
            m.yf = s("yf", [P, KT, SEQ])
            m.yc = m.ab[:, :, :, :].rearrange("p t g c -> p (t g) c")
            m.yp = s("yp", [P, KT, SEQ])
            m.gs = s("gs", [P, 2, SEQ])
            m.th = s("th", [P, 2, SEQ])
            m.cvp = m.yf[:, 0:GROUPS, :]
            m.mg = s("mg", [P, 2, SEQ])
            return m

        c1 = ExitStack()
        with c1:
            m1 = scope1(c1)
        c2 = ExitStack()
        with c2:
            m2 = scope2(c2)

        def ffn_weights(L, which):
            l = L % DEPTH
            if L < DEPTH:
                n = "ffn1" if which == 0 else "ffn2"
                return T[n + "_w_gate"][l], T[n + "_w_up"][l], T[n + "_w_down"][l]
            s = "a" if which == 0 else "b"
            return T[f"w1_{s}_2"][l], T[f"w3_{s}_2"][l], T[f"w2_{s}_2"][l]

        block = ctx.enter_context(nc.Block())

        def a_flat(tile, nt=KT):
            return tile[:, 0:nt * 2 * P].rearrange("p (t n) -> p t n", t=nt)

        def a_gate_up(tile):
            return tile[:, :].rearrange("p (g t n) -> p g t n", g=2, t=KT)

        def two(ap):
            return ap.rearrange("p (t c) -> p t c", t=2)

        @block.sync
        def _(sp):
            k = 0
            b = 0

            def rows(w):
                return w.rearrange("(t p) n -> p t n", p=P)

            def gate_up_unit(wg, wu, at, u, wait):
                sp.wait_ge(a_split, wait)
                dst = a_gate_up(raw_a[u])
                sp.dma_start(dst[:, 0], rows(wg)[:, :, at]).then_inc(a_full[u], 16)
                sp.dma_start(dst[:, 1], rows(wu)[:, :, at]).then_inc(a_full[u], 16)

            def down_unit(wd, at, v, wait):
                sp.wait_ge(b_split, wait)
                sp.dma_start(raw_b[v][:, :], wd[at, :]).then_inc(b_full[v], 16)

            def first_gate_up(L, which, u):
                nonlocal k
                wg, wu, _ = ffn_weights(L, which)
                gate_up_unit(wg, wu, slice(u * P, (u + 1) * P), k % 2, k + 1)
                k += 1

            def first_down(L, which):
                nonlocal b
                down_unit(ffn_weights(L, which)[2], slice(0, P), b % 2, b + 1)
                b += 1

            def ffn(L, which):
                nonlocal k, b
                wg, wu, wd = ffn_weights(L, which)
                with sp.Fori(0, FFU // 2 - 1) as i:
                    for e in range(2):
                        gate_up_unit(wg, wu, bass.ds(i * (2 * P) + (e + 2) * P, P), (k + e) % 2, i * 2 + (k + e + 1))
                        down_unit(wd, bass.ds(i * (2 * P) + (e + 1) * P, P), (b + e) % 2, i * 2 + (b + e + 1))
                k += FFU - 2
                b += FFU - 2

            def last_down(L, which):
                nonlocal b
                down_unit(ffn_weights(L, which)[2], slice((FFU - 1) * P, FFU * P), b % 2, b + 1)
                b += 1

            def panel(w, start, nt=KT):
                nonlocal k
                sp.wait_ge(a_split, k + 1)
                sp.dma_start(a_flat(raw_a[k % 2], nt), rows(w)[:, :, start:start + 2 * P])\
                  .then_inc(a_full[k % 2], 32)
                k += 1

            def row_unit(w, j):
                nonlocal b
                sp.wait_ge(b_split, b + 1)
                sp.dma_start(raw_b[b % 2][:, :], w[j * P:(j + 1) * P, :]).then_inc(b_full[b % 2], 16)
                b += 1

            for t in range(NT):
                sp.dma_start(x[:, t, :], T["x"][0, t * P:(t + 1) * P, :]).then_inc(consts_in, 16)
            sp.dma_start(eye[:, :], T["k_eye"]).then_inc(consts_in, 16)
            first_gate_up(0, 0, 0)
            first_gate_up(0, 0, 1)
            first_down(0, 0)
            for L in range(2 * DEPTH):
                l = L % DEPTH
                ffn(L, 0)
                if L < DEPTH:
                    panel(T["w_in"][l], PANELS1[0][1])
                    last_down(L, 0)
                    panel(T["w_in"][l], PANELS1[1][1])
                    row_unit(T["w_out"][l], 0)
                    for _, start in PANELS1[2:]:
                        panel(T["w_in"][l], start)
                    first_gate_up(L, 1, 0)
                    first_gate_up(L, 1, 1)
                    for j in range(1, KT):
                        row_unit(T["w_out"][l], j)
                    first_down(L, 1)
                else:
                    w = T["w_in_2"][l]
                    starts = [OFF2[name] + j * 2 * P for name, j in PANELS2]
                    gates = [OFF2["G"] + g * DM + m * 2 * P for m in range(4) for g in range(3)]
                    panel(w, starts[0])
                    last_down(L, 0)
                    panel(w, starts[1])
                    row_unit(T["w_o_2"][l], 0)
                    for start in starts[2:]:
                        panel(w, start)
                    for j in range(4):
                        panel(T["w_conv_out_2"][l], j * 2 * P, nt=4)
                    panel(w, gates[0])
                    panel(w, gates[1])
                    for m in range(4):
                        for g in range(3):
                            n = 3 * m + g + 2
                            if n < len(gates):
                                panel(w, gates[n])
                            else:
                                first_gate_up(L, 1, n - len(gates))
                            if g == 1 and m:
                                row_unit(T["w_o_2"][l], 2 * m)
                        row_unit(T["w_o_2"][l], 2 * m + 1)
                    first_down(L, 1)
                ffn(L, 1)
                if L < 2 * DEPTH - 1:
                    first_gate_up(L + 1, 0, 0)
                last_down(L, 1)
                if L < 2 * DEPTH - 1:
                    first_gate_up(L + 1, 0, 1)
                    first_down(L + 1, 0)
                if l == DEPTH - 1:
                    g = T["final_norm"] if L < DEPTH else T["g_final_2"]
                    sp.wait_ge(ssq_done, squares_before(L + 1))
                    sp.dma_start(xn[:, 1, :], g.rearrange("(o n) -> o n", o=1).broadcast_to([P, DM])).then_inc(gain_in, 16)
            for t in range(NT):
                sp.wait_ge(x_done, 4 * (3 * 2 * DEPTH + 1) + 2 * t + 2)
                sp.dma_start(out[0, t * P:(t + 1) * P, :], x[:, t, :]).then_inc(stored, 16)
            sp.wait_ge(stored, 16 * NT)

        @block.gpsimd
        def _(pool):
            nparam = 0

            m = m1
            n_const = 0

            def const(dst, src):
                nonlocal n_const
                pool.dma_start(dst, src).then_inc(block1_in, 16)
                n_const += 1
            const(m.dft[:, :, :, :].rearrange("p a t n -> p (a t) n"), T["k_dft"].rearrange("a (t p) n -> p (a t) n", p=P))
            const(m.decay[:, :, :], T["k_decay"].rearrange("(t p) n -> p t n", p=P))
            const(m.rotm[:, :], T["k_rot"])
            const(m.invf[:, :], T["k_invf"])
            const(m.pos[:, :], T["positions"].broadcast_to([QKD, SEQ]))
            assert n_const == N_BLOCK1

            def powers(cols_, waits):
                pool.wait_ge(*waits)
                return pool.tensor_tensor(rstd[:, cols_], var[:, cols_], minus_half[:, cols_], ALU.pow)

            def load1(L):
                l = L % DEPTH
                if l:
                    pool.wait_ge(xT_split, KT * (norms_before(L - 1) + 3))
                s = params_in[L]
                pool.dma_start(m.wqb[:, :, :], T["mla_w_qb"][l].rearrange("(t p) n -> p t n", p=P)).then_inc(s, 16)
                pool.dma_start(m.wkvb[:, :], T["mla_w_kvb"][l]).then_inc(s, 16)
                pool.dma_start(m.w4, T["hy_filt_w4"][l]).then_inc(s, 16)
                pool.dma_start(m.emb, T["k_emb"]).then_inc(s, 16)
                pool.dma_start(m.w1, T["hy_filt_w1"][l]).then_inc(s, 16)
                pool.dma_start(m.w2, T["hy_filt_w2"][l]).then_inc(s, 16)
                pool.dma_start(m.w3, T["hy_filt_w3"][l]).then_inc(s, 16)
                for i, n in enumerate(("hy_filt_b1", "hy_filt_b2", "hy_filt_b3", "hy_filt_freq")):
                    pool.dma_start(m.fcol[:, i:i + 1], T[n][l].rearrange("(p o) -> p o", o=1)).then_inc(s, 16)
                pool.dma_start(m.dB, T["hy_bias_d"][l].rearrange("(q o) c -> q o c", q=1).broadcast_to([P, 2, CW])).then_inc(s, 16)
                for i, n in enumerate(("conv_ln_g", "conv_ln_b")):
                    pool.dma_start(m.lngb[:, i, :], T[n][l].rearrange("(o c) -> o c", o=1).broadcast_to([P, CW])).then_inc(s, 16)

            def load2(L):
                l = L % DEPTH
                m = m2
                s = params_in[L]
                if l:
                    pool.wait_ge(xT_split, KT * (norms_before(L - 1) + 3))
                else:
                    pool.wait_ge(xT_split, KT * (norms_before(L - 1) + 3))
                    pool.dma_start(m.seq[:, :, :, :].rearrange("p a t n -> p (a t) n"),
                                   T["k_seq"].rearrange("a (t p) n -> p (a t) n", p=P)).then_inc(block2_in, 16)
                    pool.dma_start(m.chan[:, :], T["k_chan"]).then_inc(block2_in, 16)
                    pool.dma_start(m.count[:, :, :], T["k_count"]).then_inc(block2_in, 16)
                pool.dma_start(m.wf[:, :, :], T["w_fourier_2"][l].rearrange("g p n -> p g n")).then_inc(s, 16)
                pool.dma_start(m.wp[:, :, :], T["w_pool_2"][l].rearrange("g p n -> p g n")).then_inc(s, 16)

            vk = 0

            def norm():
                nonlocal vk
                vk += 1
                powers(slice(0, 2), (var_done, vk)).then_inc(rstd_done, 1)

            pool.wait_ge(half_set, 1)
            for L in range(2 * DEPTH):
                if L < DEPTH:
                    load1(L)
                    norm()
                    norm()
                    pool.wait_ge(taken[small[L, "stat"] % 4], small[L, "stat"] // 4 + 1)
                    pool.tensor_tensor(rstd[:, 0:4], var[:, 0:4], minus_half[:, 0:4], ALU.pow).then_inc(ev["qkv_rstd"], 1)
                    pool.wait_ge(ev["ln_var"], nth(L, "ln_var"))
                    pool.tensor_tensor(rstd[:, 6:8], var[:, 6:8], minus_half[:, 6:8], ALU.pow).then_inc(ev["ln_rstd"], 1)
                    vk += 1
                    powers(slice(0, 6), (var_done, vk)).then_inc(rstd_done, 1)
                else:
                    load2(L)
                    norm()
                    norm()
                norm()
                if L % DEPTH == DEPTH - 1:
                    norm()

        @block.tensor
        def _(pe):
            k = b = h = 0
            n = 0
            done = {}

            pe.wait_ge(half_set, 1)
            pe.matmul(pair[0][0:1, 0, 0:4], ones[:, 0:1], ones[:, 0:4], start=True, stop=True).then_inc(proj_done, CREDIT)
            pe.matmul(pair[1][0:1, 0, 0:4], ones[:, 0:1], ones[:, 0:4], start=True, stop=True).then_inc(down_done, CREDIT)
            u = 0
            yn = 0
            nr = 0

            def columns(layers):
                for L in layers:
                    r = ROWS1 if L < DEPTH else ROWS2
                    mm = pe.transpose(cols_psum[:, L, 0:r], xn[0:r, L // 2, (L % 2) * P:(L % 2 + 1) * P], eye[0:r, 0:r])
                mm.then_inc(rows_T, 1)

            def transposes(t, src, ready):
                for j in range(2):
                    ready(t, j)
                    for i in range(4):
                        kt = 4 * j + i
                        mm = pe.transpose(acc[:, 2 * j + t, i * P:(i + 1) * P], src[:, t, kt * P:(kt + 1) * P], eye[:, :])
                    mm.then_inc(xT_in_psum, 1)

            def x_updated(t, j):
                if u:
                    pe.wait_ge(x_done, 4 * (u - 1) + 2 * t + j + 1)

            def y_scaled(t, j):
                pe.wait_ge(xn_done, yn * NT + t + 1)

            def spread():
                nonlocal nr
                nr += 1
                pe.wait_ge(diag_done, nr)
                for t in range(NT):
                    mm = pe.matmul(rb_psum[:, t * P:(t + 1) * P], ones[:, :], diag[:, t, :], start=True, stop=True)
                mm.then_inc(rb_in_psum, 1)

            def project(k, par, blocks, src, nt, first):
                pe.wait_ge(a_hi_ready, k + 1)
                pe.wait_ge(a_split, k + 1 + CREDIT)
                pe.wait_ge(pair_read, k + 1)
                for e in range(2):
                    for kt in range(nt):
                        if first and e == 0:
                            pe.wait_ge(xT_split, KT * (n - 1) + kt + 1)
                        hi, lo = blocks(a_hi[par], e, kt), blocks(a_lo[par], e, kt)
                        pe.matmul(pair[par][:, e, :], hi, src[:, kt, 0, :], start=(kt == 0), stop=False)
                        pe.matmul(pair[par][:, e, :], hi, src[:, kt, 1, :], start=False, stop=False)
                        mm = pe.matmul(pair[par][:, e, :], lo, src[:, kt, 0, :], start=False, stop=(kt == nt - 1))
                mm.then_inc(proj_done, 1)

            def gate_up(tile, e, kt):
                return a_gate_up(tile)[:, e, kt, :]

            def panel_block(tile, e, kt):
                return a_flat(tile)[:, kt, e * P:(e + 1) * P]

            def kv_block(tile, e, kt):
                return a_flat(tile)[:, kt, e * NOPE:e * NOPE + P]

            def conv_block(tile, e, kt):
                return a_flat(tile, 4)[:, kt, e * P:(e + 1) * P]

            def down(b, par, parts, first):
                pe.wait_ge(b_hi_ready, b + 1)
                pe.wait_ge(b_split, b + 1 + CREDIT)
                for t in range(NT):
                    hi, lo = parts(t)
                    for j in range(2):
                        pe.matmul(acc[:, 2 * j + t, :], hi, b_hi[par][:, j * HALF:(j + 1) * HALF], start=first, stop=False)
                    for j in range(2):
                        pe.matmul(acc[:, 2 * j + t, :], hi, b_lo[par][:, j * HALF:(j + 1) * HALF], start=False, stop=False)
                    for j in range(2):
                        mm = pe.matmul(acc[:, 2 * j + t, :], lo, b_hi[par][:, j * HALF:(j + 1) * HALF], start=False, stop=False)
                mm.then_inc(down_done, 1)

            def last_down(b, par, parts, to_transpose=True):
                nonlocal u
                pe.wait_ge(b_hi_ready, b + 1)
                pe.wait_ge(b_split, b + 1 + CREDIT)
                u += 1
                for t in range(NT):
                    hi, lo = parts(t)
                    for j in range(2):
                        at = slice(j * HALF, (j + 1) * HALF)
                        if to_transpose and (t, j) == (NT - 1, 1):
                            transposes(0, x, x_updated)
                        pe.matmul(acc[:, 2 * j + t, :], hi, b_hi[par][:, at], start=False, stop=False)
                        pe.matmul(acc[:, 2 * j + t, :], hi, b_lo[par][:, at], start=False, stop=False)
                        mm = pe.matmul(acc[:, 2 * j + t, :], lo, b_hi[par][:, at], start=False, stop=True)
                        mm.then_inc(down_done if (t, j) == (NT - 1, 1) else acc_bank, 1)

            def from_h(h, par):
                pe.wait_ge(h_hi_ready, h + 1)
                pe.wait_ge(h_split, h + 1)
                return lambda t: (hT[par][:, 0, t * P:(t + 1) * P], hT[par][:, 1, t * P:(t + 1) * P])

            def ffn(to_transpose=True):
                nonlocal k, b, h, n
                n += 1
                transposes(1, x, x_updated)
                project(k, k % 2, gate_up, xT, KT, True)
                spread()
                project(k + 1, (k + 1) % 2, gate_up, xT, KT, False)
                down(b, b % 2, from_h(h, h % 2), True)
                with pe.Fori(0, FFU // 2 - 1) as i:
                    for e in range(2):
                        project(i * 2 + (k + 2 + e), (k + e) % 2, gate_up, xT, KT, False)
                        down(i * 2 + (b + 1 + e), (b + 1 + e) % 2, from_h(i * 2 + (h + 1 + e), (h + 1 + e) % 2), False)
                last_down(b + FFU - 1, (b + FFU - 1) % 2, from_h(h + FFU - 1, (h + FFU - 1) % 2), to_transpose)
                k += FFU
                b += FFU
                h += FFU

            def take(L, name):
                s = small[L, name]
                if s >= 4:
                    pe.wait_ge(taken[s % 4], s // 4)
                return acc[:, s % 4, :]

            def got(L, name):
                s = small[L, name]
                pe.wait_ge(taken[s % 4], s // 4 + 1)

            def mixer1(L):
                nonlocal k, b, n, yn
                m = m1
                cf, sf, ci, si = (m.dft[:, i] for i in range(4))
                n += 1
                transposes(1, x, x_updated)
                pk = {}
                ip = 0
                for it in order_mix1():
                    i = int(it[-1]) if it[-1].isdigit() else None
                    kind = it.rstrip("0123456789")
                    if it == "A":
                        project(k, k % 2, kv_block if PANELS1[ip][0] == "kv" else panel_block, xT, KT, ip == 0)
                        ip += 1
                        if ip == 1:
                            spread()
                            pe.wait_ge(params_in[L], 16 * N_PARAM1)
                            if L == 0:
                                pe.wait_ge(block1_in, 16 * N_BLOCK1)
                        k += 1
                    elif kind == "f":
                        o = take(L, it)
                        if i == 0:
                            pe.matmul(o[0:FILT, 0:SEQ], m.w1, m.emb, start=True, stop=True).then_inc(made, 1)
                        else:
                            pe.wait_ge(ev["filt_hidden"], nth(L, "filt_hidden", i - 1))
                            pe.matmul(o[0:FILT, 0:SEQ], (m.w2, m.w3)[i - 1], m.hdn, start=True, stop=True).then_inc(made, 1)
                    elif it == "stat":
                        o = take(L, it)
                        pe.wait_ge(ev["qkv_squares"], nth(L, "qkv_squares"))
                        for t in range(NT):
                            for e in range(2):
                                pe.matmul(o[:, t:t + 1], gu[:, e, t * P:(t + 1) * P], ones[:, 0:1], start=(e == 0), stop=(e == 1))
                        for t in range(NT):
                            mm = pe.matmul(o[:, NT + t:NT + t + 1], sh[:, 0, t * P:(t + 1) * P], ones[:, 0:1], start=True, stop=True)
                        mm.then_inc(made, 1)
                    elif kind == "h":
                        pe.wait_ge(ev["filt_hidden"], nth(L, "filt_hidden", 2))
                        for t in range(NT):
                            o = take(L, f"{it}t{t}")
                            pe.matmul(o, m.hdn[:, t * P:(t + 1) * P], m.w4[:, i * 2 * CW:(i + 1) * 2 * CW],
                                      start=True, stop=True).then_inc(made, 1)
                    elif it == "kb":
                        o = take(L, it)
                        pe.wait_ge(ev["kv_diag"], nth(L, "kv_diag"))
                        for t in range(NT):
                            mm = pe.matmul(o[:, t * P:(t + 1) * P], ones[:, :], m.kvn[:, t * P:(t + 1) * P], start=True, stop=True)
                        mm.then_inc(made, 1)
                    elif it == "values":
                        got(L, "kb")
                        wv = m.wkvb[:, :].rearrange("p (h c) -> p h c", h=HEADS)[:, :, NOPE:NOPE + VD]
                        for t in range(NT):
                            o = take(L, f"val{t}")
                            pe.matmul(o.rearrange("p (h c) -> p h c", h=HEADS), m.kvn[:, t * P:(t + 1) * P], wv,
                                      start=True, stop=True).then_inc(made, 1)
                    elif kind == "short":
                        o = take(L, it)
                        pe.wait_ge(ev["short_done"], nth(L, "short_done", i))
                        for t in range(NT):
                            for e in range(2):
                                mm = pe.transpose(o[:, t * CW + e * P:t * CW + (e + 1) * P], m.sc[:, e, t * P:(t + 1) * P], eye[:, :])
                        mm.then_inc(made, 1)
                    elif kind == "n":
                        o = take(L, it)
                        pe.wait_ge(ev["filt_abs"], nth(L, "filt_abs", i))
                        pe.wait_ge(ev["filt_sums"], nth(L, "filt_sums", i))
                        for j in range(4):
                            pe.matmul(o[:, 0:CW], ones[:, :], m.ab[:, j // 2, j % 2, :], start=(j == 0), stop=(j == 3))
                        for t in range(NT):
                            mm = pe.matmul(o[0:1, CW:2 * CW], sf[:, t, 0:1], m.ks[:, t, :], start=(t == 0), stop=(t == NT - 1))
                        mm.then_inc(made, 1)
                    elif kind == "spec" or kind == "fwd":
                        if kind == "spec":
                            srcs = [("A", cf, m.ks), ("B", sf, m.kd)]
                        else:
                            got(L, "short0" if i == 0 else "inv0")
                            srcs = [("re", cf, m.tv[0]), ("im", sf, m.tv[0])]
                        for nm, mat, src in srcs:
                            o = take(L, f"{nm}{i}")
                            for ft in range(2):
                                for t in range(NT):
                                    mm = pe.matmul(o[:, ft * CW:(ft + 1) * CW], mat[:, t, ft * P:(ft + 1) * P], src[:, t, :],
                                                   start=(t == 0), stop=(t == NT - 1))
                            mm.then_inc(made, 1)
                    elif kind == "inv":
                        o = take(L, it)
                        pe.wait_ge(ev["spectrum"], nth(L, "spectrum", i))
                        for t in range(NT):
                            for ft in range(2):
                                pe.matmul(o[:, t * CW:(t + 1) * CW], ci[:, ft, t * P:(t + 1) * P], m.Yr[:, ft, :],
                                          start=(ft == 0), stop=False)
                                mm = pe.matmul(o[:, t * CW:(t + 1) * CW], si[:, ft, t * P:(t + 1) * P], m.Yi[:, ft, :],
                                               start=False, stop=(ft == 1))
                        mm.then_inc(made, 1)
                    elif kind == "q":
                        o = take(L, it)
                        pe.wait_ge(ev["q_gained"], nth(L, "q_gained"))
                        for e in range(2):
                            c = (2 * i + e) * QKD
                            for j in range(2):
                                mm = pe.matmul(o[0:QKD, e * SEQ:(e + 1) * SEQ], m.wqb[:, j, c:c + QKD], m.qn[:, j, :],
                                               start=(j == 0), stop=(j == 1))
                        mm.then_inc(made, 1)
                    elif kind == "rot":
                        o = take(L, it)
                        got(L, f"q{i}")
                        pe.matmul(o[0:QKD, :], m.rotm[:, :], m.qraw, start=True, stop=True).then_inc(made, 1)
                    elif it == "kpe":
                        o = take(L, it)
                        pe.matmul(o[0:QKD, 0:SEQ], m.rotm[NOPE:QKD, :], m.hk[NOPE:QKD, 1, :], start=True, stop=True).then_inc(made, 1)
                    elif kind == "k":
                        o = take(L, it)
                        got(L, "kb")
                        for e in range(2):
                            c = (2 * i + e) * (NOPE + VD)
                            mm = pe.matmul(o[0:NOPE, e * SEQ:(e + 1) * SEQ], m.wkvb[:, c:c + NOPE], m.kvn[:, :], start=True, stop=True)
                        mm.then_inc(made, 1)
                    elif kind == "s":
                        o = take(L, it)
                        p2, e = i // 2, i % 2
                        pe.wait_ge(ev["q_roped"], nth(L, "q_roped", p2))
                        pe.wait_ge(ev["kpe_roped"], nth(L, "kpe_roped"))
                        got(L, f"k{p2}")
                        for t in range(NT):
                            mm = pe.matmul(o[:, t * SEQ:(t + 1) * SEQ], m.qp[p2 % 2][:, e * SEQ + t * P:e * SEQ + (t + 1) * P],
                                           m.kT[p2 % 2][:, e * SEQ:(e + 1) * SEQ], start=True, stop=True)
                        mm.then_inc(made, 1)
                    elif kind == "p":
                        o = take(L, it)
                        got(L, f"s{i}")
                        for t in range(NT):
                            for kk in range(NT):
                                mm = pe.transpose(o[:, kk * SEQ + t * P:kk * SEQ + (t + 1) * P],
                                                  m.Pm[i % 2][:, t, kk * P:(kk + 1) * P], eye[:, :])
                        mm.then_inc(made, 1)
                    elif kind == "o":
                        o = take(L, it)
                        got(L, f"p{i}")
                        got(L, "val1")
                        for t in range(NT):
                            for kk in range(NT):
                                mm = pe.matmul(o[:, t * VD:(t + 1) * VD], m.PT[i % 2][:, kk * SEQ + t * P:kk * SEQ + (t + 1) * P],
                                               m.V[:, kk, i * VD:(i + 1) * VD], start=(kk == 0), stop=(kk == NT - 1))
                        mm.then_inc(made, 1)
                    elif it == "conv_out":
                        o = take(L, it)
                        pe.wait_ge(ev["conv_done"], nth(L, "conv_done"))
                        for t in range(NT):
                            for e in range(2):
                                mm = pe.transpose(o[:, t * CW + e * P:t * CW + (e + 1) * P], m.co[:, e, t * P:(t + 1) * P], eye[:, :])
                        mm.then_inc(made, 1)
                n += 1
                for t in range(NT):
                    transposes(t, xn, y_scaled)
                yn += 1
                pe.wait_ge(xT_split, KT * n)
                for j in range(KT):
                    y_parts = lambda t, j=j: (xT[:, j, 0, t * P:(t + 1) * P], xT[:, j, 1, t * P:(t + 1) * P])
                    if j < KT - 1:
                        down(b, b % 2, y_parts, j == 0)
                    else:
                        last_down(b, b % 2, y_parts)
                    b += 1

            def mixer2(L):
                nonlocal k, b, h, n
                m = m2
                n += 1
                transposes(1, x, x_updated)
                first_k = k
                ia = gm = 0
                for it in order_mix2():
                    i = int(it[-1]) if it[-1].isdigit() else None
                    if it == "A":
                        project(k, k % 2, panel_block, xT, KT, ia == 0)
                        ia += 1
                        k += 1
                        if ia == 1:
                            spread()
                            pe.wait_ge(params_in[L], 16 * N_PARAM2)
                            pe.wait_ge(block2_in, 16 * N_BLOCK2)
                    elif it[0] == "c":
                        o = take(L, it)
                        pe.wait_ge(pair_read, first_k + i // 2 + 1 + CREDIT)
                        for t in range(NT):
                            mm = pe.matmul(o[:, t * SEQ:(t + 1) * SEQ], m.uF[:, i, t * P:(t + 1) * P], m.chan[:, :], start=True, stop=True)
                        mm.then_inc(made, 1)
                    elif it[0] == "t":
                        o = take(L, it)
                        got(L, f"c{2 * i + 1}")
                        got(L, f"c{2 * i}")
                        for e in range(2):
                            g = 2 * i + e
                            for t in range(NT):
                                for a in range(2):
                                    mm = pe.matmul(o[:, e * SEQ:(e + 1) * SEQ], m.ab[:, t, g, a * P:(a + 1) * P], m.seq[:, a, t, :],
                                                   start=(t == 0 and a == 0), stop=(t == NT - 1 and a == 1))
                        mm.then_inc(made, 1)
                    elif it[:2] in ("yf", "yp"):
                        o = take(L, it)
                        if it[1] == "f":
                            got(L, f"t{i // 2}")
                            w, src = m.wf, m.fT[:, i, :]
                        else:
                            pe.wait_ge(ev["pooled"], nth(L, "pooled"))
                            w, src = m.wp, m.d1[:, i, 0:SEQ]
                        for e in range(2):
                            mm = pe.matmul(o[:, e * SEQ:(e + 1) * SEQ], w[:, i, e * P:(e + 1) * P], src, start=True, stop=True)
                        mm.then_inc(made, 1)
                    elif it[0] == "Y":
                        if i == 0:
                            pe.wait_ge(ev["bc_split"], nth(L, "bc_split", 1))
                        project(k, k % 2, conv_block, m.bc, 4, False)
                        k += 1
                    elif it == "G":
                        for g in range(3):
                            project(k, k % 2, panel_block, xT, KT, False)
                            k += 1
                            if g == 0 and gm == 0:
                                for s in range(4):
                                    got(L, f"yp{s}")
                            if g == 0 and gm > 0:
                                for e in range(2):
                                    down(b, b % 2, from_h(h, h % 2), gm == 1 and e == 0)
                                    b += 1
                                    h += 1
                        gm += 1
                down(b, b % 2, from_h(h, h % 2), False)
                last_down(b + 1, (b + 1) % 2, from_h(h + 1, (h + 1) % 2))
                b += 2
                h += 2

            pe.wait_ge(consts_in, 16 * 3)
            transposes(0, x, x_updated)
            pe.wait_ge(rows_in, 16 * 10)
            columns([0])
            for L in range(2 * DEPTH):
                ffn()
                if L == 0:
                    pe.wait_ge(more_rows_in, 16 * 20)
                    columns(range(1, 2 * DEPTH))
                if L < DEPTH:
                    mixer1(L)
                else:
                    mixer2(L)
                block_end = L % DEPTH == DEPTH - 1
                ffn(not block_end)
                if L == DEPTH - 1:
                    u += 1
                    transposes(0, x, x_updated)

        @block.scalar
        def _(act):
            k = b = h = f = n = xk = sq = 0
            steps = 0

            def load_vectors(L):
                l = L % DEPTH
                s = rows_in if L == 0 else more_rows_in
                if L < DEPTH:
                    names = [("ffn1", T["ffn1_norm"][l]), ("mix", T["mix_norm"][l]), ("q", T["mla_q_norm"][l]),
                             ("kv", T["mla_kv_norm"][l]), ("dww", T["conv_dw_w"][l]), ("dwb", T["conv_dw_b"][l]),
                             ("hsw", T["hy_short_w"][l]), ("hsb", T["hy_short_b"][l]), ("out", T["out_norm"][l]),
                             ("ffn2", T["ffn2_norm"][l])]
                    at = COL1
                else:
                    names = [("ffn1", T["g_ffn1_2"][l]), ("mix", T["g_mix_2"][l]), ("wc", T["w_conv_2"][l]),
                             ("ps", T["pool_scale_2"][l]), ("ffn2", T["g_ffn2_2"][l])]
                    at = COL2
                for n, ap in names:
                    o, cnt = at[n]
                    if len(ap.shape) == 1:
                        src = ap.rearrange("(c p) -> c p", p=P)
                    else:
                        src = ap.rearrange("j (c p) -> (j c) p", p=P)
                    act.dma_start(xn[o:o + cnt, L // 2, (L % 2) * P:(L % 2 + 1) * P], src).then_inc(s, 16)

            for L in range(2 * DEPTH):
                load_vectors(L)

            def link(ins):
                nonlocal steps
                steps += 1
                ins.then_inc(act_step, 1)
                act.wait_ge(act_step, steps)

            def split_a(k, par, use):
                act.wait_ge(a_full[par], (use + 1) * 32)
                act.wait_ge(proj_done, k + 1)
                act.activation(a_hi[par][:, :], raw_a[par][:, :], ACT.Copy).then_inc(a_hi_ready, 1)

            def split_b(b, par, use):
                act.wait_ge(b_full[par], (use + 1) * 16)
                act.wait_ge(down_done, b + 1)
                act.activation(b_hi[par][:, :], raw_b[par][:, :], ACT.Copy).then_inc(b_hi_ready, 1)

            def squares(where, ready):
                for t in range(NT):
                    ready(t)
                    act.activation(where(t), x[:, t, :], ACT.Square, accum_out=ssq[:, t:t + 1]).then_inc(ssq_done, 1)

            def norm_to_xT(L, gain):
                nonlocal n
                for j in range(2):
                    act.wait_ge(xT_in_psum, 4 * n + 2 + j + 1)
                    for i in range(4):
                        kt = 4 * j + i
                        ins = act.activation(two(xT[:, kt, 0, :]), acc_halves[:, j, :, i * P:(i + 1) * P], ACT.Copy,
                                             scale=colv(L, gain, kt))
                    ins.then_inc(xT_hi, 1)
                n += 1

            def norm(L, gain):
                norm_to_xT(L, gain)
                squares(lambda t: xn[:, t, :], lambda t: None)

            def ffn_step(k, b, m, h, kh, ka, ua, kb_, ub, more_a=True, more_b=True):
                act.wait_ge(gate_scaled, m + 1)
                act.activation(sh[:, 0, :], gu[:, 0, :], ACT.Silu).then_inc(silu_done, 1)
                act.wait_ge(h_done, m + 1)
                act.activation(hT[kh][:, 0, :], sh[:, 1, :], ACT.Copy).then_inc(h_hi_ready, 1)
                if more_a:
                    split_a(k + 2, ka, ua)
                if more_b:
                    split_b(b + 1, kb_, ub)

            def ffn(L, gain, last, first=False):
                nonlocal k, b, h, f, xk
                if not first:
                    norm(L, gain)
                with act.Fori(0, FFU // 2 - 1 if last else FFU // 2) as i:
                    for e in range(2):
                        ffn_step(i * 2 + (k + e), i * 2 + (b + e), i * 2 + (f + e), i * 2 + (h + e), (h + e) % 2,
                                 (k + e) % 2, i + (k + e + 2) // 2, (b + e + 1) % 2, i + (b + e + 1) // 2)
                if last:
                    for j in (FFU - 2, FFU - 1):
                        ffn_step(k + j, b + j, f + j, h + j, (h + j) % 2, k % 2, 0, (b + j + 1) % 2, (b + j + 1) // 2,
                                 more_a=False, more_b=j < FFU - 1)
                k += FFU
                b += FFU
                h += FFU
                f += FFU
                xk += 1

            def read(L, name):
                act.wait_ge(made, small[L, name] + 1)
                return acc[:, small[L, name] % 4, :]

            def free(L, name):
                return taken[small[L, name] % 4]

            def panel():
                nonlocal k
                split_a(k + 2, k % 2, (k + 2) // 2)
                k += 1

            def row_split():
                nonlocal b
                split_b(b + 1, (b + 1) % 2, (b + 1) // 2)
                b += 1

            def mixer1(L):
                nonlocal k, b, xk, h
                m = m1
                norm(L, "mix")
                pk = {}
                ip = 0
                rows_done = 0
                for it in order_mix1():
                    i = int(it[-1]) if it[-1].isdigit() else None
                    kind = it.rstrip("0123456789")
                    if it == "A":
                        pk[PANELS1[ip][0]] = k
                        panel()
                        ip += 1
                    elif it == "B":
                        row_split()
                        rows_done += 1
                    elif it == "glu":
                        act.wait_ge(pair_read, pk["cg"] + 1 + CREDIT)
                        act.activation(m.cg[:, :, :], m.cg[:, :, :], ACT.Tanh, scale=0.5).then_inc(ev["gate_tanh"], 1)
                    elif kind == "f":
                        act.wait_ge(ev["filt_arg"], nth(L, "filt_arg", i))
                        act.activation(m.hdn, m.farg, ACT.Sin).then_inc(ev["filt_hidden"], 1)
                    elif kind == "h":
                        act.wait_ge(ev["filt_taps"], nth(L, "filt_taps", i))
                        act.activation(m.ab, m.kt, ACT.Abs).then_inc(ev["filt_abs"], 1)
                    elif it == "rope":
                        if L == 0:
                            for a in range(2):
                                act.wait_ge(ev["rope_arg"], a + 1)
                                act.activation(m.cs[:, a, :], m.ra[:, a, :], ACT.Sin).then_inc(ev["rope_done"], 1)
                    elif it == "qkv_sq":
                        act.wait_ge(pair_read, pk["kv"] + 1 + CREDIT)
                        act.activation(gu[:, :, :], m.hq[:, :, :], ACT.Square)
                        act.activation(sh[:, 0, :], m.hk[:, 0, :], ACT.Square).then_inc(ev["qkv_squares"], 1)
                        act.wait_ge(ev["qkv_squares"], nth(L, "qkv_squares"))
                        for e in range(2):
                            ins = act.activation(m.qn[:, e, :], m.hq[:, e, :], ACT.Copy, scale=colv(L, "q", e))
                        ins.then_inc(ev["q_gained"], 1)
                    elif it == "values":
                        for t in range(NT):
                            o = read(L, f"val{t}")
                            act.activation(m.V[:, t, :], o, ACT.Copy).then_inc(free(L, f"val{t}"), 1)
                    elif kind == "short":
                        act.wait_ge(pair_read, pk[("v", "x1", "x2")[i]] + 1 + CREDIT)
                        for e in range(2):
                            ins = act.activation(m.sc[:, e, :], m.hs[:, e, 1:SEQ + 1], ACT.Identity,
                                                 scale=colv(L, "hsw", 6 + 2 * i + e), bias=colv(L, "hsb", 2 * i + e))
                        ins.then_inc(ev["short_mid"], 1)
                        o = read(L, it)
                        act.activation(m.tv[i][:, :, :], two(o), ACT.Copy).then_inc(free(L, it), 1)
                    elif kind == "q":
                        o = read(L, it)
                        if i:
                            act.wait_ge(ev["q_roped"], nth(L, "q_roped", i - 1))
                        act.activation(m.qraw, o[0:QKD, :], ACT.Copy).then_inc(free(L, it), 1)
                    elif kind == "k" and i is not None:
                        o = read(L, it)
                        act.activation(m.kT[i % 2][0:NOPE, :], o[0:NOPE, :], ACT.Copy).then_inc(free(L, it), 1)
                    elif kind == "s":
                        act.wait_ge(ev["neg_max"], nth(L, "neg_max", i))
                        o = read(L, it)
                        for t in range(NT):
                            ins = act.activation(m.Pm[i % 2][:, t, :], o[:, t * SEQ:(t + 1) * SEQ], ACT.Exp, scale=m.qs[:, t:t + 1],
                                                 bias=m.mx[:, 2 * i + t:2 * i + t + 1], accum_out=m.sm[:, 2 * i + t:2 * i + t + 1])
                        ins.then_inc(free(L, it), 1)
                    elif kind == "p":
                        o = read(L, it)
                        if i >= 2:
                            act.wait_ge(made, small[L, f"o{i - 2}"] + 1)
                        act.activation(m.PT[i % 2], o, ACT.Copy).then_inc(free(L, it), 1)
                    elif it == "conv_out":
                        act.wait_ge(ev["ln_done"], nth(L, "ln_done"))
                        y = xn[:, :, 2 * CW:3 * CW]
                        act.activation(y, y, ACT.Silu).then_inc(ev["conv_silu"], 1)
                    elif it == "y_norm":
                        act.wait_ge(ev["conv_silu"], nth(L, "conv_silu"))
                        act.wait_ge(taken[small[L, "o7"] % 4], small[L, "o7"] // 4 + 1)
                        act.wait_ge(taken[small[L, "inv1"] % 4], small[L, "inv1"] // 4 + 1)
                        for s, (lo, hi) in enumerate(((0, 512), (512, 768), (768, 1024))):
                            for t in range(NT):
                                ins = act.activation(junk[:, 0:hi - lo], xn[:, t, lo:hi],
                                                     ACT.Square, accum_out=ssq[:, 2 * s + t:2 * s + t + 1])
                                if (s, t) != (2, NT - 1):
                                    link(ins)
                        ins.then_inc(ssq_done, 1)
                norm_to_xT(L, "out")
                for j in range(rows_done, KT):
                    row_split()
                xk += 1

            def mixer2(L):
                nonlocal k, b, xk, h
                m = m2
                norm(L, "mix")
                gm = 0
                for it in order_mix2():
                    i = int(it[-1]) if it[-1].isdigit() else None
                    if it == "A" or it[0] == "Y":
                        panel()
                    elif it[0] == "c":
                        o = read(L, it)
                        act.activation(m.ab[:, :, i, :], two(o), ACT.Copy).then_inc(free(L, it), 1)
                    elif it[0] == "t":
                        o = read(L, it)
                        act.activation(m.fT[:, 2 * i:2 * i + 2, :], two(o), ACT.Copy).then_inc(free(L, it), 1)
                    elif it[:2] == "yf":
                        o = read(L, it)
                        act.activation(m.yf[:, 2 * i:2 * i + 2, :], two(o), ACT.Copy).then_inc(free(L, it), 1)
                    elif it[:2] == "yp":
                        o = read(L, it)
                        for e in range(2):
                            ins = act.activation(m.yp[:, 2 * i + e, :], o[:, e * SEQ:(e + 1) * SEQ], ACT.Copy, scale=colv(L, "ps", 2 * i + e))
                        ins.then_inc(free(L, it), 1)
                    elif it[:2] == "bc":
                        act.wait_ge(ev["bc_f32"], nth(L, "bc_f32", i))
                        act.activation(m.bc[:, 2 * i:2 * i + 2, 0, :], m.gs[:, :, :], ACT.Copy).then_inc(ev["bc_hi"], 1)
                    elif it == "G":
                        for g in range(3):
                            panel()
                            act.wait_ge(pair_read, k + CREDIT)
                            act.activation(m.th[:, :, :], m.gs[:, :, :], ACT.Tanh, scale=0.5).then_inc(ev["gate_done"], 1)
                            if g == 1 and gm:
                                row_split()
                        act.wait_ge(ev["merged"], nth(L, "merged", gm))
                        for e in range(2):
                            act.activation(hT[h % 2][:, 0, :], m.mg[:, e, :], ACT.Copy).then_inc(h_hi_ready, 1)
                            h += 1
                            if e == 0:
                                row_split()
                        gm += 1
                row_split()
                xk += 1

            def final_norm():
                nonlocal xk
                for t in range(NT):
                    act.wait_ge(x_done, 4 * (xk - 1) + 2 * t + 2)
                    ins = act.activation(xn[:, 0, :], x[:, t, :], ACT.Square, accum_out=ssq[:, t:t + 1])
                    ins.then_inc(ssq_done, 1)
                    if t == 0:
                        act.wait_ge(ssq_done, squares_before(L + 1) + 1)
                xk += 1

            act.wait_ge(cols_done, 1)
            norm_to_xT(0, "ffn1")
            split_a(0, 0, 0)
            squares(lambda t: b_lo[t][:, :], lambda t: None)
            split_a(1, 1, 0)
            split_b(0, 0, 0)
            for L in range(2 * DEPTH):
                ffn(L, "ffn1", False, first=L == 0)
                if L < DEPTH:
                    mixer1(L)
                else:
                    mixer2(L)
                ffn(L, "ffn2", L == 2 * DEPTH - 1)
                if L % DEPTH == DEPTH - 1:
                    final_norm()

        @block.vector
        def _(dve):
            k = b = h = f = n = sq = vk = nr = 0
            steps = 0

            def step(ins):
                nonlocal steps
                steps += 1
                ins.then_inc(dve_step, 1)
                return steps

            def link(ins):
                dve.wait_ge(dve_step, step(ins))

            def split_a(k, par):
                dve.wait_ge(a_hi_ready, k + 1)
                dve.tensor_tensor(a_lo[par][:, :], raw_a[par][:, :], a_hi[par][:, :], SUB).then_inc(a_split, 1)

            def split_b(b, par):
                dve.wait_ge(b_hi_ready, b + 1)
                dve.tensor_tensor(b_lo[par][:, :], raw_b[par][:, :], b_hi[par][:, :], SUB).then_inc(b_split, 1)

            def scaled(k, par, dst):
                dve.wait_ge(proj_done, k + 1 + CREDIT)
                dve.tensor_tensor(dst, pair[par][:, :, :], bcast(rb[:, :], 2), MULT).then_inc(pair_read, 1)

            def variance(cols_, width):
                return dve.tensor_scalar(var[:, cols_], ssq[:, cols_], 1.0 / width, EPS, MULT, ADD)

            def xT_low(L, gain):
                nonlocal n
                for j in range(2):
                    dve.wait_ge(xT_hi, 2 * n + j + 1)
                    for i in range(4):
                        kt = 4 * j + i
                        dve.scalar_tensor_tensor(two(xT[:, kt, 1, :]), acc_halves[:, j, :, i * P:(i + 1) * P], colv(L, gain, kt),
                                                 two(xT[:, kt, 0, :].bitcast(F32)), MULT, SUB).then_inc(xT_split, 1)
                n += 1

            def norm(L, gain, next_a=False, next_b=True, first=False):
                nonlocal sq, vk, nr
                xT_low(L, gain)
                if first:
                    split_a(0, 0)
                if next_a:
                    split_a(k + 1, (k + 1) % 2)
                sq += NT
                vk += 1
                dve.wait_ge(ssq_done, sq)
                variance(slice(0, 2), DM).then_inc(var_done, 1)
                if next_b:
                    split_b(b, b % 2)
                dve.wait_ge(rstd_done, vk)
                for t in range(NT):
                    ins = dve.tensor_scalar(diag[:, t, :], eye[:, :], rstd[:, t:t + 1], None, MULT)
                ins.then_inc(diag_done, 1)
                nr += 1
                dve.wait_ge(rb_in_psum, nr)
                dve.tensor_copy(rb[:, :], rb_psum[:, :]).then_inc(rb_read, 1)
                dve.wait_ge(rb_read, nr)

            def update_x(scale, b):
                nonlocal phases
                phases += 1
                for q in range(4):
                    if q < 3:
                        dve.wait_ge(acc_bank, 3 * (phases - 1) + q + 1)
                    else:
                        dve.wait_ge(down_done, b + 1 + CREDIT)
                    xq = x[:, q // 2, (q % 2) * HALF:(q % 2 + 1) * HALF]
                    dve.scalar_tensor_tensor(xq, acc[:, 2 * (q % 2) + q // 2, :], scale, xq, MULT, ADD).then_inc(x_done, 1)
            phases = 0

            def h_low(h, kh, src):
                dve.wait_ge(h_hi_ready, h + 1)
                dve.tensor_tensor(hT[kh][:, 1, :], src, hT[kh][:, 0, :], SUB).then_inc(h_split, 1)

            def ffn(L, gain, last, next_a):
                nonlocal k, b, h, f
                norm(L, gain, next_a=next_a, first=L == 0 and gain == "ffn1")

                def one(k, b, m, h, ka, kb_, kh, more=True):
                    dve.wait_ge(proj_done, k + 1 + CREDIT)
                    dve.tensor_tensor(gu[:, 0, :], pair[ka][:, 0, :], rb[:, :], MULT).then_inc(gate_scaled, 1)
                    dve.tensor_tensor(gu[:, 1, :], pair[ka][:, 1, :], rb[:, :], MULT).then_inc(pair_read, 1)
                    dve.wait_ge(pair_read, k + 1 + CREDIT)
                    dve.wait_ge(silu_done, m + 1)
                    dve.tensor_tensor(sh[:, 1, :], sh[:, 0, :], gu[:, 1, :], MULT).then_inc(h_done, 1)
                    dve.wait_ge(h_done, m + 1)
                    h_low(h, kh, sh[:, 1, :])
                    if more:
                        split_a(k + 2, ka)
                        split_b(b + 1, (kb_ + 1) % 2)
                with dve.Fori(0, FFU // 2 - 1) as i:
                    for e in range(2):
                        one(i * 2 + (k + e), i * 2 + (b + e), i * 2 + (f + e), i * 2 + (h + e), (k + e) % 2, (b + e) % 2, (h + e) % 2)
                j = FFU - 2
                one(k + j, b + j, f + j, h + j, (k + j) % 2, (b + j) % 2, (h + j) % 2, more=False)
                if not last:
                    split_a(k + j + 2, (k + j) % 2)
                split_b(b + j + 1, (b + j + 1) % 2)
                j = FFU - 1
                one(k + j, b + j, f + j, h + j, (k + j) % 2, (b + j) % 2, (h + j) % 2, more=False)
                k += FFU
                b += FFU
                h += FFU
                f += FFU
                update_x(0.5, b - 1)

            def read(L, name):
                dve.wait_ge(made, small[L, name] + 1)
                return acc[:, small[L, name] % 4, :]

            def free(L, name):
                return taken[small[L, name] % 4]

            def took(L, name):
                dve.wait_ge(free(L, name), small[L, name] // 4 + 1)

            def panel(dst, factors=True):
                nonlocal k
                if factors:
                    scaled(k, k % 2, dst)
                else:
                    dve.wait_ge(proj_done, k + 1 + CREDIT)
                    dve.tensor_copy(dst, pair[k % 2][:, :, :]).then_inc(pair_read, 1)
                split_a(k + 2, k % 2)
                k += 1

            def row_split():
                nonlocal b
                split_b(b + 1, (b + 1) % 2)
                b += 1

            def reduced(src, tmp, dst, turn):
                link(dve.tensor_scalar(tmp, src, 1.0 / TWO_PI, turn, MULT, ADD))
                link(dve.tensor_scalar(tmp, tmp, ROUND, ROUND, ADD, SUB))
                link(dve.scalar_tensor_tensor(dst, tmp, -PI_A, src, MULT, ADD))
                link(dve.scalar_tensor_tensor(dst, tmp, -PI_B, dst, MULT, ADD))
                link(dve.scalar_tensor_tensor(dst, tmp, -PI_C, dst, MULT, ADD))
                if turn:
                    link(dve.tensor_scalar(dst, dst, TWO_PI * turn, None, ADD))
                return dve.tensor_scalar(dst, dst, PI_F, -PI_F, ALU.min, ALU.max)

            def bcast(ap, n_):
                q = ap.rearrange("p (o c) -> p o c", o=1)
                return q.broadcast_to([q.shape[0], n_, q.shape[2]])

            def mixer1(L):
                nonlocal k, b, sq, vk
                m = m1
                norm(L, "mix", next_a=True)
                if L == 0:
                    dve.wait_ge(rows_T, 2)
                    for i in range(1, 2 * DEPTH):
                        r = ROWS1 if i < DEPTH else ROWS2
                        ins = dve.tensor_copy(cols[:, i, 0:r], cols_psum[:, i, 0:r])
                    ins.then_inc(cols_done, 1)
                    dve.wait_ge(cols_done, 2)
                dst = {"ca": m.ca[:, :, :], "cg": m.cg[:, :, :], "q": m.hq[:, :, :], "kv": m.hk[:, :, :],
                       "v": m.hs[:, :, 1:SEQ + 1], "x1": m.hs[:, :, 1:SEQ + 1], "x2": m.hs[:, :, 1:SEQ + 1]}
                dve.wait_ge(params_in[L], 16 * N_PARAM1)
                ip = taps = rows_done = 0
                tap_step = [0, 0]
                pk = {}
                for it in order_mix1():
                    i = int(it[-1]) if it[-1].isdigit() else None
                    kind = it.rstrip("0123456789")
                    if it == "A":
                        pk[PANELS1[ip][0]] = k
                        panel(dst[PANELS1[ip][0]])
                        ip += 1
                    elif it == "B":
                        row_split()
                        rows_done += 1
                    elif it == "glu":
                        dve.wait_ge(ev["gate_tanh"], nth(L, "gate_tanh"))
                        link(dve.scalar_tensor_tensor(m.u[:, :, PADC:PADC + SEQ], m.cg[:, :, :], 1.0, m.ca[:, :, :], ADD, MULT))
                    elif it == "taps":
                        for j in tap_range(taps):
                            for e in range(2):
                                src = m.u[:, e, j:j + SEQ]
                                if j == 0:
                                    tap_step[e] = step(dve.tensor_scalar(m.co[:, e, :], src, colv(L, "dww", 2 * j + e), None, MULT))
                                else:
                                    dve.wait_ge(dve_step, tap_step[e])
                                    tap_step[e] = step(dve.scalar_tensor_tensor(m.co[:, e, :], src, colv(L, "dww", 2 * j + e),
                                                                               m.co[:, e, :], MULT, ADD))
                        taps += 1
                    elif kind == "f":
                        o = read(L, it)
                        dve.tensor_scalar(m.farg, o[0:FILT, 0:SEQ], m.fcol[:, i:i + 1], m.fcol[:, 3:4], ADD, MULT).then_inc(free(L, it), 1)
                        took(L, it)
                        reduced(m.farg, m.fq, m.farg, 0.0).then_inc(ev["filt_arg"], 1)
                    elif it == "rope":
                        if L == 0:
                            dve.wait_ge(block1_in, 16 * N_BLOCK1)
                            link(dve.tensor_copy(m.posf, m.pos[:, :]))
                            link(dve.tensor_scalar(m.posf, m.posf, m.invf[:, 0:1], None, MULT))
                            for a, turn in enumerate((0.25, 0.0)):
                                reduced(m.posf, m.fq96, m.ra[:, a, :], turn).then_inc(ev["rope_arg"], 1)
                                dve.wait_ge(ev["rope_arg"], a + 1)
                    elif kind == "h":
                        if i:
                            dve.wait_ge(ev["filt_abs"], nth(L, "filt_abs", i - 1))
                        elif L == 0:
                            dve.wait_ge(ev["rope_done"], 2)
                        for t in range(NT):
                            o = read(L, f"{it}t{t}")
                            dve.tensor_tensor(m.kt[:, t], two(o), bcast(m.decay[:, t, :], 2), MULT).then_inc(free(L, f"{it}t{t}"), 1)
                        for t in range(NT):
                            took(L, f"{it}t{t}")
                        link(dve.memset(m.kt[0:1, 0, 1, :], 0.0))
                        dve.tensor_tensor(m.ks, m.kt[:, :, 0, :], m.kt[:, :, 1, :], ADD).then_inc(ev["filt_taps"], 1)
                        dve.tensor_tensor(m.kd, m.kt[:, :, 0, :], m.kt[:, :, 1, :], SUB).then_inc(ev["filt_sums"], 1)
                    elif kind == "n":
                        o = read(L, it)
                        link(dve.reciprocal(m.rn, o[:, 0:CW]))
                        dve.tensor_tensor(m.KN[:, i, :], o[0:1, CW:2 * CW], m.rn[0:1, :], MULT).then_inc(free(L, it), 1)
                        took(L, it)
                        link(dve.tensor_tensor(m.KN[:, i, :], m.KN[:, i, :], m.dB[0:1, i, :], ADD))
                    elif kind == "spec":
                        o = read(L, f"A{i}")
                        dve.tensor_tensor(m.KA[i][:, :, :], two(o), bcast(m.rn, 2), MULT).then_inc(free(L, f"A{i}"), 1)
                        o = read(L, f"B{i}")
                        dve.tensor_tensor(m.KB[i][:, :, :], two(o), bcast(m.rn, 2), MULT).then_inc(free(L, f"B{i}"), 1)
                        took(L, f"A{i}")
                        link(dve.tensor_tensor(m.KA[i][:, :, :], m.KA[i][:, :, :], bcast(m.dB[:, i, :], 2), ADD))
                        took(L, f"B{i}")
                        link(dve.memset(m.KB[i][0:1, 0, :], 0.0))
                    elif it == "stat":
                        o = read(L, it)
                        dve.tensor_scalar(var[:, 0:2], o[:, 0:2], 1.0 / QR, EPS, MULT, ADD)
                        dve.tensor_scalar(var[:, 2:4], o[:, 2:4], 1.0 / KVR, EPS, MULT, ADD).then_inc(free(L, it), 1)
                        dve.wait_ge(ev["qkv_rstd"], nth(L, "qkv_rstd"))
                        dve.tensor_scalar(m.qs[:, 0:2], rstd[:, 0:2], float(QKD) ** -0.5, None, MULT)
                        link(dve.tensor_scalar(m.qs[:, 2:4], rstd[:, 0:2], -float(QKD) ** -0.5, None, MULT))
                        for t in range(NT):
                            ins = dve.tensor_scalar(m.kvn[:, t * P:(t + 1) * P], eye[:, :], rstd[:, 2 + t:3 + t], None, MULT)
                        ins.then_inc(ev["kv_diag"], 1)
                    elif it == "kb":
                        o = read(L, it)
                        dve.scalar_tensor_tensor(m.kvn[:, :], m.hk[:, 0, :], colv(L, "kv"), o[:, 0:SEQ], MULT, MULT).then_inc(free(L, it), 1)
                    elif kind == "short":
                        dve.wait_ge(ev["short_mid"], nth(L, "short_mid", i))
                        s0 = [step(dve.scalar_tensor_tensor(m.sc[:, e, :], m.hs[:, e, 0:SEQ], colv(L, "hsw", 2 * i + e), m.sc[:, e, :],
                                                            MULT, ADD)) for e in range(2)]
                        for e in range(2):
                            dve.wait_ge(dve_step, s0[e])
                            ins = dve.scalar_tensor_tensor(m.sc[:, e, :], m.hs[:, e, 2:SEQ + 2], colv(L, "hsw", 12 + 2 * i + e),
                                                           m.sc[:, e, :], MULT, ADD)
                        ins.then_inc(ev["short_done"], 1)
                    elif kind == "fwd":
                        r = read(L, f"re{i}")
                        link(dve.tensor_tensor(m.Yr[:, :, :], two(r), m.KA[i][:, :, :], MULT))
                        dve.tensor_tensor(m.Yi[:, :, :], two(r), m.KB[i][:, :, :], MULT).then_inc(free(L, f"re{i}"), 1)
                        q = read(L, f"im{i}")
                        link(dve.tensor_tensor(m.tmp[:, :, :], two(q), m.KB[i][:, :, :], MULT))
                        link(dve.tensor_tensor(m.Yr[:, :, :], m.Yr[:, :, :], m.tmp[:, :, :], SUB))
                        link(dve.tensor_tensor(m.tmp[:, :, :], two(q), m.KA[i][:, :, :], MULT))
                        took(L, f"re{i}")
                        link(dve.tensor_tensor(m.Yi[:, :, :], m.Yi[:, :, :], m.tmp[:, :, :], ADD))
                        dve.tensor_tensor(m.Yi[0:1, 0, :], q[0:1, 0:CW], m.KN[:, i, :], MULT).then_inc(free(L, f"im{i}"), 1)
                        took(L, f"im{i}")
                        dve.tensor_copy(m.mx[0:1, 0:1], m.Yi[0:1, 0, 0:1]).then_inc(ev["spectrum"], 1)
                    elif kind == "inv":
                        o = read(L, it)
                        if i == 0:
                            dve.wait_ge(free(L, "short1"), small[L, "short1"] // 4 + 1)
                            dve.tensor_tensor(m.tv[0][:, :, :], two(o), m.tv[1][:, :, :], MULT).then_inc(free(L, it), 1)
                        else:
                            dve.wait_ge(free(L, "short2"), small[L, "short2"] // 4 + 1)
                            dve.tensor_tensor(xn[:, :, 3 * CW:4 * CW], two(o), m.tv[2][:, :, :], MULT).then_inc(free(L, it), 1)
                    elif kind == "rot":
                        o = read(L, it)
                        took(L, f"q{i}")
                        link(dve.tensor_tensor(two(m.qc), two(m.qraw), bcast(m.cs[:, 0, :], 2), MULT))
                        dve.tensor_tensor(two(m.qp[i % 2]), two(o[0:QKD, :]), bcast(m.cs[:, 1, :], 2), MULT).then_inc(free(L, it), 1)
                        took(L, it)
                        dve.tensor_tensor(m.qp[i % 2], m.qp[i % 2], m.qc, ADD).then_inc(ev["q_roped"], 1)
                    elif it == "kpe":
                        r = slice(NOPE, QKD)
                        o = read(L, it)
                        link(dve.tensor_tensor(m.kpe[r], m.hk[r, 1, :], m.cs[r, 0, :], MULT))
                        dve.tensor_tensor(m.kpe2[r], o[r, 0:SEQ], m.cs[r, 1, :], MULT).then_inc(free(L, it), 1)
                        took(L, it)
                        for j in range(2):
                            ins = dve.tensor_tensor(two(m.kT[j])[r], bcast(m.kpe[r], 2), bcast(m.kpe2[r], 2), ADD)
                        ins.then_inc(ev["kpe_roped"], 1)
                    elif kind == "s":
                        o = read(L, it)
                        link(dve.tensor_reduce(m.mx[:, 2 * i:2 * i + 2], two(o), AX, ALU.max))
                        dve.tensor_tensor(m.mx[:, 2 * i:2 * i + 2], m.mx[:, 2 * i:2 * i + 2], m.qs[:, 2:4], MULT).then_inc(ev["neg_max"], 1)
                    elif kind == "o":
                        took(L, f"s{i}")
                        link(dve.reciprocal(m.rs[:, 2 * i:2 * i + 2], m.sm[:, 2 * i:2 * i + 2]))
                        o = read(L, it)
                        dve.tensor_tensor(xn[:, :, i * VD:(i + 1) * VD], o[:, 0:2 * VD].rearrange("p (t c) -> p t c", t=2),
                                          m.rs[:, 2 * i:2 * i + 2].rearrange("p (t o) -> p t o", o=1).broadcast_to([P, NT, VD]),
                                          MULT).then_inc(free(L, it), 1)
                    elif it == "conv_out":
                        for e in range(2):
                            dve.wait_ge(dve_step, tap_step[e])
                            ins = dve.tensor_scalar(m.co[:, e, :], m.co[:, e, :], 0.5, colv(L, "dwb", e), MULT, ADD)
                        ins.then_inc(ev["conv_done"], 1)
                        o = read(L, it)
                        y = xn[:, :, 2 * CW:3 * CW]
                        dve.tensor_copy(y, two(o)).then_inc(free(L, it), 1)
                        took(L, it)
                        for t in range(NT):
                            st = step(dve.bn_stats(m.bn[:, t, :], y[:, t, :]))
                        dve.wait_ge(dve_step, st)
                        for t in range(NT):
                            st = step(dve.bn_aggr(m.mv[:, t, :], m.bn[:, t, :]))
                        dve.wait_ge(dve_step, st)
                        dve.tensor_scalar(var[:, 6:8], m.mv[:, :, 1], EPS, None, ADD).then_inc(ev["ln_var"], 1)
                        dve.wait_ge(ev["ln_rstd"], nth(L, "ln_rstd"))
                        for t in range(NT):
                            st = step(dve.tensor_scalar(y[:, t, :], y[:, t, :], m.mv[:, t, 0:1], rstd[:, 6 + t:7 + t], SUB, MULT))
                        dve.wait_ge(dve_step, st)
                        link(dve.tensor_tensor(y, y, bcast(m.lngb[:, 0, :], 2), MULT))
                        dve.tensor_tensor(y, y, bcast(m.lngb[:, 1, :], 2), ADD).then_inc(ev["ln_done"], 1)
                sq += 1
                vk += 1
                dve.wait_ge(ssq_done, sq)
                variance(slice(0, 2), 2 * CW)
                variance(slice(2, 6), CW).then_inc(var_done, 1)
                dve.wait_ge(rstd_done, vk)
                for t in range(NT):
                    for s, (lo, hi) in enumerate(((0, 512), (512, 768), (768, 1024))):
                        ins = dve.tensor_scalar(xn[:, t, lo:hi], xn[:, t, lo:hi], rstd[:, 2 * s + t:2 * s + t + 1], None, MULT)
                    ins.then_inc(xn_done, 1)
                xT_low(L, "out")
                for j in range(rows_done, KT - 1):
                    row_split()
                b += 1
                update_x(1.0, b - 1)

            def mixer2(L):
                nonlocal k, b, h
                m = m2
                if L == DEPTH:
                    dve.memset(m.uP[:, :, 0:PADP], 0.0)
                    dve.memset(m.uP[:, :, PADP + SEQ:], 0.0)
                    dve.memset(m.z[:, :, 0:1], 0.0)
                    link(dve.memset(m.z[:, :, SEQ + 1:], 0.0))
                norm(L, "mix", next_a=True)
                ia = gm = 0
                for it in order_mix2():
                    i = int(it[-1]) if it[-1].isdigit() else None
                    if it == "A":
                        name, j = PANELS2[ia]
                        panel({"F": m.uF[:, 2 * j:2 * j + 2, :], "P": m.uP[:, 2 * j:2 * j + 2, PADP:PADP + SEQ],
                               "C": m.c[:, :, :], "V": m.v[:, :, :], "B": m.gs[:, :, :]}[name])
                        ia += 1
                    elif it[0] == "Y":
                        panel(m.yc[:, 2 * i:2 * i + 2, :], factors=False)
                    elif it == "pool":
                        dve.wait_ge(pair_read, k + CREDIT)
                        if L == DEPTH:
                            dve.wait_ge(block2_in, 16 * N_BLOCK2)
                        w = SEQ + 2 * PADP
                        link(dve.tensor_tensor(m.d1[:, :, 0:w - 1], m.uP[:, :, 0:w - 1], m.uP[:, :, 1:w], ADD))
                        link(dve.tensor_tensor(m.d2[:, 1:4, 0:w - 3], m.d1[:, 1:4, 0:w - 3], m.d1[:, 1:4, 2:w - 1], ADD))
                        link(dve.tensor_tensor(m.d1[:, 2:4, 0:w - 7], m.d2[:, 2:4, 0:w - 7], m.d2[:, 2:4, 4:w - 3], ADD))
                        link(dve.tensor_tensor(m.d2[:, 3, 0:w - 15], m.d1[:, 3, 0:w - 15], m.d1[:, 3, 8:w - 7], ADD))
                        for g, d in enumerate((m.d1, m.d2, m.d1, m.d2)):
                            at = PADP - WINDOWS[g] // 2
                            link(dve.tensor_tensor(m.cvp[:, g, :], d[:, g, at:at + SEQ], m.count[:, g, :], MULT))
                        dve.tensor_tensor(m.d1[:, :, 0:SEQ], m.cvp[:, :, :], m.uP[:, :, PADP:PADP + SEQ], SUB).then_inc(ev["pooled"], 1)
                    elif it[0] == "z":
                        zz = m.z[:, 2 * i:2 * i + 2, :]
                        dve.wait_ge(pair_read, k + CREDIT)
                        link(dve.tensor_tensor(zz[:, :, 1:SEQ + 1], m.c[:, :, :], m.v[:, :, :], MULT))
                        st = [step(dve.tensor_scalar(m.cv[:, e, :], zz[:, e, 0:SEQ], colv(L, "wc", 2 * i + e), None, MULT)) for e in range(2)]
                        for j in (1, 2):
                            for e in range(2):
                                dve.wait_ge(dve_step, st[e])
                                st[e] = step(dve.scalar_tensor_tensor(m.cv[:, e, :], zz[:, e, j:j + SEQ], colv(L, "wc", 4 * j + 2 * i + e),
                                                                      m.cv[:, e, :], MULT, ADD))
                        dve.wait_ge(dve_step, st[1])
                    elif it[:2] == "bc":
                        dve.wait_ge(pair_read, k + CREDIT)
                        dve.tensor_tensor(m.gs[:, :, :], m.gs[:, :, :], m.cv[:, :, :], MULT).then_inc(ev["bc_f32"], 1)
                        dve.wait_ge(ev["bc_hi"], nth(L, "bc_hi", i))
                        dve.tensor_tensor(m.bc[:, 2 * i:2 * i + 2, 1, :], m.gs[:, :, :], m.bc[:, 2 * i:2 * i + 2, 0, :], SUB)\
                           .then_inc(ev["bc_split"], 1)
                    elif it == "G":
                        for g, y in enumerate((m.yf, m.yc, m.yp)):
                            yy = y[:, 2 * gm:2 * gm + 2, :]
                            panel(m.gs[:, :, :])
                            if g == 1 and gm:
                                row_split()
                            dve.wait_ge(ev["gate_done"], nth(L, "gate_done", 3 * gm + g))
                            if g == 0:
                                if gm == 0:
                                    for s in ("yf", "yp"):
                                        for q in range(4):
                                            took(L, f"{s}{q}")
                                link(dve.scalar_tensor_tensor(m.mg[:, :, :], m.th[:, :, :], 1.0, yy, ADD, MULT))
                            else:
                                link(dve.scalar_tensor_tensor(m.cv[:, :, :], m.th[:, :, :], 1.0, yy, ADD, MULT))
                                ins = dve.tensor_tensor(m.mg[:, :, :], m.mg[:, :, :], m.cv[:, :, :], ADD)
                                if g == 1:
                                    link(ins)
                                else:
                                    ins.then_inc(ev["merged"], 1)
                        for e in range(2):
                            h_low(h, h % 2, m.mg[:, e, :])
                            h += 1
                            if e == 0:
                                row_split()
                        gm += 1
                b += 1
                update_x(0.5, b - 1)

            def final_norm(L):
                nonlocal sq, vk
                sq += NT
                vk += 1
                dve.wait_ge(ssq_done, sq)
                variance(slice(0, 2), DM).then_inc(var_done, 1)
                dve.wait_ge(rstd_done, vk)
                dve.wait_ge(gain_in, 16 * (L // DEPTH + 1))
                for q in range(4):
                    t, at = q // 2, slice((q % 2) * HALF, (q % 2 + 1) * HALF)
                    dve.scalar_tensor_tensor(x[:, t, at], x[:, t, at], rstd[:, t:t + 1], xn[:, 1, at], MULT, MULT).then_inc(x_done, 1)

            dve.memset(ones[:, :], 1.0)
            dve.memset(junk[:, 0:1], 0.0).then_inc(a_split, CREDIT)
            dve.memset(junk[:, 1:2], 0.0).then_inc(b_split, CREDIT)
            dve.memset(junk[:, 2:3], 0.0).then_inc(pair_read, CREDIT)
            dve.memset(m1.u[:, :, 0:PADC], 0.0)
            dve.memset(m1.u[:, :, PADC + SEQ:], 0.0)
            dve.memset(m1.hs[:, :, 0:1], 0.0)
            dve.memset(m1.hs[:, :, SEQ + 1:], 0.0)
            dve.memset(minus_half[:, :], -0.5).then_inc(half_set, 1)
            dve.wait_ge(rows_T, 1)
            dve.tensor_copy(cols[:, 0, 0:ROWS1], cols_psum[:, 0, 0:ROWS1]).then_inc(cols_done, 1)
            dve.wait_ge(cols_done, 1)
            for L in range(2 * DEPTH):
                ffn(L, "ffn1", False, next_a=True)
                if L < DEPTH:
                    mixer1(L)
                else:
                    mixer2(L)
                ffn(L, "ffn2", L == 2 * DEPTH - 1, next_a=False)
                if L % DEPTH == DEPTH - 1:
                    final_norm(L)


def kernel(**inputs):
    import concourse.bacc as bacc
    from concourse.bass_utils import run_bass_kernel_spmd

    nc = bacc.Bacc("TRN2", target_bir_lowering=False, num_devices=1)
    arrays = {n: np.ascontiguousarray(v) for n, v in inputs.items()}
    arrays.update(host_constants())
    feed = {f"in_{n}": v for n, v in arrays.items()}
    T = {n: nc.dram_tensor(f"in_{n}", v.shape, mybir.dt.from_np(v.dtype), kind="ExternalInput").ap() for n, v in arrays.items()}
    out = nc.dram_tensor("out_0", (1, SEQ, DM), mybir.dt.float32, kind="ExternalOutput").ap()
    build(nc, T, out)
    r = run_bass_kernel_spmd(nc, [feed], core_ids=[0])
    return r.results[0]["out_0"]
```

```python
import math

import numpy as np

import concourse.bass as bass
from concourse import mybir
from contextlib import ExitStack

P = 128
SEQ = 256
DM = 1024
FF = 2816
DEPTH = 2
EPS = 1e-6
NT = SEQ // P
KT = DM // P
FFU = FF // P
HALF = 512
A_COLS = 2 * KT * P
HEADS, NOPE, ROPE, VD = 8, 64, 32, 64
QKD = NOPE + ROPE
QR, KVR = 256, 128
CW = 256
CK = 31
PADC = CK // 2
FILT = 64
EMB = 33
NFFT = 2 * SEQ
PANELS1 = [("ca", 416), ("cg", 672), ("q", 0), ("kv", 256), ("v", 928), ("x1", 1184), ("x2", 1440)]
GROUPS = 4
PANELS2 = ([("F", 0), ("F", 1), ("P", 0), ("P", 1), ("C", 0), ("V", 0), ("B", 0), ("C", 1), ("V", 1), ("B", 1)])
OFF2 = {"F": 0, "B": 512, "C": 1024, "V": 1536, "P": 2048, "G": 2560}
WINDOWS = (2, 4, 8, 16)
PADP = 8

COL1, COL2 = {}, {}
_n = 0
for _name, _k in (("ffn1", 8), ("mix", 8), ("q", 2), ("kv", 1), ("dww", 62), ("dwb", 2), ("hsw", 18), ("hsb", 6),
                  ("out", 8), ("ffn2", 8)):
    COL1[_name] = (_n, _k)
    _n += _k
ROWS1 = _n
_n = 0
for _name, _k in (("ffn1", 8), ("mix", 8), ("wc", 12), ("ps", 8), ("ffn2", 8)):
    COL2[_name] = (_n, _k)
    _n += _k
ROWS2 = _n

TWO_PI = 2.0 * math.pi
PI_A = 6.28125
PI_B = float(np.float32(np.round((TWO_PI - PI_A) * 2.0**21) / 2.0**21))
PI_C = float(TWO_PI - PI_A - PI_B)
ROUND = 12582912.0
PI_F = 3.1415925

CREDIT = 2


ORDER1 = {
    "pe": """A A A A A stat A kb short0 A short1 re0 val0 short2 im0 q0 k0 kpe rot0 val1 inv0 s0 s1 p0 re1 im1 q1
             o0 rot1 k1 inv1 s2 k2 q2 p1 s3 o1 rot2 p2 q3 p3 s4 o2 s5 p4 rot3 k3 o3 o4 s6 p5 s7 o5 p6 o6 conv_out
             p7 o7 yT""".split(),
    "act": """A A A glu A qkv_sq A short0 A copy0 short1 A short2 copy1 copy2 val0 k0 q0 val1 s0 s1 p0 row q1 k1
             s2 q2 p1 k2 s3 p2 q3 p3 s4 s5 p4 k3 p5 s6 p6 s7 conv_out ysq p7 msq yhi""".split(),
    "dve": """A A A glu taps A taps taps stat A short0 taps A taps kb short1 A short2 taps re0 taps im0 taps kpe
             rot0 taps inv0 s0 s1 taps taps re1 im1 o0 rot1 taps taps s2 taps inv1 taps s3 o1 rot2 taps taps s4
             taps s5 o2 taps rot3 row o3 s6 o4 taps s7 o5 cbias conv_out o6 yn o7 ylo mn""".split(),
}

FILTER_ITEMS = [["f0"], ["f1"], ["f2"], ["h0"], ["n0", "A0"], ["B0"], ["h1"], ["n1", "A1"], ["B1"], []]
FILTER_UNITS = len(FILTER_ITEMS)


N_PARAM1 = 14
N_PARAM2 = 2
N_BLOCK1 = 3
N_BLOCK2 = 3
TAP_PARTS = ORDER1["dve"].count("taps")


Y_TILES = [4, 5, 6, 7, 0, 1, 2, 3]


X_TILES = [0, 1, 4, 5, 2, 3, 6, 7]


def tap_range(part):
    return range(CK * part // TAP_PARTS, CK * (part + 1) // TAP_PARTS)


def small_steps1():
    s = []
    for it in ORDER1["pe"]:
        if it not in ("A", "yT"):
            s.append(it)
    return s


def filter_steps():
    s = []
    for it in sum(FILTER_ITEMS, []):
        s += [f"{it}t{t}" for t in range(NT)] if it in ("h0", "h1") else [it]
    return s


FILTER_STEPS = filter_steps()


SMALL1 = small_steps1()


ORDER2 = {
    "pe": """A A c0 c1 c2 c3 A A t0 A A A t1 A A A yf0 yf1 yf2 yf3 yp0 yp1 yp2 yp3 Y0 Y1 Y2 Y3""".split(),
    "act": """A A c0 c1 c2 c3 A A t0 A A A bc0 t1 A A A bc1 yf0 yf1 yf2 yf3 yp0 yp1 yp2 yp3 Y0 Y1 Y2 Y3""".split(),
    "dve": """A A A A pool A A z0 A bc0 A A z1 A bc1 Y0 Y1 Y2 Y3""".split(),
}


SMALL2 = [it for it in ORDER2["pe"] if it != "A" and it[0] != "Y"]


def conv_width(i):
    return A_COLS // 2 if len(PANELS2) <= i + 2 < len(PANELS2) + 4 else A_COLS


def norms_before(L):
    return 3 * L


def squares_before(L):
    return 6 * L + (2 if L > DEPTH else 0)


def host_constants():
    f64 = np.float64
    t = np.arange(SEQ, dtype=f64)
    f = np.arange(SEQ, dtype=f64)
    ang = 2 * np.pi * np.outer(t, f) / NFFT
    alt = np.where(np.arange(SEQ) % 2 == 0, 1.0, -1.0)
    cf = np.cos(ang)
    sf = -np.sin(ang)
    sf[:, 0] = alt
    w = np.full(SEQ, 2.0 / NFFT)
    w[0] = 1.0 / NFFT
    ci = w[:, None] * np.cos(ang.T)
    si = -w[:, None] * np.sin(ang.T)
    si[0, :] = alt / NFFT
    ps = 2 * np.pi * np.outer(t, t) / SEQ
    k = np.arange(P, dtype=f64)
    pc = 2 * np.pi * np.outer(k, k) / P
    norm = 1.0 / math.sqrt(SEQ * P)
    f32 = np.float32
    tt = np.linspace(0.0, 1.0, SEQ, dtype=f32)[:, None]
    bands = (EMB - 1) // 2
    a = (f32(2.0 * math.pi) * np.arange(SEQ, dtype=f32)[:, None] / f32(SEQ)).astype(f32)
    fb = np.linspace(1e-4, bands - 1, bands, dtype=f32)[None, :]
    z = np.concatenate([tt, np.cos(fb * a), -np.sin(fb * a)], axis=-1).astype(f32)
    max_decay = math.log(1e-2) / 0.3
    min_decay = math.log(1e-2) / 1.5
    deltas = np.linspace(min_decay, max_decay, CW, dtype=f32)
    decay = np.exp(-tt * np.abs(deltas)).astype(f32)
    rot = np.zeros((QKD, QKD))
    for i in range(ROPE // 2):
        rot[NOPE + 16 + i, NOPE + i] = -1.0
        rot[NOPE + i, NOPE + 16 + i] = 1.0
    invf = np.zeros((QKD, 1), f32)
    base = 1.0 / (f32(10000.0) ** (np.arange(0, ROPE, 2, dtype=f32) / f32(ROPE)))
    invf[NOPE:NOPE + 16, 0] = base
    invf[NOPE + 16:, 0] = base
    rc = np.zeros((P, GROUPS, SEQ))
    for g, win in enumerate(WINDOWS):
        cnt = np.minimum(t + win // 2, SEQ) - np.maximum(t - win // 2, 0)
        rc[:, g, :] = 1.0 / cnt
    out = {
        "k_dft": np.stack([cf, sf, ci, si]),
        "k_seq": np.stack([np.cos(ps) * norm, -np.sin(ps) * norm]),
        "k_chan": np.concatenate([np.cos(pc), np.sin(pc)], axis=1),
        "k_emb": np.ascontiguousarray(z.T),
        "k_decay": decay,
        "k_rot": rot,
        "k_invf": invf,
        "k_count": rc,
        "k_eye": np.eye(P),
    }
    return {n: np.ascontiguousarray(v, dtype=f32) for n, v in out.items()}


def build(nc: bass.Bass, T, out: bass.AP):
    F32 = mybir.dt.float32
    F32R = mybir.dt.float32r
    I32 = mybir.dt.int32
    ALU = mybir.AluOpType
    ACT = mybir.ActivationFunctionType
    AX = mybir.AxisListType.X
    MULT, ADD, SUB = ALU.mult, ALU.add, ALU.subtract

    ctx = ExitStack()
    with ctx:
        def sb(name, shape, dt=F32):
            return ctx.enter_context(nc.sbuf_tensor(name, shape, dt))

        def sem(name):
            return ctx.enter_context(nc.semaphore(name))

        acc = ctx.enter_context(nc.psum_tensor("acc", [P, 4, HALF], F32))
        pair = [ctx.enter_context(nc.psum_tensor(f"pair{i}", [P, 2, SEQ], F32)) for i in range(2)]
        side = ctx.enter_context(nc.psum_tensor("side", [P, 2, HALF], F32))
        rb_psum = side[:, 0, 0:SEQ]
        cols_psum = side[:, 1, :].rearrange("p (l c) -> p l c", c=P)
        acc_halves = acc[:, :, :].rearrange("p (j t) n -> p j t n", j=2)

        raw_a = [sb(f"raw_a{i}", [P, A_COLS]) for i in range(2)]
        raw_b = [sb(f"raw_b{i}", [P, DM]) for i in range(2)]
        a_hi = [sb(f"a_hi{i}", [P, A_COLS], F32R) for i in range(2)]
        a_lo = [sb(f"a_lo{i}", [P, A_COLS], F32R) for i in range(2)]
        b_hi = [sb(f"b_hi{i}", [P, DM], F32R) for i in range(2)]
        b_lo = [sb(f"b_lo{i}", [P, DM], F32R) for i in range(2)]
        x = sb("x", [P, NT, DM])
        xT = sb("xT", [P, KT, 2, SEQ], F32R)
        hT = [sb(f"hT{i}", [P, 2, SEQ], F32R) for i in range(2)]
        junk = sb("junk", [P, 2 * SEQ])
        rb = sb("rb", [P, SEQ])
        diag = sb("diag", [P, NT, P])
        gu = sb("gu", [P, 2, SEQ])
        sh = sb("sh", [P, 2, SEQ])
        xn = sb("xn", [P, NT, DM])
        cols = sb("cols", [P, 2 * DEPTH, P])
        eye = sb("eye", [P, P])
        ones = sb("ones", [P, P])
        ssq = sb("ssq", [P, 8])
        var = sb("var", [P, 8])
        rstd = sb("rstd", [P, 8])
        minus_half = sb("minus_half", [P, 8])

        a_full = [sem(f"a_full{i}") for i in range(2)]
        b_full = [sem(f"b_full{i}") for i in range(2)]
        a_hi_ready = sem("a_hi_ready")
        a_split = sem("a_split")
        b_hi_ready = sem("b_hi_ready")
        b_split = sem("b_split")
        proj_done = sem("proj_done")
        pair_read = sem("pair_read")
        gate_scaled = sem("gate_scaled")
        silu_done = sem("silu_done")
        h_done = sem("h_done")
        h_hi_ready = sem("h_hi_ready")
        h_split = sem("h_split")
        down_done = sem("down_done")
        acc_bank = sem("acc_bank")
        x_done = sem("x_done")
        ssq_done = sem("ssq_done")
        var_done = sem("var_done")
        rstd_done = sem("rstd_done")
        diag_done = sem("diag_done")
        rb_in_psum = sem("rb_in_psum")
        rb_read = sem("rb_read")
        xT_in_psum = sem("xT_in_psum")
        xT_hi = sem("xT_hi")
        xT_split = sem("xT_split")
        made = sem("made")
        taken = [sem(f"taken{i}") for i in range(4)]
        side_made = sem("side_made")
        side_taken = [sem(f"side_taken{i}") for i in range(2)]
        dve_step = sem("dve_step")
        act_step = sem("act_step")
        consts_in = sem("consts_in")
        rows_in = sem("rows_in")
        rope_in = sem("rope_in")
        rows_T = sem("rows_T")
        cols_done = sem("cols_done")
        more_rows_in = sem("more_rows_in")
        params_in = [sem(f"params_in{i}") for i in range(2 * DEPTH)]
        gain_in = sem("gain_in")
        stored = sem("stored")
        half_set = sem("half_set")
        block1_in = sem("block1_in")
        block2_in = sem("block2_in")
        EVENTS1 = {"gate_tanh": 1, "filt_arg": 3, "filt_hidden": 3, "filt_taps": 2, "filt_abs": 2, "filt_sums": 2,
                   "qkv_squares": 1, "q_gained": 1, "qkv_rstd": 1, "kv_diag": 1, "short_mid": 3, "short_done": 3,
                   "spectrum": 2, "q_roped": 4, "kpe_roped": 1, "neg_max": HEADS, "conv_done": 1, "ln_var": 1,
                   "ln_rstd": 1, "ln_done": 1, "conv_silu": 1, "rope_arg": 2, "rope_done": 2,
                   "y_squares": 2, "y_var": 2, "y_rstd": 2, "y_scaled": 2, "y_in_psum": 2, "y_hi": 2, "y_split": KT}
        EVENTS2 = {"pooled": 1, "bc_f32": 2, "bc_hi": 2, "bc_split": 2, "gate_done": 12, "merged": 4}
        ev = {n: sem(n) for n in (*EVENTS1, *EVENTS2)}

        def nth(L, name, i=0):
            return (L % DEPTH) * (EVENTS1 if name in EVENTS1 else EVENTS2)[name] + i + 1

        def colv(L, name, i=0, parts=P):
            o = (COL1 if L < DEPTH else COL2)[name][0]
            return cols[0:parts, L, o + i:o + i + 1]

        small = {}
        for L in range(2 * DEPTH):
            base = L * len(SMALL1) if L < DEPTH else DEPTH * len(SMALL1) + (L - DEPTH) * len(SMALL2)
            for n, name in enumerate(SMALL1 if L < DEPTH else SMALL2):
                small[L, name] = base + n

        def is_filter(name):
            return name in FILTER_STEPS

        for L in range(DEPTH):
            for n, name in enumerate(FILTER_STEPS):
                small[L, name] = L * len(FILTER_STEPS) + n

        def made_by(name):
            return side_made if is_filter(name) else made

        def place(L, name):
            n, s = (2, side_taken) if is_filter(name) else (4, taken)
            i = small[L, name]
            return (side if is_filter(name) else acc)[:, i % n, :], s[i % n], i // n

        class Obj:
            pass

        def scope1(c):
            def s(name, shape, dt=F32):
                return c.enter_context(nc.sbuf_tensor(name, shape, dt))
            m = Obj()
            m.dft = s("dft", [P, 4, NT, SEQ])
            m.decay = s("decay", [P, NT, CW])
            m.cs = s("cossin", [QKD, 2, SEQ])
            m.rotm = s("rotm", [QKD, QKD])
            m.invf = s("invf", [QKD, 1])
            m.lngb = s("lngb", [P, 2, CW])
            m.wqb = s("wqb", [P, 2, HEADS * QKD])
            m.wkvb = s("wkvb", [P, HEADS * (NOPE + VD)])
            early = s("early", [P, 6088])
            m.w4 = early[0:FILT, 0:1024]
            m.emb = early[0:EMB, 1024:1280]
            m.w1 = early[0:EMB, 1280:1344]
            m.w2 = early[0:FILT, 1344:1408]
            m.w3 = early[0:FILT, 1408:1472]
            m.fcol = early[0:FILT, 1472:1476]
            m.dB = early[:, 1480:1992].rearrange("p (o c) -> p o c", o=2)
            m.farg = early[0:FILT, 1992:2248]
            m.fq = early[0:FILT, 2248:2504]
            m.hdn = early[0:FILT, 2504:2760]
            m.kt = early[:, 2760:3784].rearrange("p (t d c) -> p t d c", t=NT, d=2)
            m.ab = early[:, 3784:4808].rearrange("p (t d c) -> p t d c", t=NT, d=2)
            m.ks = early[:, 4808:5320].rearrange("p (t c) -> p t c", t=NT)
            m.kd = early[:, 5320:5832].rearrange("p (t c) -> p t c", t=NT)
            m.rn = early[:, 5832:6088]
            m.V = early[:, 4808:5832].rearrange("p (t c) -> p t c", t=NT)
            m.qraw = early[0:QKD, 0:512]
            m.qc = early[0:QKD, 1024:1536]
            m.qp = [early[0:QKD, 512:1024], early[0:QKD, 1992:2504]]
            m.kT = [early[0:QKD, 2760:3272], early[0:QKD, 3272:3784]]
            m.PT = [early[:, 3784:4296], early[:, 4296:4808]]
            m.kpe = early[0:QKD, 2504:2760]
            m.kpe2 = early[0:QKD, 5832:6088]
            m.posf = early[0:QKD, 2760:3016]
            m.fq96 = early[0:QKD, 3016:3272]
            m.ra = early[0:QKD, 3272:3784].rearrange("p (a c) -> p a c", a=2)
            m.Pm = [gu, sh]
            m.KA = [s(f"KA{o}", [P, 2, CW]) for o in range(2)]
            m.KB = [s(f"KB{o}", [P, 2, CW]) for o in range(2)]
            m.KN = s("KN", [1, 2, CW])
            m.ca = s("ca", [P, 2, SEQ])
            m.cg = s("cg", [P, 2, SEQ])
            m.u = s("u", [P, 2, SEQ + 2 * PADC])
            m.co = s("co", [P, 2, SEQ])
            m.hq = s("hq", [P, 2, SEQ])
            m.hk = s("hk", [P, 2, SEQ])
            m.kvn = s("kvn", [P, SEQ])
            m.hs = [s(f"hs{i}", [P, 2, SEQ + 2]) for i in range(2)]
            m.sc = [s(f"sc{i}", [P, 2, SEQ]) for i in range(2)]
            m.tv = [s(f"tv{j}", [P, NT, CW]) for j in range(3)]
            m.pos = m.tv[0][0:QKD, 0, :].bitcast(I32)
            m.tmp = m.cg
            m.Yr = m.ca
            m.Yi = s("Yi", [P, 2, CW])
            m.mx = s("mx", [P, 2 * HEADS])
            m.sm = s("sm", [P, 2 * HEADS])
            m.rs = s("rs", [P, 2 * HEADS])
            m.qs = s("qs", [P, 4])
            m.bn = s("bn", [P, NT, 6])
            m.mv = s("mv", [P, NT, 2])
            return m

        def scope2(c):
            def s(name, shape, dt=F32):
                return c.enter_context(nc.sbuf_tensor(name, shape, dt))
            m = Obj()
            m.seq = s("seq", [P, 2, NT, SEQ])
            m.chan = s("chan", [P, 2 * P])
            m.count = s("count", [P, GROUPS, SEQ])
            m.wf = s("wf", [P, GROUPS, SEQ])
            m.wp = s("wp", [P, GROUPS, SEQ])
            m.uF = s("uF", [P, GROUPS, SEQ])
            m.ab = s("ab2", [P, NT, GROUPS, 2 * P])
            m.fT = s("fT", [P, GROUPS, SEQ])
            m.uP = s("uP", [P, GROUPS, SEQ + 2 * PADP])
            m.d1 = s("d1", [P, GROUPS, SEQ + 2 * PADP])
            m.d2 = s("d2", [P, GROUPS, SEQ + 2 * PADP])
            m.c = s("c2", [P, 2, SEQ])
            m.v = s("v2", [P, 2, SEQ])
            m.z = s("z2", [P, GROUPS, SEQ + 2])
            m.cv = s("cv2", [P, 2, SEQ])
            m.bc = s("bc2", [P, GROUPS, 2, SEQ], F32R)
            m.yf = s("yf", [P, KT, SEQ])
            m.yc = m.ab[:, :, :, :].rearrange("p t g c -> p (t g) c")
            m.yp = s("yp", [P, KT, SEQ])
            m.gs = s("gs", [P, 2, SEQ])
            m.th = [s(f"th{i}", [P, 2, SEQ]) for i in range(2)]
            m.cvp = m.yf[:, 0:GROUPS, :]
            m.mg = s("mg", [P, 2, SEQ])
            return m

        c1 = ExitStack()
        with c1:
            m1 = scope1(c1)
        c2 = ExitStack()
        with c2:
            m2 = scope2(c2)

        def ffn_weights(L, which):
            l = L % DEPTH
            if L < DEPTH:
                n = "ffn1" if which == 0 else "ffn2"
                return T[n + "_w_gate"][l], T[n + "_w_up"][l], T[n + "_w_down"][l]
            s = "a" if which == 0 else "b"
            return T[f"w1_{s}_2"][l], T[f"w3_{s}_2"][l], T[f"w2_{s}_2"][l]

        block = ctx.enter_context(nc.Block())

        def a_flat(tile, nt=KT):
            return tile[:, 0:nt * 2 * P].rearrange("p (t n) -> p t n", t=nt)

        def a_gate_up(tile):
            return tile[:, :].rearrange("p (g t n) -> p g t n", g=2, t=KT)

        def two(ap):
            return ap.rearrange("p (t c) -> p t c", t=2)

        @block.sync
        def _(sp):
            k = 0
            b = 0

            def rows(w):
                return w.rearrange("(t p) n -> p t n", p=P)

            def gate_up_unit(wg, wu, at, u, wait):
                sp.wait_ge(a_split, wait)
                dst = a_gate_up(raw_a[u])
                sp.dma_start(dst[:, 0], rows(wg)[:, :, at]).then_inc(a_full[u], 16)
                sp.dma_start(dst[:, 1], rows(wu)[:, :, at]).then_inc(a_full[u], 16)

            def down_unit(wd, at, v, wait):
                sp.wait_ge(b_split, wait)
                sp.dma_start(raw_b[v][:, :], wd[at, :]).then_inc(b_full[v], 16)

            def first_gate_up(L, which, u):
                nonlocal k
                wg, wu, _ = ffn_weights(L, which)
                gate_up_unit(wg, wu, slice(u * P, (u + 1) * P), k % 2, k + 1)
                k += 1

            def first_down(L, which):
                nonlocal b
                down_unit(ffn_weights(L, which)[2], slice(0, P), b % 2, b + 1)
                b += 1

            def ffn(L, which):
                nonlocal k, b
                wg, wu, wd = ffn_weights(L, which)
                with sp.Fori(0, FFU // 2 - 1) as i:
                    for e in range(2):
                        gate_up_unit(wg, wu, bass.ds(i * (2 * P) + (e + 2) * P, P), (k + e) % 2, i * 2 + (k + e + 1))
                        down_unit(wd, bass.ds(i * (2 * P) + (e + 1) * P, P), (b + e) % 2, i * 2 + (b + e + 1))
                k += FFU - 2
                b += FFU - 2

            def last_down(L, which):
                nonlocal b
                down_unit(ffn_weights(L, which)[2], slice((FFU - 1) * P, FFU * P), b % 2, b + 1)
                b += 1

            def panel(w, start, nt=KT):
                nonlocal k
                sp.wait_ge(a_split, k + 1)
                sp.dma_start(a_flat(raw_a[k % 2], nt), rows(w)[:, :, start:start + 2 * P])\
                  .then_inc(a_full[k % 2], 32)
                k += 1

            def row_unit(w, j):
                nonlocal b
                sp.wait_ge(b_split, b + 1)
                sp.dma_start(raw_b[b % 2][:, :], w[j * P:(j + 1) * P, :]).then_inc(b_full[b % 2], 16)
                b += 1

            for t in range(NT):
                sp.dma_start(x[:, t, :], T["x"][0, t * P:(t + 1) * P, :]).then_inc(consts_in, 16)
            sp.dma_start(eye[:, :], T["k_eye"]).then_inc(consts_in, 16)
            first_gate_up(0, 0, 0)
            first_gate_up(0, 0, 1)
            first_down(0, 0)
            for L in range(2 * DEPTH):
                l = L % DEPTH
                ffn(L, 0)
                if L < DEPTH:
                    panel(T["w_in"][l], PANELS1[0][1])
                    last_down(L, 0)
                    panel(T["w_in"][l], PANELS1[1][1])
                    row_unit(T["w_out"][l], Y_TILES[0])
                    for _, start in PANELS1[2:]:
                        panel(T["w_in"][l], start)
                    first_gate_up(L, 1, 0)
                    first_gate_up(L, 1, 1)
                    for j in Y_TILES[1:]:
                        row_unit(T["w_out"][l], j)
                    first_down(L, 1)
                else:
                    w = T["w_in_2"][l]
                    starts = [OFF2[name] + j * 2 * P for name, j in PANELS2]
                    gates = [OFF2["G"] + g * DM + m * 2 * P for m in range(4) for g in range(3)]
                    panel(w, starts[0])
                    last_down(L, 0)
                    panel(w, starts[1])
                    row_unit(T["w_o_2"][l], 0)
                    for start in starts[2:]:
                        panel(w, start)
                    for j in range(4):
                        panel(T["w_conv_out_2"][l], j * 2 * P, nt=4)
                    panel(w, gates[0])
                    panel(w, gates[1])
                    for m in range(4):
                        for g in range(3):
                            n = 3 * m + g + 2
                            if n < len(gates):
                                panel(w, gates[n])
                            else:
                                first_gate_up(L, 1, n - len(gates))
                            if m and g == 0:
                                row_unit(T["w_o_2"][l], 2 * m - 1)
                            if m and g == 2:
                                row_unit(T["w_o_2"][l], 2 * m)
                    row_unit(T["w_o_2"][l], KT - 1)
                    first_down(L, 1)
                ffn(L, 1)
                if L < 2 * DEPTH - 1:
                    first_gate_up(L + 1, 0, 0)
                last_down(L, 1)
                if L < 2 * DEPTH - 1:
                    first_gate_up(L + 1, 0, 1)
                    first_down(L + 1, 0)
                if l == DEPTH - 1:
                    g = T["final_norm"] if L < DEPTH else T["g_final_2"]
                    sp.wait_ge(ssq_done, squares_before(L + 1))
                    sp.dma_start(xn[:, 1, :], g.rearrange("(o n) -> o n", o=1).broadcast_to([P, DM])).then_inc(gain_in, 16)
            for q in range(4):
                t, at = q // 2, slice((q % 2) * HALF, (q % 2 + 1) * HALF)
                sp.wait_ge(x_done, 4 * (3 * 2 * DEPTH + 1) + q + 1)
                sp.dma_start(out[0, t * P:(t + 1) * P, at], x[:, t, at]).then_inc(stored, 16)
            sp.wait_ge(stored, 16 * 4)

        @block.gpsimd
        def _(pool):

            def load_vectors(L):
                l = L % DEPTH
                if L < DEPTH:
                    names = [("ffn1", T["ffn1_norm"][l]), ("mix", T["mix_norm"][l]), ("q", T["mla_q_norm"][l]),
                             ("kv", T["mla_kv_norm"][l]), ("dww", T["conv_dw_w"][l]), ("dwb", T["conv_dw_b"][l]),
                             ("hsw", T["hy_short_w"][l]), ("hsb", T["hy_short_b"][l]), ("out", T["out_norm"][l]),
                             ("ffn2", T["ffn2_norm"][l])]
                    at = COL1
                else:
                    names = [("ffn1", T["g_ffn1_2"][l]), ("mix", T["g_mix_2"][l]), ("wc", T["w_conv_2"][l]),
                             ("ps", T["pool_scale_2"][l]), ("ffn2", T["g_ffn2_2"][l])]
                    at = COL2
                for n, ap in names:
                    o, cnt = at[n]
                    if len(ap.shape) == 1:
                        src = ap.rearrange("(c p) -> c p", p=P)
                    else:
                        src = ap.rearrange("j (c p) -> (j c) p", p=P)
                    if L or n != "ffn1":
                        pool.dma_start(xn[o:o + cnt, L // 2, (L % 2) * P:(L % 2 + 1) * P], src).then_inc(more_rows_in, 16)


            def load_constants():
                m = m1
                def const(dst, src):
                    pool.dma_start(dst, src).then_inc(block1_in, 16)
                const(m.dft[:, :, :, :].rearrange("p a t n -> p (a t) n"), T["k_dft"].rearrange("a (t p) n -> p (a t) n", p=P))
                const(m.decay[:, :, :], T["k_decay"].rearrange("(t p) n -> p t n", p=P))
                const(m.rotm[:, :], T["k_rot"])

            def powers(cols_, waits):
                pool.wait_ge(*waits)
                return pool.tensor_tensor(rstd[:, cols_], var[:, cols_], minus_half[:, cols_], ALU.pow)

            def load1(L):
                m = m1
                l = L % DEPTH
                if l:
                    pool.wait_ge(xT_split, KT * (norms_before(L - 1) + 3))
                s = params_in[L]
                pool.dma_start(m.wqb[:, :, :], T["mla_w_qb"][l].rearrange("(t p) n -> p t n", p=P)).then_inc(s, 16)
                pool.dma_start(m.wkvb[:, :], T["mla_w_kvb"][l]).then_inc(s, 16)
                pool.dma_start(m.w4, T["hy_filt_w4"][l]).then_inc(s, 16)
                pool.dma_start(m.emb, T["k_emb"]).then_inc(s, 16)
                pool.dma_start(m.w1, T["hy_filt_w1"][l]).then_inc(s, 16)
                pool.dma_start(m.w2, T["hy_filt_w2"][l]).then_inc(s, 16)
                pool.dma_start(m.w3, T["hy_filt_w3"][l]).then_inc(s, 16)
                for i, n in enumerate(("hy_filt_b1", "hy_filt_b2", "hy_filt_b3", "hy_filt_freq")):
                    pool.dma_start(m.fcol[:, i:i + 1], T[n][l].rearrange("(p o) -> p o", o=1)).then_inc(s, 16)
                pool.dma_start(m.dB, T["hy_bias_d"][l].rearrange("(q o) c -> q o c", q=1).broadcast_to([P, 2, CW])).then_inc(s, 16)
                for i, n in enumerate(("conv_ln_g", "conv_ln_b")):
                    pool.dma_start(m.lngb[:, i, :], T[n][l].rearrange("(o c) -> o c", o=1).broadcast_to([P, CW])).then_inc(s, 16)

            def load2(L):
                l = L % DEPTH
                m = m2
                s = params_in[L]
                if l:
                    pool.wait_ge(xT_split, KT * (norms_before(L - 1) + 3))
                else:
                    pool.wait_ge(xT_split, KT * (norms_before(L - 1) + 3))
                    pool.dma_start(m.seq[:, :, :, :].rearrange("p a t n -> p (a t) n"),
                                   T["k_seq"].rearrange("a (t p) n -> p (a t) n", p=P)).then_inc(block2_in, 16)
                    pool.dma_start(m.chan[:, :], T["k_chan"]).then_inc(block2_in, 16)
                    pool.dma_start(m.count[:, :, :], T["k_count"]).then_inc(block2_in, 16)
                pool.dma_start(m.wf[:, :, :], T["w_fourier_2"][l].rearrange("g p n -> p g n")).then_inc(s, 16)
                pool.dma_start(m.wp[:, :, :], T["w_pool_2"][l].rearrange("g p n -> p g n")).then_inc(s, 16)

            vk = 0

            def norm(at=slice(0, NT)):
                nonlocal vk
                vk += 1
                powers(at, (var_done, vk)).then_inc(rstd_done, 1)

            pool.wait_ge(half_set, 1)
            for L in range(2 * DEPTH):
                if L == 0:
                    norm()
                    for i in range(2 * DEPTH):
                        load_vectors(i)
                    load_constants()
                if L < DEPTH:
                    load1(L)
                    if L:
                        norm()
                    norm()
                    pool.wait_ge(taken[small[L, "stat"] % 4], small[L, "stat"] // 4 + 1)
                    pool.tensor_tensor(rstd[:, 0:4], var[:, 0:4], minus_half[:, 0:4], ALU.pow).then_inc(ev["qkv_rstd"], 1)
                    pool.wait_ge(ev["ln_var"], nth(L, "ln_var"))
                    pool.tensor_tensor(rstd[:, 6:8], var[:, 6:8], minus_half[:, 6:8], ALU.pow).then_inc(ev["ln_rstd"], 1)
                    for i, at in enumerate((slice(2, 6), slice(0, 2))):
                        pool.wait_ge(ev["y_var"], nth(L, "y_var", i))
                        pool.tensor_tensor(rstd[:, at], var[:, at], minus_half[:, at], ALU.pow).then_inc(ev["y_rstd"], 1)
                else:
                    load2(L)
                    norm()
                    norm()
                norm()
                if L % DEPTH == DEPTH - 1:
                    for t in range(NT):
                        norm(slice(t, t + 1))

        @block.tensor
        def _(pe):
            k = b = h = 0
            n = 0

            pe.wait_ge(half_set, 1)
            pe.matmul(pair[0][0:1, 0, 0:4], ones[:, 0:1], ones[:, 0:4], start=True, stop=True).then_inc(proj_done, CREDIT)
            pe.matmul(pair[1][0:1, 0, 0:4], ones[:, 0:1], ones[:, 0:4], start=True, stop=True).then_inc(down_done, CREDIT)
            u = 0
            nr = 0

            def columns(layers, rows=P):
                for L in layers:
                    r = min(ROWS1 if L < DEPTH else ROWS2, rows)
                    mm = pe.transpose(cols_psum[:, L, 0:r], xn[0:r, L // 2, (L % 2) * P:(L % 2 + 1) * P], eye[0:r, 0:r])
                mm.then_inc(rows_T, 1)

            def transposes(parts):
                for t, j in parts:
                    if u:
                        pe.wait_ge(x_done, 4 * (u - 1) + 2 * t + j + 1)
                    for i in range(4):
                        kt = 4 * j + i
                        mm = pe.transpose(acc[:, 2 * j + t, i * P:(i + 1) * P], x[:, t, kt * P:(kt + 1) * P], eye[:, :])
                    mm.then_inc(xT_in_psum, 1)

            def y_transposes(L, part):
                pe.wait_ge(ev["y_scaled"], nth(L, "y_scaled", part))
                if part:
                    pe.wait_ge(ev["y_split"], nth(L, "y_split", 3))
                for t in range(NT):
                    for i in range(4):
                        kt = Y_TILES[4 * part + i]
                        mm = pe.transpose(side[:, t, i * P:(i + 1) * P], xn[:, t, kt * P:(kt + 1) * P], eye[:, :])
                mm.then_inc(ev["y_in_psum"], 1)

            def spread():
                nonlocal nr
                nr += 1
                pe.wait_ge(diag_done, nr)
                for t in range(NT):
                    mm = pe.matmul(rb_psum[:, t * P:(t + 1) * P], ones[:, :], diag[:, t, :], start=True, stop=True)
                mm.then_inc(rb_in_psum, 1)

            def project(k, par, blocks, src, nt, first):
                pe.wait_ge(a_hi_ready, k + 1)
                pe.wait_ge(a_split, k + 1 + CREDIT)
                pe.wait_ge(pair_read, k + 1)
                for e in range(2):
                    for i, kt in enumerate(X_TILES if nt == KT else range(nt)):
                        if first and e == 0:
                            pe.wait_ge(xT_split, KT * (n - 1) + i + 1)
                        hi, lo = blocks(a_hi[par], e, kt), blocks(a_lo[par], e, kt)
                        pe.matmul(pair[par][:, e, :], hi, src[:, kt, 0, :], start=(i == 0), stop=False)
                        pe.matmul(pair[par][:, e, :], hi, src[:, kt, 1, :], start=False, stop=False)
                        mm = pe.matmul(pair[par][:, e, :], lo, src[:, kt, 0, :], start=False, stop=(i == nt - 1))
                mm.then_inc(proj_done, 1)

            def gate_up(tile, e, kt):
                return a_gate_up(tile)[:, e, kt, :]

            def panel_block(tile, e, kt):
                return a_flat(tile)[:, kt, e * P:(e + 1) * P]

            def kv_block(tile, e, kt):
                return a_flat(tile)[:, kt, e * NOPE:e * NOPE + P]

            def conv_block(tile, e, kt):
                return a_flat(tile, 4)[:, kt, e * P:(e + 1) * P]

            def down(b, par, parts, first):
                pe.wait_ge(b_hi_ready, b + 1)
                pe.wait_ge(b_split, b + 1 + CREDIT)
                for t in range(NT):
                    hi, lo = parts(t)
                    for j in range(2):
                        pe.matmul(acc[:, 2 * j + t, :], hi, b_hi[par][:, j * HALF:(j + 1) * HALF], start=first, stop=False)
                    for j in range(2):
                        pe.matmul(acc[:, 2 * j + t, :], hi, b_lo[par][:, j * HALF:(j + 1) * HALF], start=False, stop=False)
                    for j in range(2):
                        mm = pe.matmul(acc[:, 2 * j + t, :], lo, b_hi[par][:, j * HALF:(j + 1) * HALF], start=False, stop=False)
                mm.then_inc(down_done, 1)

            def last_down(b, par, parts, to_transpose=True):
                nonlocal u
                pe.wait_ge(b_hi_ready, b + 1)
                pe.wait_ge(b_split, b + 1 + CREDIT)
                u += 1
                for t in range(NT):
                    hi, lo = parts(t)
                    for j in range(2):
                        at = slice(j * HALF, (j + 1) * HALF)
                        if to_transpose and (t, j) == (NT - 1, 1):
                            transposes([(0, 0), (0, 1)])
                        pe.matmul(acc[:, 2 * j + t, :], hi, b_hi[par][:, at], start=False, stop=False)
                        pe.matmul(acc[:, 2 * j + t, :], hi, b_lo[par][:, at], start=False, stop=False)
                        mm = pe.matmul(acc[:, 2 * j + t, :], lo, b_hi[par][:, at], start=False, stop=True)
                        mm.then_inc(down_done if (t, j) == (NT - 1, 1) else acc_bank, 1)

            def from_h(h, par):
                pe.wait_ge(h_hi_ready, h + 1)
                pe.wait_ge(h_split, h + 1)
                return lambda t: (hT[par][:, 0, t * P:(t + 1) * P], hT[par][:, 1, t * P:(t + 1) * P])

            def take(L, name):
                o, used, before = place(L, name)
                if before:
                    pe.wait_ge(used, before)
                return o

            def got(L, name):
                _, used, before = place(L, name)
                pe.wait_ge(used, before + 1)

            def transform(o, mat, src):
                for ft in range(2):
                    for t in range(NT):
                        mm = pe.matmul(o[:, ft * CW:(ft + 1) * CW], mat[:, t, ft * P:(ft + 1) * P], src[:, t, :],
                                       start=(t == 0), stop=(t == NT - 1))
                mm.then_inc(made if src is m1.tv[0] else side_made, 1)

            def filter_items(L, items):
                m = m1
                cf, sf = m.dft[:, 0], m.dft[:, 1]
                for it in items:
                    kind = it.rstrip("0123456789")
                    i = int(it[-1]) if kind != it else None
                    if kind == "f":
                        o = take(L, it)
                        if i == 0:
                            pe.matmul(o[0:FILT, 0:SEQ], m.w1, m.emb, start=True, stop=True).then_inc(side_made, 1)
                        else:
                            pe.wait_ge(ev["filt_hidden"], nth(L, "filt_hidden", i - 1))
                            pe.matmul(o[0:FILT, 0:SEQ], (m.w2, m.w3)[i - 1], m.hdn, start=True, stop=True).then_inc(side_made, 1)
                    elif kind == "h":
                        pe.wait_ge(ev["filt_hidden"], nth(L, "filt_hidden", 2))
                        for t in range(NT):
                            o = take(L, f"{it}t{t}")
                            pe.matmul(o, m.hdn[:, t * P:(t + 1) * P], m.w4[:, i * 2 * CW:(i + 1) * 2 * CW],
                                      start=True, stop=True).then_inc(side_made, 1)
                    elif kind == "n":
                        o = take(L, it)
                        pe.wait_ge(ev["filt_abs"], nth(L, "filt_abs", i))
                        pe.wait_ge(ev["filt_sums"], nth(L, "filt_sums", i))
                        for j in range(4):
                            pe.matmul(o[:, 0:CW], ones[:, :], m.ab[:, j // 2, j % 2, :], start=(j == 0), stop=(j == 3))
                        for t in range(NT):
                            mm = pe.matmul(o[0:1, CW:2 * CW], sf[:, t, 0:1], m.ks[:, t, :], start=(t == 0), stop=(t == NT - 1))
                        mm.then_inc(side_made, 1)
                    elif kind in ("A", "B"):
                        o = take(L, it)
                        transform(o, cf if kind == "A" else sf, m.ks if kind == "A" else m.kd)

            def ffn(to_transpose=True, filters=None):
                nonlocal k, b, h, n
                ends = 0 if filters is None else FILTER_UNITS
                n += 1
                transposes([(1, 0), (1, 1)])
                project(k, k % 2, gate_up, xT, KT, True)
                spread()
                project(k + 1, (k + 1) % 2, gate_up, xT, KT, False)
                down(b, b % 2, from_h(h, h % 2), True)
                with pe.Fori(0, (FFU - 2 - ends) // 2) as i:
                    for e in range(2):
                        project(i * 2 + (k + 2 + e), (k + e) % 2, gate_up, xT, KT, False)
                        down(i * 2 + (b + 1 + e), (b + 1 + e) % 2, from_h(i * 2 + (h + 1 + e), (h + 1 + e) % 2), False)
                if ends:
                    pe.wait_ge(params_in[filters], 16 * N_PARAM1)
                    if filters == 0:
                        pe.wait_ge(block1_in, 16 * N_BLOCK1)
                for j in range(FFU - 1 - ends, FFU - 1):
                    project(k + j + 1, (k + j + 1) % 2, gate_up, xT, KT, False)
                    down(b + j, (b + j) % 2, from_h(h + j, (h + j) % 2), False)
                    filter_items(filters, FILTER_ITEMS[j - (FFU - 1 - ends)])
                last_down(b + FFU - 1, (b + FFU - 1) % 2, from_h(h + FFU - 1, (h + FFU - 1) % 2), to_transpose)
                k += FFU
                b += FFU
                h += FFU

            def mixer1(L):
                nonlocal k, b, n
                m = m1
                cf, sf, ci, si = (m.dft[:, i] for i in range(4))
                n += 1
                transposes([(1, 0), (1, 1)])
                ip = 0
                for it in ORDER1["pe"]:
                    i = int(it[-1]) if it[-1].isdigit() else None
                    kind = it.rstrip("0123456789")
                    if it == "A":
                        project(k, k % 2, kv_block if PANELS1[ip][0] == "kv" else panel_block, xT, KT, ip == 0)
                        ip += 1
                        if ip == 1:
                            spread()
                        k += 1
                    elif it == "stat":
                        o = take(L, it)
                        pe.wait_ge(ev["qkv_squares"], nth(L, "qkv_squares"))
                        for t in range(NT):
                            for e in range(2):
                                pe.matmul(o[:, t:t + 1], gu[:, e, t * P:(t + 1) * P], ones[:, 0:1], start=(e == 0), stop=(e == 1))
                        for t in range(NT):
                            mm = pe.matmul(o[:, NT + t:NT + t + 1], sh[:, 0, t * P:(t + 1) * P], ones[:, 0:1], start=True, stop=True)
                        mm.then_inc(made, 1)
                    elif it == "kb":
                        o = take(L, it)
                        pe.wait_ge(ev["kv_diag"], nth(L, "kv_diag"))
                        for t in range(NT):
                            mm = pe.matmul(o[:, t * P:(t + 1) * P], ones[:, :], m.kvn[:, t * P:(t + 1) * P], start=True, stop=True)
                        mm.then_inc(made, 1)
                    elif kind == "val":
                        got(L, "kb")
                        wv = m.wkvb[:, :].rearrange("p (h c) -> p h c", h=HEADS)[:, :, NOPE:NOPE + VD]
                        o = take(L, it)
                        pe.matmul(o.rearrange("p (h c) -> p h c", h=HEADS), m.kvn[:, i * P:(i + 1) * P], wv,
                                  start=True, stop=True).then_inc(made, 1)
                    elif it == "yT":
                        y_transposes(L, 0)
                    elif kind == "short":
                        o = take(L, it)
                        pe.wait_ge(ev["short_done"], nth(L, "short_done", i))
                        for t in range(NT):
                            for e in range(2):
                                mm = pe.transpose(o[:, t * CW + e * P:t * CW + (e + 1) * P], m.sc[i % 2][:, e, t * P:(t + 1) * P], eye[:, :])
                        mm.then_inc(made, 1)
                    elif kind in ("re", "im"):
                        got(L, "short0" if i == 0 else "inv0")
                        o = take(L, it)
                        transform(o, cf if kind == "re" else sf, m.tv[0])
                    elif kind == "inv":
                        o = take(L, it)
                        pe.wait_ge(ev["spectrum"], nth(L, "spectrum", i))
                        for t in range(NT):
                            for ft in range(2):
                                pe.matmul(o[:, t * CW:(t + 1) * CW], ci[:, ft, t * P:(t + 1) * P], m.Yr[:, ft, :],
                                          start=(ft == 0), stop=False)
                                mm = pe.matmul(o[:, t * CW:(t + 1) * CW], si[:, ft, t * P:(t + 1) * P], m.Yi[:, ft, :],
                                               start=False, stop=(ft == 1))
                        mm.then_inc(made, 1)
                    elif kind == "q":
                        o = take(L, it)
                        pe.wait_ge(ev["q_gained"], nth(L, "q_gained"))
                        for e in range(2):
                            c = (2 * i + e) * QKD
                            for j in range(2):
                                mm = pe.matmul(o[0:QKD, e * SEQ:(e + 1) * SEQ], m.wqb[:, j, c:c + QKD], m.hq[:, j, :],
                                               start=(j == 0), stop=(j == 1))
                        mm.then_inc(made, 1)
                    elif kind == "rot":
                        o = take(L, it)
                        got(L, f"q{i}")
                        pe.matmul(o[0:QKD, :], m.rotm[:, :], m.qraw, start=True, stop=True).then_inc(made, 1)
                    elif it == "kpe":
                        o = take(L, it)
                        pe.matmul(o[0:QKD, 0:SEQ], m.rotm[NOPE:QKD, :], m.hk[NOPE:QKD, 1, :], start=True, stop=True).then_inc(made, 1)
                    elif kind == "k":
                        o = take(L, it)
                        got(L, "kb")
                        for e in range(2):
                            c = (2 * i + e) * (NOPE + VD)
                            mm = pe.matmul(o[0:NOPE, e * SEQ:(e + 1) * SEQ], m.wkvb[:, c:c + NOPE], m.kvn[:, :], start=True, stop=True)
                        mm.then_inc(made, 1)
                    elif kind == "s":
                        o = take(L, it)
                        p2, e = i // 2, i % 2
                        pe.wait_ge(ev["q_roped"], nth(L, "q_roped", p2))
                        pe.wait_ge(ev["kpe_roped"], nth(L, "kpe_roped"))
                        got(L, f"k{p2}")
                        for t in range(NT):
                            mm = pe.matmul(o[:, t * SEQ:(t + 1) * SEQ], m.qp[p2 % 2][:, e * SEQ + t * P:e * SEQ + (t + 1) * P],
                                           m.kT[p2 % 2][:, e * SEQ:(e + 1) * SEQ], start=True, stop=True)
                        mm.then_inc(made, 1)
                    elif kind == "p":
                        o = take(L, it)
                        got(L, f"s{i}")
                        for t in range(NT):
                            for kk in range(NT):
                                mm = pe.transpose(o[:, kk * SEQ + t * P:kk * SEQ + (t + 1) * P],
                                                  m.Pm[i % 2][:, t, kk * P:(kk + 1) * P], eye[:, :])
                        mm.then_inc(made, 1)
                    elif kind == "o":
                        o = take(L, it)
                        got(L, f"p{i}")
                        got(L, "val1")
                        for t in range(NT):
                            for kk in range(NT):
                                mm = pe.matmul(o[:, t * VD:(t + 1) * VD], m.PT[i % 2][:, kk * SEQ + t * P:kk * SEQ + (t + 1) * P],
                                               m.V[:, kk, i * VD:(i + 1) * VD], start=(kk == 0), stop=(kk == NT - 1))
                        mm.then_inc(made, 1)
                    elif it == "conv_out":
                        o = take(L, it)
                        pe.wait_ge(ev["conv_done"], nth(L, "conv_done"))
                        for t in range(NT):
                            for e in range(2):
                                mm = pe.transpose(o[:, t * CW + e * P:t * CW + (e + 1) * P], m.co[:, e, t * P:(t + 1) * P], eye[:, :])
                        mm.then_inc(made, 1)
                for name in SMALL1[-4:]:
                    got(L, name)
                for j in range(KT):
                    if j == 2:
                        y_transposes(L, 1)
                    pe.wait_ge(ev["y_split"], nth(L, "y_split", j))
                    kt = Y_TILES[j]
                    y_parts = lambda t, kt=kt: (xT[:, kt, 0, t * P:(t + 1) * P], xT[:, kt, 1, t * P:(t + 1) * P])
                    if j < KT - 1:
                        down(b, b % 2, y_parts, j == 0)
                    else:
                        last_down(b, b % 2, y_parts)
                    b += 1

            def mixer2(L):
                nonlocal k, b, h, n
                m = m2
                n += 1
                transposes([(1, 0), (1, 1)])
                first_k = k
                ia = gm = 0
                for it in ORDER2["pe"] + ["G"] * 4:
                    i = int(it[-1]) if it[-1].isdigit() else None
                    if it == "A":
                        project(k, k % 2, panel_block, xT, KT, ia == 0)
                        ia += 1
                        k += 1
                        if ia == 1:
                            spread()
                            pe.wait_ge(params_in[L], 16 * N_PARAM2)
                            pe.wait_ge(block2_in, 16 * N_BLOCK2)
                    elif it[0] == "c":
                        o = take(L, it)
                        pe.wait_ge(pair_read, first_k + i // 2 + 1 + CREDIT)
                        for t in range(NT):
                            mm = pe.matmul(o[:, t * SEQ:(t + 1) * SEQ], m.uF[:, i, t * P:(t + 1) * P], m.chan[:, :], start=True, stop=True)
                        mm.then_inc(made, 1)
                    elif it[0] == "t":
                        o = take(L, it)
                        got(L, f"c{2 * i + 1}")
                        got(L, f"c{2 * i}")
                        for e in range(2):
                            g = 2 * i + e
                            for t in range(NT):
                                for a in range(2):
                                    mm = pe.matmul(o[:, e * SEQ:(e + 1) * SEQ], m.ab[:, t, g, a * P:(a + 1) * P], m.seq[:, a, t, :],
                                                   start=(t == 0 and a == 0), stop=(t == NT - 1 and a == 1))
                        mm.then_inc(made, 1)
                    elif it[:2] in ("yf", "yp"):
                        o = take(L, it)
                        if it[1] == "f":
                            got(L, f"t{i // 2}")
                            w, src = m.wf, m.fT[:, i, :]
                        else:
                            pe.wait_ge(ev["pooled"], nth(L, "pooled"))
                            w, src = m.wp, m.d1[:, i, 0:SEQ]
                        for e in range(2):
                            mm = pe.matmul(o[:, e * SEQ:(e + 1) * SEQ], w[:, i, e * P:(e + 1) * P], src, start=True, stop=True)
                        mm.then_inc(made, 1)
                    elif it[0] == "Y":
                        if i == 0:
                            pe.wait_ge(ev["bc_split"], nth(L, "bc_split", 1))
                        project(k, k % 2, conv_block, m.bc, 4, False)
                        k += 1
                    elif it == "G":
                        for g in range(3):
                            project(k, k % 2, panel_block, xT, KT, False)
                            k += 1
                            if g == 0 and gm == 0:
                                for name in SMALL2[-4:]:
                                    got(L, name)
                            if gm > 0 and g == (2 if gm == 3 else 1):
                                for e in range(2):
                                    down(b, b % 2, from_h(h, h % 2), gm == 1 and e == 0)
                                    b += 1
                                    h += 1
                        gm += 1
                down(b, b % 2, from_h(h, h % 2), False)
                last_down(b + 1, (b + 1) % 2, from_h(h + 1, (h + 1) % 2))
                b += 2
                h += 2

            pe.wait_ge(consts_in, 16 * 3)
            transposes([(0, 0), (0, 1)])
            pe.wait_ge(rows_in, 16)
            columns([0], KT)
            for L in range(2 * DEPTH):
                ffn(filters=L if L < DEPTH else None)
                if L < DEPTH:
                    for name in FILTER_STEPS[-2:]:
                        got(L, name)
                if L == 0:
                    pe.wait_ge(more_rows_in, 16 * (10 * DEPTH + 5 * DEPTH - 1))
                    columns(range(2 * DEPTH))
                if L < DEPTH:
                    mixer1(L)
                else:
                    mixer2(L)
                block_end = L % DEPTH == DEPTH - 1
                ffn(not block_end)
                if L == DEPTH - 1:
                    u += 1
                    transposes([(0, 0), (0, 1)])

        @block.scalar
        def _(act):
            k = b = h = f = n = xk = 0
            steps = 0

            act.dma_start(m1.pos, T["positions"].broadcast_to([QKD, SEQ])).then_inc(rope_in, 16)
            act.dma_start(m1.invf[:, :], T["k_invf"]).then_inc(rope_in, 16)
            act.dma_start(xn[0:KT, 0, 0:P], T["ffn1_norm"][0].rearrange("(c p) -> c p", p=P)).then_inc(rows_in, 16)

            def link(ins):
                nonlocal steps
                steps += 1
                ins.then_inc(act_step, 1)
                act.wait_ge(act_step, steps)

            def split_a(k, par, use, width=A_COLS):
                act.wait_ge(a_full[par], (use + 1) * 32)
                act.wait_ge(proj_done, k + 1)
                act.activation(a_hi[par][:, 0:width], raw_a[par][:, 0:width], ACT.Copy).then_inc(a_hi_ready, 1)

            def split_b(b, par, use):
                act.wait_ge(b_full[par], (use + 1) * 16)
                act.wait_ge(down_done, b + 1)
                act.activation(b_hi[par][:, :], raw_b[par][:, :], ACT.Copy).then_inc(b_hi_ready, 1)

            def squares(where):
                for t in range(NT):
                    act.activation(where(t), x[:, t, :], ACT.Square, accum_out=ssq[:, t:t + 1]).then_inc(ssq_done, 1)

            def norm_to_xT(L, gain):
                nonlocal n
                for turn in range(KT // 2):
                    if turn < 2:
                        act.wait_ge(xT_in_psum, 4 * n + 2 + turn + 1)
                    else:
                        act.wait_ge(xT_split, KT * n + 2 * (turn - 1))
                    for kt in X_TILES[2 * turn:2 * turn + 2]:
                        ins = act.activation(two(xT[:, kt, 0, :]), acc_halves[:, kt // 4, :, kt % 4 * P:(kt % 4 + 1) * P], ACT.Copy,
                                             scale=colv(L, gain, kt))
                    ins.then_inc(xT_hi, 1)
                n += 1

            def norm(L, gain):
                norm_to_xT(L, gain)
                squares(lambda t: xn[:, t, :])

            def read(L, name):
                act.wait_ge(made_by(name), small[L, name] + 1)
                return place(L, name)[0]

            def free(L, name):
                return place(L, name)[1]

            def filter_items(L, items):
                m = m1
                for it in items:
                    kind = it.rstrip("0123456789")
                    i = int(it[-1]) if kind != it else None
                    if kind == "f":
                        act.wait_ge(ev["filt_arg"], nth(L, "filt_arg", i))
                        act.activation(m.hdn, m.farg, ACT.Sin).then_inc(ev["filt_hidden"], 1)
                    elif kind == "h":
                        act.wait_ge(ev["filt_taps"], nth(L, "filt_taps", i))
                        act.activation(m.ab, m.kt, ACT.Abs).then_inc(ev["filt_abs"], 1)

            def ffn_step(k, b, m, h, kh, ka, ua, kb_, ub, more_a=True, more_b=True, filters=None, items=()):
                act.wait_ge(gate_scaled, m + 1)
                act.activation(sh[:, 0, :], gu[:, 0, :], ACT.Silu).then_inc(silu_done, 1)
                act.wait_ge(h_done, m + 1)
                act.activation(hT[kh][:, 0, :], sh[:, 1, :], ACT.Copy).then_inc(h_hi_ready, 1)
                if more_a:
                    split_a(k + 2, ka, ua)
                if more_b:
                    split_b(b + 1, kb_, ub)
                filter_items(filters, items)

            def ffn(L, gain, last, first=False):
                nonlocal k, b, h, f, xk
                if not first:
                    norm(L, gain)
                ends = FILTER_UNITS if L < DEPTH and gain == "ffn1" else 2 if last else 0
                with act.Fori(0, (FFU - ends) // 2) as i:
                    for e in range(2):
                        ffn_step(i * 2 + (k + e), i * 2 + (b + e), i * 2 + (f + e), i * 2 + (h + e), (h + e) % 2,
                                 (k + e) % 2, i + (k + e + 2) // 2, (b + e + 1) % 2, i + (b + e + 1) // 2)
                for j in range(FFU - ends, FFU):
                    ffn_step(k + j, b + j, f + j, h + j, (h + j) % 2, (k + j) % 2, (k + j + 2) // 2, (b + j + 1) % 2, (b + j + 1) // 2,
                             more_a=not last, more_b=not last or j < FFU - 1,
                             filters=L, items=() if last else FILTER_ITEMS[j - (FFU - ends)])
                k += FFU
                b += FFU
                h += FFU
                f += FFU
                xk += 1

            def panel(width=A_COLS):
                nonlocal k
                split_a(k + 2, k % 2, (k + 2) // 2, width)
                k += 1

            def row_split():
                nonlocal b
                split_b(b + 1, (b + 1) % 2, (b + 1) // 2)
                b += 1

            def mixer1(L):
                nonlocal k, b, xk, h
                m = m1
                norm(L, "mix")
                pk = {name: k + i for i, (name, _) in enumerate(PANELS1)}
                rows_done = 0

                def y_high(part):
                    act.wait_ge(ev["y_in_psum"], nth(L, "y_in_psum", part))
                    act.wait_ge(proj_done, pk["x2"] + 1 + CREDIT)
                    for i in range(4):
                        kt = Y_TILES[4 * part + i]
                        ins = act.activation(two(xT[:, kt, 0, :]), side[:, :, i * P:(i + 1) * P], ACT.Copy, scale=colv(L, "out", kt))
                    ins.then_inc(ev["y_hi"], 1)

                def y_squares(segments):
                    for s, lo, hi in segments:
                        for t in range(NT):
                            ins = act.activation(junk[:, 0:hi - lo], xn[:, t, lo:hi], ACT.Square, accum_out=ssq[:, 2 * s + t:2 * s + t + 1])
                            if (s, t) != (segments[-1][0], NT - 1):
                                link(ins)
                    ins.then_inc(ev["y_squares"], 1)

                for it in ORDER1["act"]:
                    i = int(it[-1]) if it[-1].isdigit() else None
                    kind = it.rstrip("0123456789")
                    if it == "A":
                        panel()
                    elif it == "row":
                        row_split()
                        rows_done += 1
                    elif it == "glu":
                        act.wait_ge(pair_read, pk["cg"] + 1 + CREDIT)
                        act.activation(m.cg[:, :, :], m.cg[:, :, :], ACT.Tanh, scale=0.5).then_inc(ev["gate_tanh"], 1)
                    elif it == "qkv_sq":
                        act.wait_ge(pair_read, pk["kv"] + 1 + CREDIT)
                        act.activation(gu[:, :, :], m.hq[:, :, :], ACT.Square)
                        act.activation(sh[:, 0, :], m.hk[:, 0, :], ACT.Square).then_inc(ev["qkv_squares"], 1)
                        act.wait_ge(ev["qkv_squares"], nth(L, "qkv_squares"))
                        for e in range(2):
                            ins = act.activation(m.hq[:, e, :], m.hq[:, e, :], ACT.Copy, scale=colv(L, "q", e))
                        ins.then_inc(ev["q_gained"], 1)
                    elif kind == "val":
                        o = read(L, it)
                        act.activation(m.V[:, i, :], o, ACT.Copy).then_inc(free(L, it), 1)
                    elif kind == "short":
                        act.wait_ge(pair_read, pk[("v", "x1", "x2")[i]] + 1 + CREDIT)
                        for e in range(2):
                            ins = act.activation(m.sc[i % 2][:, e, :], m.hs[i % 2][:, e, 1:SEQ + 1], ACT.Identity,
                                                 scale=colv(L, "hsw", 6 + 2 * i + e), bias=colv(L, "hsb", 2 * i + e))
                        ins.then_inc(ev["short_mid"], 1)
                    elif kind == "copy":
                        o = read(L, f"short{i}")
                        act.activation(m.tv[i][:, :, :], two(o), ACT.Copy).then_inc(free(L, f"short{i}"), 1)
                    elif kind == "q":
                        o = read(L, it)
                        if i:
                            act.wait_ge(ev["q_roped"], nth(L, "q_roped", i - 1))
                        act.activation(m.qraw, o[0:QKD, :], ACT.Copy).then_inc(free(L, it), 1)
                    elif kind == "k" and i is not None:
                        o = read(L, it)
                        act.activation(m.kT[i % 2][0:NOPE, :], o[0:NOPE, :], ACT.Copy).then_inc(free(L, it), 1)
                    elif kind == "s":
                        act.wait_ge(ev["neg_max"], nth(L, "neg_max", i))
                        o = read(L, it)
                        for t in range(NT):
                            ins = act.activation(m.Pm[i % 2][:, t, :], o[:, t * SEQ:(t + 1) * SEQ], ACT.Exp, scale=m.qs[:, t:t + 1],
                                                 bias=m.mx[:, 2 * i + t:2 * i + t + 1], accum_out=m.sm[:, 2 * i + t:2 * i + t + 1])
                        ins.then_inc(free(L, it), 1)
                    elif kind == "p":
                        o = read(L, it)
                        if i >= 2:
                            act.wait_ge(made, small[L, f"o{i - 2}"] + 1)
                        act.activation(m.PT[i % 2], o, ACT.Copy).then_inc(free(L, it), 1)
                    elif it == "conv_out":
                        act.wait_ge(ev["ln_done"], nth(L, "ln_done"))
                        y = xn[:, :, 2 * CW:3 * CW]
                        act.activation(y, y, ACT.Silu).then_inc(ev["conv_silu"], 1)
                    elif it == "ysq":
                        act.wait_ge(ev["conv_silu"], nth(L, "conv_silu"))
                        act.wait_ge(taken[small[L, "inv1"] % 4], small[L, "inv1"] // 4 + 1)
                        y_squares([(1, 512, 768), (2, 768, 1024)])
                    elif it == "yhi":
                        y_high(0)
                    elif it == "msq":
                        act.wait_ge(taken[small[L, "o7"] % 4], small[L, "o7"] // 4 + 1)
                        y_squares([(0, 0, 512)])
                for j in range(rows_done, KT):
                    if j == rows_done + 2:
                        y_high(1)
                    row_split()
                xk += 1

            def mixer2(L):
                nonlocal k, b, xk, h
                m = m2
                norm(L, "mix")
                gm = ip = 0

                def merged_high(gm):
                    nonlocal h
                    act.wait_ge(ev["merged"], nth(L, "merged", gm))
                    for e in range(2):
                        act.activation(hT[h % 2][:, 0, :], m.mg[:, e, :], ACT.Copy).then_inc(h_hi_ready, 1)
                        h += 1
                        if e == 0:
                            row_split()
                for it in ORDER2["act"] + ["G"] * 4:
                    i = int(it[-1]) if it[-1].isdigit() else None
                    if it == "A" or it[0] == "Y":
                        panel(conv_width(ip))
                        ip += 1
                    elif it[0] == "c":
                        o = read(L, it)
                        act.activation(m.ab[:, :, i, :], two(o), ACT.Copy).then_inc(free(L, it), 1)
                    elif it[0] == "t":
                        o = read(L, it)
                        act.activation(m.fT[:, 2 * i:2 * i + 2, :], two(o), ACT.Copy).then_inc(free(L, it), 1)
                    elif it[:2] == "yf":
                        o = read(L, it)
                        act.activation(m.yf[:, 2 * i:2 * i + 2, :], two(o), ACT.Copy).then_inc(free(L, it), 1)
                    elif it[:2] == "yp":
                        o = read(L, it)
                        for e in range(2):
                            ins = act.activation(m.yp[:, 2 * i + e, :], o[:, e * SEQ:(e + 1) * SEQ], ACT.Copy, scale=colv(L, "ps", 2 * i + e))
                        ins.then_inc(free(L, it), 1)
                    elif it[:2] == "bc":
                        act.wait_ge(ev["bc_f32"], nth(L, "bc_f32", i))
                        act.activation(m.bc[:, 2 * i:2 * i + 2, 0, :], m.gs[:, :, :], ACT.Copy).then_inc(ev["bc_hi"], 1)
                    elif it == "G":
                        for g in range(3):
                            if (gm, g) != (3, 2):
                                panel()
                            else:
                                k += 1
                            act.wait_ge(pair_read, k + CREDIT)
                            act.activation(m.th[(3 * gm + g) % 2][:, :, :], m.gs[:, :, :], ACT.Tanh, scale=0.5).then_inc(ev["gate_done"], 1)
                            if gm and g == 0:
                                merged_high(gm - 1)
                            if gm and g == 2:
                                row_split()
                        gm += 1
                merged_high(gm - 1)
                split_a(k + 1, (k + 1) % 2, (k + 1) // 2)
                row_split()
                xk += 1

            def final_norm():
                nonlocal xk
                for t in range(NT):
                    act.wait_ge(x_done, 4 * (xk - 1) + 2 * t + 2)
                    ins = act.activation(xn[:, 0, :], x[:, t, :], ACT.Square, accum_out=ssq[:, t:t + 1])
                    ins.then_inc(ssq_done, 1)
                    if t == 0:
                        act.wait_ge(ssq_done, squares_before(L + 1) + 1)
                xk += 1

            for i in range(2):
                act.wait_ge(ev["rope_arg"], i + 1)
                act.activation(m1.cs[:, i, :], m1.ra[:, i, :], ACT.Sin).then_inc(ev["rope_done"], 1)
            act.wait_ge(cols_done, 1)
            norm_to_xT(0, "ffn1")
            split_a(0, 0, 0)
            squares(lambda t: b_lo[t][:, :])
            split_a(1, 1, 0)
            split_b(0, 0, 0)
            for L in range(2 * DEPTH):
                ffn(L, "ffn1", False, first=L == 0)
                if L == 0:
                    act.wait_ge(cols_done, 2)
                if L < DEPTH:
                    mixer1(L)
                else:
                    mixer2(L)
                ffn(L, "ffn2", L == 2 * DEPTH - 1)
                if L % DEPTH == DEPTH - 1:
                    final_norm()

        @block.vector
        def _(dve):
            k = b = h = f = n = sq = vk = nr = 0
            steps = 0

            def step(ins):
                nonlocal steps
                steps += 1
                ins.then_inc(dve_step, 1)
                return steps

            def link(ins):
                dve.wait_ge(dve_step, step(ins))

            def split_a(k, par, width=A_COLS):
                dve.wait_ge(a_hi_ready, k + 1)
                dve.tensor_tensor(a_lo[par][:, 0:width], raw_a[par][:, 0:width], a_hi[par][:, 0:width], SUB).then_inc(a_split, 1)

            def split_b(b, par):
                dve.wait_ge(b_hi_ready, b + 1)
                dve.tensor_tensor(b_lo[par][:, :], raw_b[par][:, :], b_hi[par][:, :], SUB).then_inc(b_split, 1)

            def scaled(k, par, dst):
                dve.wait_ge(proj_done, k + 1 + CREDIT)
                dve.tensor_tensor(dst, pair[par][:, :, :], bcast(rb[:, :], 2), MULT).then_inc(pair_read, 1)

            def variance(cols_, width):
                return dve.tensor_scalar(var[:, cols_], ssq[:, cols_], 1.0 / width, EPS, MULT, ADD)

            def xT_low(L, gain):
                nonlocal n
                for i, kt in enumerate(X_TILES):
                    if i % 2 == 0:
                        dve.wait_ge(xT_hi, 4 * n + i // 2 + 1)
                    dve.scalar_tensor_tensor(two(xT[:, kt, 1, :]), acc_halves[:, kt // 4, :, kt % 4 * P:(kt % 4 + 1) * P],
                                             colv(L, gain, kt), two(xT[:, kt, 0, :].bitcast(F32)), MULT, SUB).then_inc(xT_split, 1)
                n += 1

            def norm(L, gain, next_a=False, next_b=True, first=False):
                nonlocal sq, vk, nr
                xT_low(L, gain)
                if first:
                    split_a(0, 0)
                if next_a:
                    split_a(k + 1, (k + 1) % 2)
                sq += NT
                vk += 1
                dve.wait_ge(ssq_done, sq)
                variance(slice(0, 2), DM).then_inc(var_done, 1)
                if next_b:
                    split_b(b, b % 2)
                dve.wait_ge(rstd_done, vk)
                for t in range(NT):
                    ins = dve.tensor_scalar(diag[:, t, :], eye[:, :], rstd[:, t:t + 1], None, MULT)
                ins.then_inc(diag_done, 1)
                nr += 1
                dve.wait_ge(rb_in_psum, nr)
                dve.tensor_copy(rb[:, :], rb_psum).then_inc(rb_read, 1)
                dve.wait_ge(rb_read, nr)

            def update_x(scale, b):
                nonlocal phases
                phases += 1
                for q in range(4):
                    if q < 3:
                        dve.wait_ge(acc_bank, 3 * (phases - 1) + q + 1)
                    else:
                        dve.wait_ge(down_done, b + 1 + CREDIT)
                    xq = x[:, q // 2, (q % 2) * HALF:(q % 2 + 1) * HALF]
                    dve.scalar_tensor_tensor(xq, acc[:, 2 * (q % 2) + q // 2, :], scale, xq, MULT, ADD).then_inc(x_done, 1)
            phases = 0

            def h_low(h, kh, src):
                dve.wait_ge(h_hi_ready, h + 1)
                dve.tensor_tensor(hT[kh][:, 1, :], src, hT[kh][:, 0, :], SUB).then_inc(h_split, 1)

            def read(L, name):
                dve.wait_ge(made_by(name), small[L, name] + 1)
                return place(L, name)[0]

            def free(L, name):
                return place(L, name)[1]

            def took(L, name):
                dve.wait_ge(free(L, name), place(L, name)[2] + 1)

            def reduced(src, tmp, dst, turn):
                link(dve.tensor_scalar(tmp, src, 1.0 / TWO_PI, turn, MULT, ADD))
                link(dve.tensor_scalar(tmp, tmp, ROUND, ROUND, ADD, SUB))
                link(dve.scalar_tensor_tensor(dst, tmp, -PI_A, src, MULT, ADD))
                link(dve.scalar_tensor_tensor(dst, tmp, -PI_B, dst, MULT, ADD))
                link(dve.scalar_tensor_tensor(dst, tmp, -PI_C, dst, MULT, ADD))
                if turn:
                    link(dve.tensor_scalar(dst, dst, TWO_PI * turn, None, ADD))
                return dve.tensor_scalar(dst, dst, PI_F, -PI_F, ALU.min, ALU.max)

            def bcast(ap, n_):
                q = ap.rearrange("p (o c) -> p o c", o=1)
                return q.broadcast_to([q.shape[0], n_, q.shape[2]])

            def filter_items(L, items):
                m = m1
                for it in items:
                    kind = it.rstrip("0123456789")
                    i = int(it[-1]) if kind != it else None
                    if kind == "f":
                        o = read(L, it)
                        dve.tensor_scalar(m.farg, o[0:FILT, 0:SEQ], m.fcol[:, i:i + 1], m.fcol[:, 3:4], ADD, MULT).then_inc(free(L, it), 1)
                        took(L, it)
                        reduced(m.farg, m.fq, m.farg, 0.0).then_inc(ev["filt_arg"], 1)
                    elif kind == "h":
                        if i:
                            dve.wait_ge(ev["filt_abs"], nth(L, "filt_abs", i - 1))
                        for t in range(NT):
                            o = read(L, f"{it}t{t}")
                            dve.tensor_tensor(m.kt[:, t], two(o), bcast(m.decay[:, t, :], 2), MULT).then_inc(free(L, f"{it}t{t}"), 1)
                        for t in range(NT):
                            took(L, f"{it}t{t}")
                        link(dve.memset(m.kt[0:1, 0, 1, :], 0.0))
                        dve.tensor_tensor(m.ks, m.kt[:, :, 0, :], m.kt[:, :, 1, :], ADD).then_inc(ev["filt_taps"], 1)
                        dve.tensor_tensor(m.kd, m.kt[:, :, 0, :], m.kt[:, :, 1, :], SUB).then_inc(ev["filt_sums"], 1)
                    elif kind == "n":
                        o = read(L, it)
                        link(dve.reciprocal(m.rn, o[:, 0:CW]))
                        dve.tensor_tensor(m.KN[:, i, :], o[0:1, CW:2 * CW], m.rn[0:1, :], MULT).then_inc(free(L, it), 1)
                        took(L, it)
                        link(dve.tensor_tensor(m.KN[:, i, :], m.KN[:, i, :], m.dB[0:1, i, :], ADD))
                    elif kind == "A":
                        o = read(L, it)
                        dve.tensor_tensor(m.KA[i][:, :, :], two(o), bcast(m.rn, 2), MULT).then_inc(free(L, it), 1)
                        took(L, it)
                        link(dve.tensor_tensor(m.KA[i][:, :, :], m.KA[i][:, :, :], bcast(m.dB[:, i, :], 2), ADD))
                    elif kind == "B":
                        o = read(L, it)
                        dve.tensor_tensor(m.KB[i][:, :, :], two(o), bcast(m.rn, 2), MULT).then_inc(free(L, it), 1)
                        took(L, it)
                        link(dve.memset(m.KB[i][0:1, 0, :], 0.0))

            def ffn(L, gain, last, next_a):
                nonlocal k, b, h, f
                first = L == 0 and gain == "ffn1"
                norm(L, gain, next_a=next_a, first=first)

                def one(k, b, m, h, ka, kb_, kh, more=True):
                    dve.wait_ge(proj_done, k + 1 + CREDIT)
                    dve.tensor_tensor(gu[:, 0, :], pair[ka][:, 0, :], rb[:, :], MULT).then_inc(gate_scaled, 1)
                    dve.tensor_tensor(gu[:, 1, :], pair[ka][:, 1, :], rb[:, :], MULT).then_inc(pair_read, 1)
                    dve.wait_ge(pair_read, k + 1 + CREDIT)
                    dve.wait_ge(silu_done, m + 1)
                    dve.tensor_tensor(sh[:, 1, :], sh[:, 0, :], gu[:, 1, :], MULT).then_inc(h_done, 1)
                    dve.wait_ge(h_done, m + 1)
                    h_low(h, kh, sh[:, 1, :])
                    if more:
                        split_a(k + 2, ka)
                        split_b(b + 1, (kb_ + 1) % 2)
                ends = FILTER_UNITS if L < DEPTH and gain == "ffn1" else 2
                with dve.Fori(0, (FFU - ends) // 2) as i:
                    for e in range(2):
                        one(i * 2 + (k + e), i * 2 + (b + e), i * 2 + (f + e), i * 2 + (h + e), (k + e) % 2, (b + e) % 2, (h + e) % 2)
                if ends > 2:
                    dve.wait_ge(params_in[L], 16 * N_PARAM1)
                    if L == 0:
                        dve.wait_ge(block1_in, 16 * N_BLOCK1)
                for j in range(FFU - ends, FFU):
                    one(k + j, b + j, f + j, h + j, (k + j) % 2, (b + j) % 2, (h + j) % 2, more=False)
                    if j < FFU - 1:
                        if not last:
                            split_a(k + j + 2, (k + j) % 2)
                        split_b(b + j + 1, (b + j + 1) % 2)
                    if ends > 2:
                        filter_items(L, FILTER_ITEMS[j - (FFU - ends)])
                k += FFU
                b += FFU
                h += FFU
                f += FFU
                update_x(0.5, b - 1)
                if first:
                    dve.wait_ge(rows_T, 2)
                    for i in range(2 * DEPTH):
                        at = slice(0 if i else KT, ROWS1 if i < DEPTH else ROWS2)
                        ins = dve.tensor_copy(cols[:, i, at], cols_psum[:, i, at])
                    ins.then_inc(cols_done, 1)
                    dve.wait_ge(cols_done, 2)

            def panel(dst, factors=True, width=A_COLS):
                nonlocal k
                if factors:
                    scaled(k, k % 2, dst)
                else:
                    dve.wait_ge(proj_done, k + 1 + CREDIT)
                    dve.tensor_copy(dst, pair[k % 2][:, :, :]).then_inc(pair_read, 1)
                split_a(k + 2, k % 2, width)
                k += 1

            def row_split():
                nonlocal b
                split_b(b + 1, (b + 1) % 2)
                b += 1

            def mixer1(L):
                nonlocal k, b, sq, vk
                m = m1
                norm(L, "mix", next_a=True)
                dst = {"ca": m.ca[:, :, :], "cg": m.cg[:, :, :], "q": m.hq[:, :, :], "kv": m.hk[:, :, :],
                       "v": m.hs[0][:, :, 1:SEQ + 1], "x1": m.hs[1][:, :, 1:SEQ + 1], "x2": m.hs[0][:, :, 1:SEQ + 1]}
                dve.wait_ge(params_in[L], 16 * N_PARAM1)
                ip = taps = rows_done = 0
                tap_step = [0, 0]

                def y_scale(part, segments):
                    at = slice(2 * segments[0][0], 2 * segments[-1][0] + 2)
                    dve.wait_ge(ev["y_squares"], nth(L, "y_squares", part))
                    variance(at, segments[0][2] - segments[0][1]).then_inc(ev["y_var"], 1)
                    dve.wait_ge(ev["y_rstd"], nth(L, "y_rstd", part))
                    for s, lo, hi in segments:
                        for t in range(NT):
                            ins = dve.tensor_scalar(xn[:, t, lo:hi], xn[:, t, lo:hi], rstd[:, 2 * s + t:2 * s + t + 1], None, MULT)
                    ins.then_inc(ev["y_scaled"], 1)

                def y_low(part):
                    dve.wait_ge(ev["y_hi"], nth(L, "y_hi", part))
                    for i in range(4):
                        kt = Y_TILES[4 * part + i]
                        dve.scalar_tensor_tensor(two(xT[:, kt, 1, :]), side[:, :, i * P:(i + 1) * P], colv(L, "out", kt),
                                                 two(xT[:, kt, 0, :].bitcast(F32)), MULT, SUB).then_inc(ev["y_split"], 1)

                for it in ORDER1["dve"]:
                    i = int(it[-1]) if it[-1].isdigit() else None
                    kind = it.rstrip("0123456789")
                    if it == "A":
                        panel(dst[PANELS1[ip][0]])
                        ip += 1
                    elif it == "row":
                        row_split()
                        rows_done += 1
                    elif it == "glu":
                        dve.wait_ge(ev["gate_tanh"], nth(L, "gate_tanh"))
                        link(dve.scalar_tensor_tensor(m.u[:, :, PADC:PADC + SEQ], m.cg[:, :, :], 1.0, m.ca[:, :, :], ADD, MULT))
                    elif it == "taps":
                        for j in tap_range(taps):
                            for e in range(2):
                                src = m.u[:, e, j:j + SEQ]
                                if j == 0:
                                    tap_step[e] = step(dve.tensor_scalar(m.co[:, e, :], src, colv(L, "dww", 2 * j + e), None, MULT))
                                else:
                                    dve.wait_ge(dve_step, tap_step[e])
                                    tap_step[e] = step(dve.scalar_tensor_tensor(m.co[:, e, :], src, colv(L, "dww", 2 * j + e),
                                                                               m.co[:, e, :], MULT, ADD))
                        taps += 1
                    elif it == "stat":
                        o = read(L, it)
                        dve.tensor_scalar(var[:, 0:2], o[:, 0:2], 1.0 / QR, EPS, MULT, ADD)
                        dve.tensor_scalar(var[:, 2:4], o[:, 2:4], 1.0 / KVR, EPS, MULT, ADD).then_inc(free(L, it), 1)
                        dve.wait_ge(ev["qkv_rstd"], nth(L, "qkv_rstd"))
                        dve.tensor_scalar(m.qs[:, 0:2], rstd[:, 0:2], float(QKD) ** -0.5, None, MULT)
                        link(dve.tensor_scalar(m.qs[:, 2:4], rstd[:, 0:2], -float(QKD) ** -0.5, None, MULT))
                        for t in range(NT):
                            ins = dve.tensor_scalar(m.kvn[:, t * P:(t + 1) * P], eye[:, :], rstd[:, 2 + t:3 + t], None, MULT)
                        ins.then_inc(ev["kv_diag"], 1)
                    elif it == "kb":
                        o = read(L, it)
                        dve.scalar_tensor_tensor(m.kvn[:, :], m.hk[:, 0, :], colv(L, "kv"), o[:, 0:SEQ], MULT, MULT).then_inc(free(L, it), 1)
                    elif kind == "short":
                        dve.wait_ge(ev["short_mid"], nth(L, "short_mid", i))
                        s0 = [step(dve.scalar_tensor_tensor(m.sc[i % 2][:, e, :], m.hs[i % 2][:, e, 0:SEQ], colv(L, "hsw", 2 * i + e), m.sc[i % 2][:, e, :],
                                                            MULT, ADD)) for e in range(2)]
                        for e in range(2):
                            dve.wait_ge(dve_step, s0[e])
                            ins = dve.scalar_tensor_tensor(m.sc[i % 2][:, e, :], m.hs[i % 2][:, e, 2:SEQ + 2], colv(L, "hsw", 12 + 2 * i + e),
                                                           m.sc[i % 2][:, e, :], MULT, ADD)
                        ins.then_inc(ev["short_done"], 1)
                    elif kind == "re":
                        r = read(L, f"re{i}")
                        link(dve.tensor_tensor(m.Yr[:, :, :], two(r), m.KA[i][:, :, :], MULT))
                        dve.tensor_tensor(m.Yi[:, :, :], two(r), m.KB[i][:, :, :], MULT).then_inc(free(L, f"re{i}"), 1)
                    elif kind == "im":
                        q = read(L, f"im{i}")
                        link(dve.tensor_tensor(m.tmp[:, :, :], two(q), m.KB[i][:, :, :], MULT))
                        link(dve.tensor_tensor(m.Yr[:, :, :], m.Yr[:, :, :], m.tmp[:, :, :], SUB))
                        link(dve.tensor_tensor(m.tmp[:, :, :], two(q), m.KA[i][:, :, :], MULT))
                        took(L, f"re{i}")
                        link(dve.tensor_tensor(m.Yi[:, :, :], m.Yi[:, :, :], m.tmp[:, :, :], ADD))
                        dve.tensor_tensor(m.Yi[0:1, 0, :], q[0:1, 0:CW], m.KN[:, i, :], MULT).then_inc(free(L, f"im{i}"), 1)
                        took(L, f"im{i}")
                        dve.tensor_copy(m.mx[0:1, 0:1], m.Yi[0:1, 0, 0:1]).then_inc(ev["spectrum"], 1)
                    elif kind == "inv":
                        o = read(L, it)
                        if i == 0:
                            dve.wait_ge(free(L, "short1"), small[L, "short1"] // 4 + 1)
                            dve.tensor_tensor(m.tv[0][:, :, :], two(o), m.tv[1][:, :, :], MULT).then_inc(free(L, it), 1)
                        else:
                            dve.wait_ge(free(L, "short2"), small[L, "short2"] // 4 + 1)
                            dve.tensor_tensor(xn[:, :, 3 * CW:4 * CW], two(o), m.tv[2][:, :, :], MULT).then_inc(free(L, it), 1)
                    elif kind == "rot":
                        o = read(L, it)
                        took(L, f"q{i}")
                        link(dve.tensor_tensor(two(m.qc), two(m.qraw), bcast(m.cs[:, 0, :], 2), MULT))
                        dve.tensor_tensor(two(m.qp[i % 2]), two(o[0:QKD, :]), bcast(m.cs[:, 1, :], 2), MULT).then_inc(free(L, it), 1)
                        took(L, it)
                        dve.tensor_tensor(m.qp[i % 2], m.qp[i % 2], m.qc, ADD).then_inc(ev["q_roped"], 1)
                    elif it == "kpe":
                        r = slice(NOPE, QKD)
                        o = read(L, it)
                        link(dve.tensor_tensor(m.kpe[r], m.hk[r, 1, :], m.cs[r, 0, :], MULT))
                        dve.tensor_tensor(m.kpe2[r], o[r, 0:SEQ], m.cs[r, 1, :], MULT).then_inc(free(L, it), 1)
                        took(L, it)
                        for j in range(2):
                            ins = dve.tensor_tensor(two(m.kT[j])[r], bcast(m.kpe[r], 2), bcast(m.kpe2[r], 2), ADD)
                        ins.then_inc(ev["kpe_roped"], 1)
                    elif kind == "s":
                        o = read(L, it)
                        link(dve.tensor_reduce(m.mx[:, 2 * i:2 * i + 2], two(o), AX, ALU.max))
                        dve.tensor_tensor(m.mx[:, 2 * i:2 * i + 2], m.mx[:, 2 * i:2 * i + 2], m.qs[:, 2:4], MULT).then_inc(ev["neg_max"], 1)
                    elif kind == "o":
                        took(L, f"s{i}")
                        link(dve.reciprocal(m.rs[:, 2 * i:2 * i + 2], m.sm[:, 2 * i:2 * i + 2]))
                        o = read(L, it)
                        dve.tensor_tensor(xn[:, :, i * VD:(i + 1) * VD], o[:, 0:2 * VD].rearrange("p (t c) -> p t c", t=2),
                                          m.rs[:, 2 * i:2 * i + 2].rearrange("p (t o) -> p t o", o=1).broadcast_to([P, NT, VD]),
                                          MULT).then_inc(free(L, it), 1)
                    elif it == "yn":
                        y_scale(0, [(1, 512, 768), (2, 768, 1024)])
                    elif it == "ylo":
                        y_low(0)
                    elif it == "mn":
                        y_scale(1, [(0, 0, 512)])
                    elif it == "cbias":
                        for e in range(2):
                            dve.wait_ge(dve_step, tap_step[e])
                            ins = dve.tensor_scalar(m.co[:, e, :], m.co[:, e, :], 0.5, colv(L, "dwb", e), MULT, ADD)
                        ins.then_inc(ev["conv_done"], 1)
                    elif it == "conv_out":
                        o = read(L, it)
                        y = xn[:, :, 2 * CW:3 * CW]
                        dve.tensor_copy(y, two(o)).then_inc(free(L, it), 1)
                        took(L, it)
                        for t in range(NT):
                            st = step(dve.bn_stats(m.bn[:, t, :], y[:, t, :]))
                        dve.wait_ge(dve_step, st)
                        for t in range(NT):
                            st = step(dve.bn_aggr(m.mv[:, t, :], m.bn[:, t, :]))
                        dve.wait_ge(dve_step, st)
                        dve.tensor_scalar(var[:, 6:8], m.mv[:, :, 1], EPS, None, ADD).then_inc(ev["ln_var"], 1)
                        dve.wait_ge(ev["ln_rstd"], nth(L, "ln_rstd"))
                        for t in range(NT):
                            st = step(dve.tensor_scalar(y[:, t, :], y[:, t, :], m.mv[:, t, 0:1], rstd[:, 6 + t:7 + t], SUB, MULT))
                        dve.wait_ge(dve_step, st)
                        link(dve.tensor_tensor(y, y, bcast(m.lngb[:, 0, :], 2), MULT))
                        dve.tensor_tensor(y, y, bcast(m.lngb[:, 1, :], 2), ADD).then_inc(ev["ln_done"], 1)
                for j in range(rows_done, KT - 1):
                    if j == rows_done + 2:
                        y_low(1)
                    row_split()
                b += 1
                update_x(1.0, b - 1)

            def mixer2(L):
                nonlocal k, b, h
                m = m2
                if L == DEPTH:
                    dve.memset(m.uP[:, :, 0:PADP], 0.0)
                    dve.memset(m.uP[:, :, PADP + SEQ:], 0.0)
                    dve.memset(m.z[:, :, 0:1], 0.0)
                    link(dve.memset(m.z[:, :, SEQ + 1:], 0.0))
                norm(L, "mix", next_a=True)
                ia = gm = 0

                def gated(p):
                    gm, g = p // 3, p % 3
                    yy = (m.yf, m.yc, m.yp)[g][:, 2 * gm:2 * gm + 2, :]
                    if p == 0:
                        for s in ("yf", "yp"):
                            for q in range(4):
                                took(L, f"{s}{q}")
                    if g == 0:
                        dve.wait_ge(h_split, h)
                        link(dve.scalar_tensor_tensor(m.mg[:, :, :], m.th[p % 2][:, :, :], 1.0, yy, ADD, MULT))
                    else:
                        link(dve.scalar_tensor_tensor(m.cv[:, :, :], m.th[p % 2][:, :, :], 1.0, yy, ADD, MULT))
                        ins = dve.tensor_tensor(m.mg[:, :, :], m.mg[:, :, :], m.cv[:, :, :], ADD)
                        if g == 1:
                            link(ins)
                        else:
                            ins.then_inc(ev["merged"], 1)

                def merged_low():
                    nonlocal h
                    for e in range(2):
                        h_low(h, h % 2, m.mg[:, e, :])
                        h += 1
                        if e == 0:
                            row_split()
                for it in ORDER2["dve"] + ["G"] * 4:
                    i = int(it[-1]) if it[-1].isdigit() else None
                    if it == "A":
                        name, j = PANELS2[ia]
                        panel({"F": m.uF[:, 2 * j:2 * j + 2, :], "P": m.uP[:, 2 * j:2 * j + 2, PADP:PADP + SEQ],
                               "C": m.c[:, :, :], "V": m.v[:, :, :], "B": m.gs[:, :, :]}[name], width=conv_width(ia))
                        ia += 1
                    elif it[0] == "Y":
                        panel(m.yc[:, 2 * i:2 * i + 2, :], factors=False, width=conv_width(ia))
                        ia += 1
                    elif it == "pool":
                        dve.wait_ge(pair_read, k + CREDIT)
                        if L == DEPTH:
                            dve.wait_ge(block2_in, 16 * N_BLOCK2)
                        w = SEQ + 2 * PADP
                        link(dve.tensor_tensor(m.d1[:, :, 0:w - 1], m.uP[:, :, 0:w - 1], m.uP[:, :, 1:w], ADD))
                        link(dve.tensor_tensor(m.d2[:, 1:4, 0:w - 3], m.d1[:, 1:4, 0:w - 3], m.d1[:, 1:4, 2:w - 1], ADD))
                        link(dve.tensor_tensor(m.d1[:, 2:4, 0:w - 7], m.d2[:, 2:4, 0:w - 7], m.d2[:, 2:4, 4:w - 3], ADD))
                        link(dve.tensor_tensor(m.d2[:, 3, 0:w - 15], m.d1[:, 3, 0:w - 15], m.d1[:, 3, 8:w - 7], ADD))
                        for g, d in enumerate((m.d1, m.d2, m.d1, m.d2)):
                            at = PADP - WINDOWS[g] // 2
                            link(dve.tensor_tensor(m.cvp[:, g, :], d[:, g, at:at + SEQ], m.count[:, g, :], MULT))
                        dve.tensor_tensor(m.d1[:, :, 0:SEQ], m.cvp[:, :, :], m.uP[:, :, PADP:PADP + SEQ], SUB).then_inc(ev["pooled"], 1)
                    elif it[0] == "z":
                        zz = m.z[:, 2 * i:2 * i + 2, :]
                        dve.wait_ge(pair_read, k + CREDIT)
                        link(dve.tensor_tensor(zz[:, :, 1:SEQ + 1], m.c[:, :, :], m.v[:, :, :], MULT))
                        st = [step(dve.tensor_scalar(m.cv[:, e, :], zz[:, e, 0:SEQ], colv(L, "wc", 2 * i + e), None, MULT)) for e in range(2)]
                        for j in (1, 2):
                            for e in range(2):
                                dve.wait_ge(dve_step, st[e])
                                st[e] = step(dve.scalar_tensor_tensor(m.cv[:, e, :], zz[:, e, j:j + SEQ], colv(L, "wc", 4 * j + 2 * i + e),
                                                                      m.cv[:, e, :], MULT, ADD))
                        dve.wait_ge(dve_step, st[1])
                    elif it[:2] == "bc":
                        dve.wait_ge(pair_read, k + CREDIT)
                        dve.tensor_tensor(m.gs[:, :, :], m.gs[:, :, :], m.cv[:, :, :], MULT).then_inc(ev["bc_f32"], 1)
                        dve.wait_ge(ev["bc_hi"], nth(L, "bc_hi", i))
                        dve.tensor_tensor(m.bc[:, 2 * i:2 * i + 2, 1, :], m.gs[:, :, :], m.bc[:, 2 * i:2 * i + 2, 0, :], SUB)\
                           .then_inc(ev["bc_split"], 1)
                    elif it == "G":
                        for g in range(3):
                            if (gm, g) != (0, 0):
                                dve.wait_ge(ev["gate_done"], nth(L, "gate_done", 3 * gm + g - 1))
                            scaled(k, k % 2, m.gs[:, :, :])
                            if (gm, g) != (0, 0):
                                gated(3 * gm + g - 1)
                            if (gm, g) != (3, 2):
                                split_a(k + 2, k % 2)
                            else:
                                dve.wait_ge(ev["gate_done"], nth(L, "gate_done", 11))
                                gated(11)
                            k += 1
                            if gm and g == 0:
                                merged_low()
                            if gm and g == 2:
                                row_split()
                        gm += 1
                merged_low()
                split_a(k + 1, (k + 1) % 2)
                b += 1
                update_x(0.5, b - 1)

            def final_norm(L):
                nonlocal sq, vk
                for t in range(NT):
                    sq += 1
                    dve.wait_ge(ssq_done, sq)
                    variance(slice(t, t + 1), DM).then_inc(var_done, 1)
                dve.wait_ge(gain_in, 16 * (L // DEPTH + 1))
                for q in range(4):
                    t, at = q // 2, slice((q % 2) * HALF, (q % 2 + 1) * HALF)
                    if q % 2 == 0:
                        vk += 1
                        dve.wait_ge(rstd_done, vk)
                    dve.scalar_tensor_tensor(x[:, t, at], x[:, t, at], rstd[:, t:t + 1], xn[:, 1, at], MULT, MULT).then_inc(x_done, 1)

            dve.memset(ones[:, :], 1.0)
            dve.memset(junk[:, 0:1], 0.0).then_inc(a_split, CREDIT)
            dve.memset(junk[:, 1:2], 0.0).then_inc(b_split, CREDIT)
            dve.memset(junk[:, 2:3], 0.0).then_inc(pair_read, CREDIT)
            dve.memset(m1.u[:, :, 0:PADC], 0.0)
            dve.memset(m1.u[:, :, PADC + SEQ:], 0.0)
            for hs in m1.hs:
                dve.memset(hs[:, :, 0:1], 0.0)
                dve.memset(hs[:, :, SEQ + 1:], 0.0)
            dve.memset(minus_half[:, :], -0.5).then_inc(half_set, 1)
            dve.wait_ge(rope_in, 16 * 2)
            link(dve.tensor_copy(m1.posf, m1.pos))
            link(dve.tensor_scalar(m1.posf, m1.posf, m1.invf[:, 0:1], None, MULT))
            for i, turn in enumerate((0.25, 0.0)):
                reduced(m1.posf, m1.fq96, m1.ra[:, i, :], turn).then_inc(ev["rope_arg"], 1)
                dve.wait_ge(ev["rope_arg"], i + 1)
            dve.wait_ge(rows_T, 1)
            dve.tensor_copy(cols[:, 0, 0:KT], cols_psum[:, 0, 0:KT]).then_inc(cols_done, 1)
            dve.wait_ge(cols_done, 1)
            for L in range(2 * DEPTH):
                ffn(L, "ffn1", False, next_a=True)
                if L < DEPTH:
                    mixer1(L)
                else:
                    mixer2(L)
                ffn(L, "ffn2", L == 2 * DEPTH - 1, next_a=False)
                if L % DEPTH == DEPTH - 1:
                    final_norm(L)


def kernel(**inputs):
    import concourse.bacc as bacc
    from concourse.bass_utils import run_bass_kernel_spmd

    nc = bacc.Bacc("TRN2", target_bir_lowering=False, num_devices=1)
    arrays = {n: np.ascontiguousarray(v) for n, v in inputs.items()}
    arrays.update(host_constants())
    feed = {f"in_{n}": v for n, v in arrays.items()}
    T = {n: nc.dram_tensor(f"in_{n}", v.shape, mybir.dt.from_np(v.dtype), kind="ExternalInput").ap() for n, v in arrays.items()}
    out = nc.dram_tensor("out_0", (1, SEQ, DM), mybir.dt.float32, kind="ExternalOutput").ap()
    build(nc, T, out)
    r = run_bass_kernel_spmd(nc, [feed], core_ids=[0])
    return r.results[0]["out_0"]
```
